# Optimizing a Trainium2 kernel written in Bass

```python
import math
import jax, jax.numpy as jnp
from jax import lax
import numpy as np

D_MODEL = 1024
BATCH = 1
SEQ = 256
DEPTH = 1

CHUNK = 64
Q_BLOCK = 128
SB_HEAD_DIM = 64
SB_HEADS = D_MODEL // 128
SB_WIDTH = SB_HEADS * SB_HEAD_DIM
SSM_WIDTH = D_MODEL // 2
SSM_GROUP = 16
SSM_GROUPS = SSM_WIDTH // SSM_GROUP
SSM_STATE = 64
N_MEM = 256
XA_HEADS = 4
XA_HEAD_DIM = D_MODEL // XA_HEADS
D_FF = 11 * D_MODEL // 4
CONV_WIDTH = 3
RMS_EPS = 1e-6
IN_WIDTH = 3 * SB_WIDTH + SSM_WIDTH + 2 * D_MODEL


def rms_norm(x, gain):
    xf = x.astype(jnp.float32)
    y = xf * lax.rsqrt(jnp.mean(xf * xf, axis=-1, keepdims=True) + RMS_EPS)
    return (y * gain.astype(jnp.float32)).astype(x.dtype)

def stick_breaking_attention(q, k, v):
    b, s, _ = q.shape
    n_blk = s // Q_BLOCK
    qh = q.reshape(b, n_blk, Q_BLOCK, SB_HEADS, SB_HEAD_DIM).transpose(1, 0, 3, 2, 4)
    kh = k.reshape(b, s, SB_HEADS, SB_HEAD_DIM).transpose(0, 2, 1, 3)
    vh = v.reshape(b, s, SB_HEADS, SB_HEAD_DIM).transpose(0, 2, 1, 3)
    key_pos = jnp.arange(s, dtype=jnp.int32)
    scale = SB_HEAD_DIM ** -0.5

    def one_block(args):
        q_blk, blk = args
        z = jnp.einsum('bhqd,bhkd->bhqk', q_blk, kh).astype(jnp.float32) * scale
        q_pos = blk * Q_BLOCK + jnp.arange(Q_BLOCK, dtype=jnp.int32)
        causal = key_pos[None, :] < q_pos[:, None]
        log_fail = jnp.where(causal, jax.nn.log_sigmoid(-z), 0.0)
        log_remain = lax.cumsum(log_fail, axis=3, reverse=True) - log_fail
        w = jnp.where(causal, jnp.exp(jax.nn.log_sigmoid(z) + log_remain), 0.0)
        return jnp.einsum('bhqk,bhkd->bhqd', w.astype(vh.dtype), vh)

    out = lax.map(one_block, (qh, jnp.arange(n_blk, dtype=jnp.int32)))
    return out.transpose(1, 0, 3, 2, 4).reshape(b, s, SB_WIDTH)

def _linear_recurrence_combine(e_i, e_j):
    a_i, b_i = e_i
    a_j, b_j = e_j
    return a_j * a_i, a_j * b_i + b_j

def s5_branch(u, a_re, a_im, log_dt, b_re, b_im, c_re, c_im, d_skip, w_glu, b_glu):
    b, s, _ = u.shape
    f32 = jnp.float32
    ug = u.astype(f32).reshape(b, s, SSM_GROUPS, SSM_GROUP)
    lam = lax.complex(a_re.astype(f32), a_im.astype(f32))
    dt = jnp.exp(log_dt.astype(f32))[:, None]
    lam_bar = jnp.exp(lam * dt)
    b_mat = lax.complex(b_re.astype(f32), b_im.astype(f32))
    b_bar = ((lam_bar - 1.0) / lam)[:, :, None] * b_mat
    bu = jnp.einsum('gpc,bsgc->bsgp', b_bar, ug.astype(jnp.complex64))
    decay = jnp.broadcast_to(lam_bar, (1, s, SSM_GROUPS, SSM_STATE))
    _, states = lax.associative_scan(_linear_recurrence_combine, (decay, bu), axis=1)
    c_mat = lax.complex(c_re.astype(f32), c_im.astype(f32))
    y = jnp.einsum('gcp,bsgp->bsgc', c_mat, states).real
    y = y + d_skip.astype(f32).reshape(SSM_GROUPS, SSM_GROUP) * ug
    y = jax.nn.gelu(y.reshape(b, s, SSM_WIDTH)).astype(u.dtype)
    return y * jax.nn.sigmoid(y @ w_glu + b_glu)

def memory_cross_attention(h, mem_n, wq, wk, wv, wo):
    b, s, _ = h.shape
    m = mem_n.shape[1]
    q = (h @ wq).reshape(b, s, XA_HEADS, XA_HEAD_DIM)
    k = (mem_n @ wk).reshape(b, m, XA_HEADS, XA_HEAD_DIM)
    v = (mem_n @ wv).reshape(b, m, XA_HEADS, XA_HEAD_DIM)
    scores = jnp.einsum('bqhd,bmhd->bhqm', q, k).astype(jnp.float32) * (XA_HEAD_DIM ** -0.5)
    p = jax.nn.softmax(scores, axis=-1).astype(v.dtype)
    o = jnp.einsum('bhqm,bmhd->bqhd', p, v).reshape(b, s, D_MODEL)
    return o @ wo

def conv_ffn(h, w_up, conv_w, conv_b, w_down):
    up = h @ w_up
    up = lax.conv_general_dilated(
        up, conv_w[:, None, :].astype(up.dtype), window_strides=(1,),
        padding=[(CONV_WIDTH - 1, 0)], dimension_numbers=('NWC', 'WIO', 'NWC'),
        feature_group_count=2 * D_FF) + conv_b
    gate, val = jnp.split(up, 2, axis=-1)
    return (jax.nn.gelu(gate) * val) @ w_down

def _normal(key, shape, scale):
    return jax.random.normal(key, shape, jnp.float32) * scale

def first_inputs(seed: int = 0) -> dict:
    key = jax.random.key(seed)
    ks = jax.random.split(key, 32)
    L, D, G, P, C = DEPTH, D_MODEL, SSM_GROUPS, SSM_STATE, SSM_GROUP
    gain = lambda k: 1.0 + _normal(k, (L, D), 0.05)
    return {
        "x": _normal(ks[0], (BATCH, SEQ, D), 1.0),
        "mem": _normal(ks[1], (BATCH, N_MEM, D), 1.0),
        "norm_mix_pre": gain(ks[2]),
        "norm_mix_post": gain(ks[3]),
        "w_in": _normal(ks[4], (L, D, IN_WIDTH), D ** -0.5),
        "b_gate": _normal(ks[5], (L, 2 * D), 0.01),
        "ssm_a_re": -0.5 + _normal(ks[6], (L, G, P), 0.01),
        "ssm_a_im": jnp.pi * jnp.arange(P, dtype=jnp.float32)[None, None, :] + _normal(ks[7], (L, G, P), 0.01),
        "ssm_log_dt": jax.random.uniform(ks[8], (L, G), jnp.float32, math.log(1e-3), math.log(1e-1)),
        "ssm_b_re": _normal(ks[9], (L, G, P, C), (2 * C) ** -0.5),
        "ssm_b_im": _normal(ks[10], (L, G, P, C), (2 * C) ** -0.5),
        "ssm_c_re": _normal(ks[11], (L, G, C, P), (2 * P) ** -0.5),
        "ssm_c_im": _normal(ks[12], (L, G, C, P), (2 * P) ** -0.5),
        "ssm_d": _normal(ks[13], (L, SSM_WIDTH), 1.0),
        "ssm_w_glu": _normal(ks[14], (L, SSM_WIDTH, SSM_WIDTH), SSM_WIDTH ** -0.5),
        "ssm_b_glu": _normal(ks[15], (L, SSM_WIDTH), 0.01),
        "w_branch_attn": _normal(ks[16], (L, SB_WIDTH, D), SB_WIDTH ** -0.5),
        "w_branch_ssm": _normal(ks[17], (L, SSM_WIDTH, D), SSM_WIDTH ** -0.5),
        "w_out": _normal(ks[18], (L, D, D), D ** -0.5),
        "norm_xa_pre": gain(ks[19]),
        "norm_xa_post": gain(ks[20]),
        "norm_mem": gain(ks[21]),
        "xa_wq": _normal(ks[22], (L, D, D), D ** -0.5),
        "xa_wk": _normal(ks[23], (L, D, D), D ** -0.5),
        "xa_wv": _normal(ks[24], (L, D, D), D ** -0.5),
        "xa_wo": _normal(ks[25], (L, D, D), D ** -0.5),
        "norm_ffn_pre": gain(ks[26]),
        "norm_ffn_post": gain(ks[27]),
        "ffn_w_up": _normal(ks[28], (L, D, 2 * D_FF), D ** -0.5),
        "ffn_conv_w": _normal(ks[29], (L, CONV_WIDTH, 2 * D_FF), CONV_WIDTH ** -0.5),
        "ffn_conv_b": _normal(ks[30], (L, 2 * D_FF), 0.01),
        "ffn_w_down": _normal(ks[31], (L, D_FF, D), D_FF ** -0.5),
    }

def first_block(x, mem, norm_mix_pre, norm_mix_post, w_in, b_gate,
              ssm_a_re, ssm_a_im, ssm_log_dt, ssm_b_re, ssm_b_im, ssm_c_re, ssm_c_im,
              ssm_d, ssm_w_glu, ssm_b_glu, w_branch_attn, w_branch_ssm, w_out,
              norm_xa_pre, norm_xa_post, norm_mem, xa_wq, xa_wk, xa_wv, xa_wo,
              norm_ffn_pre, norm_ffn_post, ffn_w_up, ffn_conv_w, ffn_conv_b, ffn_w_down):
    splits = (SB_WIDTH, 2 * SB_WIDTH, 3 * SB_WIDTH, 3 * SB_WIDTH + SSM_WIDTH)
    for l in range(DEPTH):
        h = rms_norm(x, norm_mix_pre[l])
        proj = h @ w_in[l]
        q, k, v, u, gate_logits = jnp.split(proj, splits, axis=-1)
        gate_attn, gate_ssm = jnp.split(jax.nn.sigmoid(gate_logits + b_gate[l]), 2, axis=-1)
        o_attn = stick_breaking_attention(q, k, v)
        o_ssm = s5_branch(u, ssm_a_re[l], ssm_a_im[l], ssm_log_dt[l], ssm_b_re[l], ssm_b_im[l],
                          ssm_c_re[l], ssm_c_im[l], ssm_d[l], ssm_w_glu[l], ssm_b_glu[l])
        merged = gate_attn * (o_attn @ w_branch_attn[l]) + gate_ssm * (o_ssm @ w_branch_ssm[l])
        x = x + rms_norm(merged @ w_out[l], norm_mix_post[l])
        h = rms_norm(x, norm_xa_pre[l])
        mem_n = rms_norm(mem, norm_mem[l])
        xa = memory_cross_attention(h, mem_n, xa_wq[l], xa_wk[l], xa_wv[l], xa_wo[l])
        x = x + rms_norm(xa, norm_xa_post[l])
        h = rms_norm(x, norm_ffn_pre[l])
        f = conv_ffn(h, ffn_w_up[l], ffn_conv_w[l], ffn_conv_b[l], ffn_w_down[l])
        x = x + rms_norm(f, norm_ffn_post[l])
    return x


D_MIX = D_MODEL
D_MLSTM = D_MIX // 2
N_MLSTM_HEADS = 4
DH_MLSTM = D_MLSTM // N_MLSTM_HEADS
CONV_W = 4
D_GMLP = D_MIX - D_MLSTM
N_GMLP_GROUPS = 8
DG_GMLP = D_GMLP // N_GMLP_GROUPS
GMLP_BLOCK = 128
D_IN = 4 * D_MLSTM + 2 * N_MLSTM_HEADS + 2 * D_GMLP
N_EXPERT_GROUPS = 4
EXPERTS_PER_GROUP = 8
N_EXPERTS = N_EXPERT_GROUPS * EXPERTS_PER_GROUP
TOP_K = 2
D_FF_EXPERT = 512
MOE_BLOCK = 128
EPS = 1e-6


def rms_norm_2(x, g):
    xf = x.astype(jnp.float32)
    y = xf * lax.rsqrt(jnp.mean(xf * xf, axis=-1, keepdims=True) + EPS)
    return (y * g.astype(jnp.float32)).astype(x.dtype)

def head_rms(x):
    xf = x.astype(jnp.float32)
    return xf * lax.rsqrt(jnp.mean(xf * xf, axis=-1, keepdims=True) + EPS)

def causal_depthwise_conv(x, w):
    k = w.shape[0]
    s = x.shape[1]
    xp = jnp.pad(x, ((0, 0), (k - 1, 0), (0, 0)))
    y = w[0] * xp[:, 0:s]
    for i in range(1, k):
        y = y + w[i] * xp[:, i:i + s]
    return y

def mlstm_chunkwise(q, k, v, i_pre, f_pre):
    b_, s_, h_, dh = q.shape
    nc = s_ // CHUNK

    def to_chunks(a):
        a = a.reshape((b_, nc, CHUNK, h_) + a.shape[3:])
        return jnp.moveaxis(a, (1, 3), (0, 2))

    log_f = jax.nn.log_sigmoid(f_pre)
    xs = (to_chunks(q), to_chunks(k), to_chunks(v), to_chunks(i_pre), to_chunks(log_f))
    causal = jnp.tril(jnp.ones((CHUNK, CHUNK), dtype=bool))

    def step(carry, inp):
        c_st, n_st, m_st = carry
        qc, kc, vc, ic, lfc = inp
        bcum = jnp.cumsum(lfc, axis=-1)
        d = jnp.where(causal, bcum[..., :, None] - bcum[..., None, :] + ic[..., None, :], -jnp.inf)
        inter = bcum + m_st[..., None]
        m_t = jnp.maximum(inter, jnp.max(d, axis=-1))
        s = jnp.einsum('bhld,bhsd->bhls', qc, kc) * jnp.exp(d - m_t[..., None])
        w_inter = jnp.exp(inter - m_t)
        numer = jnp.einsum('bhls,bhsd->bhld', s, vc) + w_inter[..., None] * jnp.einsum('bhvd,bhld->bhlv', c_st, qc)
        nq = jnp.sum(s, axis=-1) + w_inter * jnp.einsum('bhd,bhld->bhl', n_st, qc)
        h = numer / jnp.maximum(jnp.abs(nq), jnp.exp(-m_t))[..., None]
        b_last = bcum[..., -1]
        w_state = b_last[..., None] - bcum + ic
        m_new = jnp.maximum(b_last + m_st, jnp.max(w_state, axis=-1))
        decay = jnp.exp(b_last + m_st - m_new)
        ws = jnp.exp(w_state - m_new[..., None])
        c_new = decay[..., None, None] * c_st + jnp.einsum('bhl,bhlv,bhld->bhvd', ws, vc, kc)
        n_new = decay[..., None] * n_st + jnp.einsum('bhl,bhld->bhd', ws, kc)
        return (c_new, n_new, m_new), h

    init = (jnp.zeros((b_, h_, dh, dh), jnp.float32), jnp.zeros((b_, h_, dh), jnp.float32),
            jnp.zeros((b_, h_), jnp.float32))
    _, hs = lax.scan(step, init, xs)
    return jnp.moveaxis(hs, (0, 2), (1, 3)).reshape(b_, s_, h_, dh)

def hybrid_mixer(xn, w_in, conv_qk, b_igate, b_fgate, g_mlstm_out, g_gmlp_v, w_spatial, b_spatial, g_gmlp_out, w_out):
    b_, s_, _ = xn.shape
    hh = N_MLSTM_HEADS
    proj = jnp.einsum('bsd,de->bse', xn, w_in)
    cuts = [2 * D_MLSTM, 3 * D_MLSTM, 4 * D_MLSTM, 4 * D_MLSTM + 2 * hh, 4 * D_MLSTM + 2 * hh + D_GMLP]
    qk, v_m, o_pre, if_pre, u_g, v_g = jnp.split(proj, cuts, axis=-1)

    qk = jax.nn.silu(causal_depthwise_conv(qk, conv_qk))
    q, k = jnp.split(qk.astype(jnp.float32), 2, axis=-1)
    q = q.reshape(b_, s_, hh, DH_MLSTM)
    k = k.reshape(b_, s_, hh, DH_MLSTM) * (DH_MLSTM ** -0.5)
    vm = v_m.astype(jnp.float32).reshape(b_, s_, hh, DH_MLSTM)
    i_pre = if_pre[..., :hh].astype(jnp.float32) + b_igate.astype(jnp.float32)
    f_pre = if_pre[..., hh:].astype(jnp.float32) + b_fgate.astype(jnp.float32)
    h_m = mlstm_chunkwise(q, k, vm, i_pre, f_pre)
    h_m = jax.nn.sigmoid(o_pre.astype(jnp.float32)).reshape(b_, s_, hh, DH_MLSTM) * h_m
    y_m = (head_rms(h_m).reshape(b_, s_, D_MLSTM) * g_mlstm_out.astype(jnp.float32)).astype(xn.dtype)

    nb = s_ // GMLP_BLOCK
    u = jax.nn.gelu(u_g)
    vg = rms_norm_2(jax.nn.gelu(v_g), g_gmlp_v)
    vb = vg.reshape(b_, nb, GMLP_BLOCK, N_GMLP_GROUPS, DG_GMLP)
    tri = jnp.tril(jnp.ones((GMLP_BLOCK, GMLP_BLOCK), dtype=w_spatial.dtype))
    mix = jnp.einsum('gts,bnsgc->bntgc', w_spatial * tri, vb) + b_spatial.T[:, :, None]
    gated = u.reshape(b_, nb, GMLP_BLOCK, N_GMLP_GROUPS, DG_GMLP) * mix
    y_g = (head_rms(gated).reshape(b_, s_, D_GMLP) * g_gmlp_out.astype(jnp.float32)).astype(xn.dtype)

    y = jnp.concatenate([y_m, y_g], axis=-1)
    return jnp.einsum('bse,ed->bsd', y, w_out)

def hierarchical_moe(xn, w_rg, b_rg, w_re, b_re, w_gate, w_up, w_down):
    b_, s_, d = xn.shape
    t = b_ * s_
    xf = xn.reshape(t, d)
    p_g = jax.nn.softmax((xf @ w_rg).astype(jnp.float32) + b_rg.astype(jnp.float32), axis=-1)
    g_sel = jnp.argmax(p_g, axis=-1)
    p_gsel = jnp.take_along_axis(p_g, g_sel[:, None], axis=-1)[:, 0]
    le = ((xf @ w_re).astype(jnp.float32) + b_re.astype(jnp.float32)).reshape(t, N_EXPERT_GROUPS, EXPERTS_PER_GROUP)
    le = jnp.take_along_axis(le, g_sel[:, None, None], axis=1)[:, 0]
    top_p, top_i = lax.top_k(jax.nn.softmax(le, axis=-1), TOP_K)
    top_p = top_p / jnp.sum(top_p, axis=-1, keepdims=True)
    weights = p_gsel[:, None] * top_p
    experts = (g_sel[:, None] * EXPERTS_PER_GROUP + top_i).astype(jnp.int32)

    n_pairs = t * TOP_K
    e_flat = experts.reshape(-1)
    tok_flat = jnp.repeat(jnp.arange(t, dtype=jnp.int32), TOP_K)
    w_flat = weights.reshape(-1)
    order = jnp.argsort(e_flat)
    e_sorted = e_flat[order]
    counts = jnp.zeros((N_EXPERTS,), jnp.int32).at[e_flat].add(1)
    padded = (counts + MOE_BLOCK - 1) // MOE_BLOCK * MOE_BLOCK
    starts = jnp.cumsum(counts) - counts
    pad_ends = jnp.cumsum(padded)
    pad_starts = pad_ends - padded
    dest = pad_starts[e_sorted] + jnp.arange(n_pairs, dtype=jnp.int32) - starts[e_sorted]
    n_blocks = n_pairs // MOE_BLOCK + N_EXPERTS
    n_rows = n_blocks * MOE_BLOCK
    row_tok = jnp.full((n_rows,), t, jnp.int32).at[dest].set(tok_flat[order])
    row_w = jnp.zeros((n_rows,), jnp.float32).at[dest].set(w_flat[order])
    block_e = jnp.minimum(jnp.searchsorted(pad_ends, jnp.arange(n_blocks, dtype=jnp.int32) * MOE_BLOCK, side='right'),
                          N_EXPERTS - 1)
    x_pad = jnp.concatenate([xf, jnp.zeros((1, d), xf.dtype)], axis=0)
    xb = x_pad[row_tok].reshape(n_blocks, MOE_BLOCK, d)

    def expert_block(args):
        xblk, e = args
        hid = jax.nn.silu(xblk @ w_gate[e]) * (xblk @ w_up[e])
        return hid @ w_down[e]

    yb = lax.map(expert_block, (xb, block_e)).reshape(n_rows, d)
    y = jax.ops.segment_sum(yb * row_w[:, None].astype(yb.dtype), row_tok, num_segments=t + 1)[:t]
    return y.reshape(b_, s_, d)

def second_inputs(seed: int = 0) -> dict:
    key = jax.random.key(seed)
    ks = jax.random.split(key, 20)
    f32 = jnp.float32
    nrm = lambda k, shape, scale: jax.random.normal(k, shape, f32) * scale
    return {
        "x": nrm(ks[0], (BATCH, SEQ, D_MODEL), 1.0),
        "norm1_g": 1.0 + nrm(ks[1], (DEPTH, D_MODEL), 0.02),
        "w_in": nrm(ks[2], (DEPTH, D_MODEL, D_IN), D_MODEL ** -0.5),
        "conv_qk": nrm(ks[3], (DEPTH, CONV_W, 2 * D_MLSTM), CONV_W ** -0.5),
        "b_igate": nrm(ks[4], (DEPTH, N_MLSTM_HEADS), 0.1),
        "b_fgate": jnp.linspace(3.0, 6.0, N_MLSTM_HEADS, dtype=f32)[None, :] + nrm(ks[5], (DEPTH, N_MLSTM_HEADS), 0.1),
        "g_mlstm_out": 1.0 + nrm(ks[6], (DEPTH, D_MLSTM), 0.02),
        "g_gmlp_v": 1.0 + nrm(ks[7], (DEPTH, D_GMLP), 0.02),
        "w_spatial": nrm(ks[8], (DEPTH, N_GMLP_GROUPS, GMLP_BLOCK, GMLP_BLOCK), 0.5 * GMLP_BLOCK ** -0.5),
        "b_spatial": 1.0 + nrm(ks[9], (DEPTH, N_GMLP_GROUPS, GMLP_BLOCK), 0.01),
        "g_gmlp_out": 1.0 + nrm(ks[10], (DEPTH, D_GMLP), 0.02),
        "w_out": nrm(ks[11], (DEPTH, D_MIX, D_MODEL), D_MIX ** -0.5),
        "norm2_g": 1.0 + nrm(ks[12], (DEPTH, D_MODEL), 0.02),
        "w_router_group": nrm(ks[13], (DEPTH, D_MODEL, N_EXPERT_GROUPS), D_MODEL ** -0.5),
        "b_router_group": nrm(ks[14], (DEPTH, N_EXPERT_GROUPS), 0.01),
        "w_router_expert": nrm(ks[15], (DEPTH, D_MODEL, N_EXPERTS), D_MODEL ** -0.5),
        "b_router_expert": nrm(ks[16], (DEPTH, N_EXPERTS), 0.01),
        "w_gate": nrm(ks[17], (DEPTH, N_EXPERTS, D_MODEL, D_FF_EXPERT), D_MODEL ** -0.5),
        "w_up": nrm(ks[18], (DEPTH, N_EXPERTS, D_MODEL, D_FF_EXPERT), D_MODEL ** -0.5),
        "w_down": nrm(ks[19], (DEPTH, N_EXPERTS, D_FF_EXPERT, D_MODEL), D_FF_EXPERT ** -0.5),
        "final_g": 1.0 + nrm(jax.random.fold_in(key, 99), (D_MODEL,), 0.02),
    }

def second_block(x, norm1_g, w_in, conv_qk, b_igate, b_fgate, g_mlstm_out, g_gmlp_v, w_spatial, b_spatial,
              g_gmlp_out, w_out, norm2_g, w_router_group, b_router_group, w_router_expert, b_router_expert,
              w_gate, w_up, w_down, final_g):
    h = x
    for l in range(DEPTH):
        h = h + hybrid_mixer(rms_norm_2(h, norm1_g[l]), w_in[l], conv_qk[l], b_igate[l], b_fgate[l],
                             g_mlstm_out[l], g_gmlp_v[l], w_spatial[l], b_spatial[l], g_gmlp_out[l], w_out[l])
        h = h + hierarchical_moe(rms_norm_2(h, norm2_g[l]), w_router_group[l], b_router_group[l],
                                 w_router_expert[l], b_router_expert[l], w_gate[l], w_up[l], w_down[l])
    return rms_norm_2(h, final_g)


def setup_inputs(seed=0):
    out = dict(first_inputs(seed))
    for name, value in second_inputs(seed + 1).items():
        if name != "x":
            out[name + "_2"] = value
    return out


def reference(
    x, mem, norm_mix_pre, norm_mix_post, w_in, b_gate, ssm_a_re, ssm_a_im, ssm_log_dt, ssm_b_re,
    ssm_b_im, ssm_c_re, ssm_c_im, ssm_d, ssm_w_glu, ssm_b_glu, w_branch_attn, w_branch_ssm,
    w_out, norm_xa_pre, norm_xa_post, norm_mem, xa_wq, xa_wk, xa_wv, xa_wo, norm_ffn_pre,
    norm_ffn_post, ffn_w_up, ffn_conv_w, ffn_conv_b, ffn_w_down, norm1_g_2, w_in_2, conv_qk_2,
    b_igate_2, b_fgate_2, g_mlstm_out_2, g_gmlp_v_2, w_spatial_2, b_spatial_2, g_gmlp_out_2,
    w_out_2, norm2_g_2, w_router_group_2, b_router_group_2, w_router_expert_2,
    b_router_expert_2, w_gate_2, w_up_2, w_down_2, final_g_2,
):
    x = first_block(
        x, mem, norm_mix_pre, norm_mix_post, w_in, b_gate, ssm_a_re, ssm_a_im, ssm_log_dt,
        ssm_b_re, ssm_b_im, ssm_c_re, ssm_c_im, ssm_d, ssm_w_glu, ssm_b_glu, w_branch_attn,
        w_branch_ssm, w_out, norm_xa_pre, norm_xa_post, norm_mem, xa_wq, xa_wk, xa_wv, xa_wo,
        norm_ffn_pre, norm_ffn_post, ffn_w_up, ffn_conv_w, ffn_conv_b, ffn_w_down,
    )
    return second_block(
        x, norm1_g_2, w_in_2, conv_qk_2, b_igate_2, b_fgate_2, g_mlstm_out_2, g_gmlp_v_2,
        w_spatial_2, b_spatial_2, g_gmlp_out_2, w_out_2, norm2_g_2, w_router_group_2,
        b_router_group_2, w_router_expert_2, b_router_expert_2, w_gate_2, w_up_2, w_down_2,
        final_g_2,
    )


_drawn_inputs = setup_inputs


def setup_inputs(seed=0):
    import zlib

    import numpy as np

    out = dict(_drawn_inputs(seed))
    spreads = {}
    factors = {'b_gate': 7.304,
     'ssm_a_re': 8.0,
     'ssm_b_re': 3.189,
     'ssm_b_im': 3.04,
     'ssm_c_re': 2.862,
     'ssm_c_im': 2.847,
     'ssm_b_glu': 6.614,
     'ffn_conv_b': 4.994,
     'norm1_g_2': 3.528,
     'b_igate_2': 8.0,
     'g_mlstm_out_2': 4.148,
     'g_gmlp_v_2': 8.0,
     'b_spatial_2': 8.0,
     'g_gmlp_out_2': 6.251,
     'norm2_g_2': 4.044,
     'b_router_group_2': 8.0,
     'b_router_expert_2': 4.932,
     'final_g_2': 2.917}
    for name, (base, spread) in spreads.items():
        noise = np.random.default_rng([zlib.crc32(name.encode()), seed]).standard_normal(out[name].shape)
        drawn = base * np.exp(spread * noise) if base else spread * noise
        out[name] = __import__('jax').numpy.asarray(drawn.astype(out[name].dtype))
    for name, factor in factors.items():
        out[name] = (out[name] * factor).astype(out[name].dtype)
    return out
```

```python
from contextlib import ExitStack

import numpy as np

import concourse.bass as bass
from concourse import mybir

ALU = mybir.AluOpType
ACT = mybir.ActivationFunctionType
F32 = mybir.dt.float32
I32 = mybir.dt.int32
AX = mybir.AxisListType

P = 128
D = 1024
T = 256
KT = D // P
TT = T // P
RING = 12
UNIT = 8 * P
EPS = 1e-6
HEADS = 8
HD = 64
STILES = 16
XH = 4
FT = 22
MH = 4
GG = 8
NE = 32
EG = 8
NG = 4
CAP = 64
MAXR = T // CAP
PAIRS = NE // 2
FE = 512
TWO_PI_HI = 6.28125
TWO_PI_LO = 2 * np.pi - 6.28125
ROUND = 12582912.0
GELU_C = 0.044715
GELU_K = float(np.sqrt(2 / np.pi))
RSQRT_SEED = 0x5F3759DF

UNITS = []
UNITS += [("u", i) for i in range(4)] + [("q", i) for i in range(4)] + [("k", i) for i in range(4)]
UNITS += [("v", i) for i in range(4)] + [("xk", i) for i in range(8)] + [("xv", i) for i in range(8)]
UNITS += [("gate", i) for i in range(16)] + [("glu", i) for i in range(2)]
for i in range(4):
    UNITS += [("ba", i), ("bs", i)]
UNITS += [("out", i) for i in range(8)] + [("xq", i) for i in range(8)] + [("xo", i) for i in range(8)]
for i in range(FT + 2):
    if i < FT:
        UNITS += [("fg", i), ("fv", i)]
    if i >= 2:
        UNITS += [("dn", i - 2)]
UNITS += [("v2", i) for i in range(4)] + [("qk2", i) for i in range(8)] + [("vg", i) for i in range(4)]
UNITS += [("ug", i) for i in range(4)] + [("o2", i) for i in range(4)] + [("out2", i) for i in range(8)]
UNIT_AT = {key: n for n, key in enumerate(UNITS)}
DENSE = len(UNITS)
PER_EXPERT = 12
assert DENSE % RING == 0 and PER_EXPERT % RING == 0

COLS = {}
for name, width in (("mix_pre", 8), ("mix_post", 8), ("xa_pre", 8), ("xa_post", 8), ("mem", 8), ("ffn_pre", 8),
                    ("ffn_post", 8), ("norm1", 8), ("norm2", 8), ("final", 8), ("b_gate", 16), ("d", 4),
                    ("b_glu", 4), ("conv0", 44), ("conv1", 44), ("conv2", 44), ("conv_b", 44), ("qk0", 8),
                    ("qk1", 8), ("qk2", 8), ("qk3", 8), ("g_mlstm", 4), ("g_v", 4), ("g_gmlp", 4)):
    COLS[name] = sum(w for _, w in COLS.values()), width
NCOLS = sum(w for _, w in COLS.values())

NORMS = ["mix_pre", "mem", "mix_post", "xa_pre", "xa_post", "ffn_pre", "ffn_post", "norm1", "norm2", "final"]


class BankRing:

    def __init__(self, banks, plan, freed):
        self.banks, self.plan, self.freed = banks, plan, freed
        self.at = {key: n for n, (key, _) in enumerate(plan)}

    def bank(self, key):
        return self.banks[self.at[key] % len(self.banks)]

    def claim(self, pe, key):
        before = self.at[key] - len(self.banks)
        if before >= 0:
            reader = self.plan[before][1]
            pe.wait_ge(self.freed[reader], sum(r == reader for _, r in self.plan[:before + 1]))

    def read(self, key):
        reader = self.plan[self.at[key]][1]
        return self.freed[reader], sum(r == reader for _, r in self.plan[:self.at[key] + 1])


def program(nc, dram, out):
    with ExitStack() as ctx:
        def sb(name, shape, dt=F32):
            return ctx.enter_context(nc.sbuf_tensor(name, shape, dt))

        def sem(name):
            return ctx.enter_context(nc.semaphore(name))

        ring = sb("ring", [P, RING, UNIT])
        x = sb("x", [P, KT, T])
        h = sb("h", [P, KT, T])
        sq = sb("sq", [P, KT, T])
        ident = sb("ident", [P, P])
        ones = sb("ones", [P, P])
        tri = sb("tri", [P, P])
        before = sb("before", [P, P])
        mask_lt = sb("mask_lt", [P, 3, P])
        mask_le = sb("mask_le", [P, 3, P])
        half_ones = sb("half_ones", [P, 2])
        head_sel = sb("head_sel", [MH, MH, P])
        slots = sb("slots", [P, CAP])
        cols = sb("cols", [P, NCOLS])
        hb = sb("hb", [P, 24])
        ms = sb("ms", [P, 24])
        ri = sb("ri", [P, 24], I32)
        rstd = sb("rstd", [P, 24])
        rt = sb("rt", [P, 24])
        rb = sb("rb", [P, T])
        arena = sb("arena", [P, 31136])
        bbd = sb("bbd", [P, 2, 4, P])

        def view(start, *shape, parts=P):
            n = int(np.prod(shape))
            v = arena[0:parts, start:start + n]
            if len(shape) == 1:
                return v
            names = "abcd"[:len(shape)]
            sizes = {names[i]: shape[i] for i in range(len(shape))}
            return v.rearrange(f"p ({' '.join(names)}) -> p {' '.join(names)}", **sizes)

        rot = view(0, 2, STILES, T)
        uT, qT, kT = view(8192, 4, T), view(9216, 4, T), view(10240, 4, T)
        v1 = view(11264, TT, 512)
        gates = view(12288, 16, T)
        xkT, xv = view(16384, KT, T), view(18432, TT, D)
        oT = view(20480, 4, T)
        yT = view(21504, 4, T)
        m1, m2, vr, wr = view(22528, 2, T), view(23040, 2, T), view(23552, 2, T), view(24064, 2, T)
        st = view(24576, 2, 2, T)
        zm, az, sp, w1 = view(25600, 384), view(25984, 384), view(26368, 384), view(26752, 384)
        zm = (zm, view(30752, 384))
        gt = view(22528, 4, T)
        cbd = view(27136, 2, STILES, 32)
        craw = view(24576, 2, STILES, 16)
        ta, tb = view(16384, STILES * 128), view(18432, STILES * 128)
        mem = view(28160, KT, T)
        powers = view(30208, 2, 2, STILES)
        ptmp = view(30272, 6, STILES)
        ssm = view(30368, 24, STILES)
        merged = view(0, KT, T)
        mg = view(2048, 2, 512)
        xqT = view(3072, KT, T)
        prob = view(5120, 2, T)
        probT = view(5632, 2, TT, T)
        xoT = view(6656, KT, T)
        post = view(8704, 2, T)
        sm = view(9216, 4, 8)
        up = view(9472, 3, 2, T + 4)
        acc = view(11040, 3, 2, T)
        fs = view(12576, 3, 2, T)
        hid = view(14112, 3, T)
        v2 = view(0, TT, 512)
        qk2 = view(1024, 8, T)
        qraw = view(3072, 2, 2, T + 4)
        qs = view(4112, 2, 2, T)
        gv = view(5136, TT, 512)
        gvs = view(6160, TT, 512)
        ug = view(7184, 4, T)
        ugs = view(8208, 4, T)
        so = view(9232, 4, T)
        hm = view(10256, 4, T)
        gm = view(11280, 4, T)
        mixw = view(12304, GG, P)
        bsp = view(13328, 4, P)
        ifr = view(13840, 10, T, parts=MH)
        gT = view(16400, TT, MH)
        decay = view(16408, 384)
        st2 = view(16792, 384)
        emb = view(17176, T)
        hden = view(17432, T)
        ycat = view(17688, KT, T)
        w_if = view(19736, KT, 8)
        b_if = view(19800, 2, parts=MH)
        vsum = view(19804, 2)
        qt = view(19808, 2, 2, T)
        xtok = view(0, TT, D)
        w_r = view(2048, KT, 36)
        b_r = view(2336, 36)
        lg = view(2400, TT, 36)
        rsm = view(2480, TT, 16)
        gsel = view(2512, TT, NG)
        lsel = view(2520, 4, TT, EG)
        lmask = view(2584, TT, NE)
        sel1, sel2 = view(2648, TT, EG), view(2664, TT, EG)
        first = view(2680, EG)
        selw = view(2688, TT, NE)
        selm = view(2752, TT, NE)
        rank = view(2816, TT, MAXR * NE + 4)
        wall = view(3080, TT, MAXR * NE + 4)
        gat = view(3344, 2, TT, CAP)
        scw = view(3600, TT, 2 * CAP)
        scwT = view(3856, T)
        xg = view(4112, 2, KT, CAP)
        ht = view(5136, 2, 4, CAP)
        hx = view(5648, 2, 4, CAP)
        yg = view(6160, D)
        cnt = view(7184, 4)
        zero = view(7200, 512)
        res = view(7712, KT, T)
        rounds = sb("rounds", [1, 1], I32)

        psum = [ctx.enter_context(nc.psum_tensor(f"psum{i}", [P, 512], F32)) for i in range(8)]
        STAT = psum[7]

        landed = [sem(f"landed{i}") for i in range(RING)]
        used = sem("used")
        s_x, s_mem, s_par = sem("x_in"), sem("mem_in"), sem("params_in")
        s_par2, s_par3 = sem("mixer2_params_in"), sem("router_params_in")
        s_out = sem("out_stored")
        consts = sem("consts_ready")
        squares, sums, scales, spread = sem("squares_ready"), sem("sums_ready"), sem("scales_ready"), sem("spread_ready")
        rb_ready = sem("spread_copied")
        h_ready, x_ready = sem("h_ready"), sem("x_ready")
        act_chain, dve_chain, pool_chain = sem("act_chain"), sem("dve_chain"), sem("pool_chain")
        p_freed = {"act": sem("pbank_freed_act"), "dve": sem("pbank_freed_dve")}
        x_freed = {"act": sem("xbank_freed_act"), "dve": sem("xbank_freed_dve")}
        dve_halves = sem("bias_halves")
        ssm_args, ssm_trig, ssm_ready = sem("ssm_args"), sem("ssm_trig"), sem("ssm_ready")
        bu_done, st_ready, y_done, y_freed = sem("bu_done"), sem("states_ready"), sem("y_done"), sem("y_freed")
        z_done, sp_ln, sp_ready = sem("z_done"), sem("softplus_ln"), sem("softplus_ready")
        cum_done, w_exp, w_ready = sem("cum_done"), sem("w_exp"), sem("w_ready")
        pv_done = sem("pv_done")
        gelu_sq, gelu_in, gelu_th = sem("gelu_squares"), sem("gelu_inner"), sem("gelu_tanh")
        y_ready, glu_th, ossm_ready = sem("y_ready"), sem("glu_tanh"), sem("ossm_ready")
        gates_th, merged_ready = sem("gates_tanh"), sem("merged_ready")
        sc_done, max_ready, prob_exp, prob_ready = sem("scores_done"), sem("max_ready"), sem("prob_exp"), sem("prob_ready")
        pt_done, pt_ready, xo_done = sem("probT_done"), sem("probT_ready"), sem("xo_done")
        up_ready, conv_g, hid_ready = sem("up_ready"), sem("conv_ready"), sem("hid_ready")
        if_done, if_ready, if_ln, if_rows, em_ready = (sem("if_done"), sem("if_ready"), sem("if_ln"),
                                                       sem("if_rows"), sem("em_ready"))
        gt_done, qpad = sem("gT_done"), sem("qk_padded")
        qk_raw, qk_conv, qk_th, qk_ready = sem("qk_raw"), sem("qk_conv"), sem("qk_tanh"), sem("qk_ready")
        rows_done, dec_in, dec_exp, s2_done, s2_ready = (sem("rows_done"), sem("decay_in"), sem("decay_exp"),
                                                         sem("scores2_done"), sem("scores2_ready"))
        em_copied, num_done, hm_ready, hsq = sem("em_copied"), sem("num_done"), sem("hm_ready"), sem("head_squares")
        vsq, vb_ready, mix_done, gm_ready = sem("v_squares"), sem("vb_ready"), sem("mix_done"), sem("gm_ready")
        so_th, hsum, hscale, hspread, ycat_ready = (sem("o_tanh"), sem("head_sums"), sem("head_scales"),
                                                    sem("head_spread"), sem("ycat_ready"))
        tr_done, tr_ready, lg_done = sem("tok_turned"), sem("tok_ready"), sem("logits_done")
        rt_max, rt_exp, sel_ready, rank_done, rank_ready = (sem("router_max"), sem("router_exp"), sem("sel_ready"),
                                                            sem("rank_done"), sem("rank_ready"))
        rounds_ready, y_zeroed = sem("rounds_ready"), sem("y_zeroed")
        g_ready, gath_done, xg_ready, hid_th, hx_ready = (sem("gather_ready"), sem("gather_done"), sem("xg_ready"),
                                                          sem("expert_tanh"), sem("hx_ready"))
        yg_ready, scw_ready, scwT_done, scwT_ready, scat_done = (sem("yg_ready"), sem("scatter_ready"),
                                                                 sem("scatterT_done"), sem("scatterT_ready"),
                                                                 sem("scatter_done"))
        silu_done = sem("silu_done")
        moe_done, res_ready = sem("moe_done"), sem("result_ready")

        pplan = [(("u", i), "act") for i in range(2)] + [(("q", i), "act") for i in range(2)]
        pplan += [(("k", i), "act") for i in range(2)] + [(("v", i), "act") for i in range(2)]
        pplan += [(("xk", i), "act") for i in range(4)] + [(("xv", i), "act") for i in range(4)]
        pplan += [(("gate", i), "act") for i in range(8)] + [(("glu", i), "act") for i in range(2)]
        for i in range(4):
            pplan += [(("ba", i), "dve"), (("bs", i), "dve")]
        pplan += [(("out", i), "dve") for i in range(4)] + [(("xq", i), "act") for i in range(4)]
        pplan += [(("xav", i), "act") for i in range(XH)]
        pplan += [(("xo", i), "dve") for i in range(4)] + [(("dn", i), "dve") for i in range(4)]
        pplan += [(("v2", i), "act") for i in range(2)] + [(("qk2", i), "act") for i in range(4)]
        pplan += [(("vg", i), "act") for i in range(2)] + [(("ug", i), "act") for i in range(2)]
        pplan += [(("o2", i), "act") for i in range(2)] + [(("out2", i), "dve") for i in range(4)]
        pb = BankRing(psum[0:4], pplan, p_freed)

        xplan = []
        for r in range(HEADS + 1):
            if r < HEADS:
                xplan += [(("bu", 2 * r), "dve"), (("z", r), "dve")]
            if r >= 1:
                xplan += [(("cum", r - 1), "dve")]
            if r < HEADS:
                xplan += [(("bu", 2 * r + 1), "dve")]
            if r >= 1:
                xplan += [(("pv", r - 1), "act")]
        for i in range(8 + 1):
            if i < 8:
                xplan += [(("sc", i), "act")]
            if i >= 1:
                xplan += [(("pt", i - 1), "act")]
        xplan += [(("up", i), "act") for i in range(FT)]
        xplan += [(("if", 0), "dve"), (("gT", 0), "act")]
        for i in range(MH + 1):
            if i < MH:
                xplan += [(("rows", i), "act")]
            if i >= 1:
                xplan += [(("num", i - 1), "dve")]
            if i < MH:
                xplan += [(("s2", i), "dve")]
        xplan += [(("mix", i), "dve") for i in range(2)] + [(("hsum", 0), "dve")]
        xplan += [(("hspread", i), "dve") for i in range(4)]
        xplan += [(("tr", i), "act") for i in range(4)]
        xplan += [(("lg", 0), "dve"), (("rank", 0), "dve")]
        xb = BankRing(psum[4:7], xplan, x_freed)

        def col(name, i=0):
            start = COLS[name][0] + i
            return cols[:, start:start + 1]

        block = ctx.enter_context(nc.Block())

        @block.sync
        def _(sp):
            sp.dma_start(x[:], dram["xT"]).then_inc(s_x, 16)
            for n in range(RING):
                sp.dma_start(ring[:, n], dram["stream"][n]).then_inc(landed[n], 16)
            stream = dram["stream"]
            with sp.Fori(1, (DENSE + NE * PER_EXPERT) // RING) as i:
                for s in range(RING):
                    sp.wait_ge(used, RING * i + (s + 1 - RING))
                    sp.dma_start(ring[:, s], stream[bass.ds(RING * i + s, 1)].rearrange("a p n -> p (a n)")
                                 ).then_inc(landed[s], 16)
            sp.wait_ge(rounds_ready, 1)
            n_rounds = sp.value_load(rounds[0:1, 0:1], min_val=1, max_val=MAXR)
            with sp.If(n_rounds > 1):
                with sp.Fori(1, n_rounds) as r:
                    with sp.Fori(0, NE) as i:
                        for s in range(RING):
                            sp.wait_ge(used, r * (NE * PER_EXPERT) + RING * i + (DENSE + s + 1 - RING))
                            sp.dma_start(ring[:, s], stream[bass.ds(RING * i + (DENSE + s), 1)].rearrange(
                                "a p n -> p (a n)")).then_inc(landed[s], 16)
            sp.wait_ge(res_ready, KT)
            sp.dma_start(out, res).then_inc(s_out, 16)
            sp.wait_ge(s_out, 16)

        @block.gpsimd
        def _(pool):
            n = [0]

            def link(ins):
                n[0] += 1
                ins.then_inc(pool_chain, 1)
                pool.wait_ge(pool_chain, n[0])

            pool.dma_start(cols[:], dram["cols"]).then_inc(s_par, 16)
            pool.dma_start(ssm[:, 0:3], dram["ssm_a"]).then_inc(s_par, 16)
            pool.dma_start(mem, dram["memT"]).then_inc(s_mem, 16)
            link(pool.memset(ones[:], 1.0))
            link(pool.memset(mask_lt[:], 1.0))
            link(pool.memset(mask_le[:], 1.0))
            link(pool.memset(head_sel[:], 1.0))
            link(pool.memset(half_ones[:], 1.0))
            link(pool.affine_select(out=ident[:], in_=ones[:], compare_op=ALU.is_equal, fill=0.0, base=0,
                                    pattern=[[-1, P]], channel_multiplier=1))
            link(pool.affine_select(out=tri[:], in_=ones[:], compare_op=ALU.is_ge, fill=0.0, base=0,
                                    pattern=[[-1, P]], channel_multiplier=1))
            link(pool.affine_select(out=before[:], in_=ones[:], compare_op=ALU.is_gt, fill=0.0, base=0,
                                    pattern=[[1, P]], channel_multiplier=-1))
            for b in (0, 2):
                link(pool.affine_select(out=mask_lt[:, b], in_=mask_lt[:, b], compare_op=ALU.is_gt, fill=0.0,
                                        base=0, pattern=[[1, P]], channel_multiplier=-1))
                link(pool.affine_select(out=mask_le[:, b], in_=mask_le[:, b], compare_op=ALU.is_ge, fill=0.0,
                                        base=0, pattern=[[1, P]], channel_multiplier=-1))
            link(pool.affine_select(out=head_sel[:], in_=head_sel[:], compare_op=ALU.is_equal, fill=0.0, base=0,
                                    pattern=[[-1, MH], [0, P]], channel_multiplier=1))
            link(pool.affine_select(out=half_ones[:, 0:1], in_=half_ones[:, 0:1], compare_op=ALU.is_gt, fill=0.0,
                                    base=64, pattern=[[0, 1]], channel_multiplier=-1))
            link(pool.affine_select(out=half_ones[:, 1:2], in_=half_ones[:, 1:2], compare_op=ALU.is_ge, fill=0.0,
                                    base=-64, pattern=[[0, 1]], channel_multiplier=1))
            link(pool.memset(bbd[:], 0.0))
            link(pool.memset(cbd[:], 0.0))
            for g in range(8):
                for c in range(2):
                    pool.dma_start(bbd[16 * g:16 * g + 16, c, :, (g % 2) * 64:(g % 2) * 64 + 64],
                                   dram["ssm_b"][16 * g:16 * g + 16, c]).then_inc(s_par, 16)
            pool.dma_start(craw[:], dram["ssm_c"]).then_inc(s_par, 16)
            pool.iota(slots[:], pattern=[[1, CAP]], base=0, channel_multiplier=0,
                      allow_small_or_imprecise_dtypes=True).then_inc(consts, 1)
            pool.wait_ge(used, UNIT_AT["dn", FT - 1] + 1)
            pool.dma_start(mixw, dram["mixw"]).then_inc(s_par2, 16)
            for g in range(2):
                pool.dma_start(bsp[64 * g:64 * g + 64], bass.AP(
                    tensor=dram["bsp"].tensor, offset=g * P, ap=[[0, 64], [2 * P, 4], [1, P]])).then_inc(s_par2, 16)
            pool.dma_start(w_if, dram["w_if"]).then_inc(s_par2, 16)
            pool.dma_start(b_if, dram["b_if"]).then_inc(s_par2, 16)
            pool.wait_ge(used, UNIT_AT["out2", 7] + 1)
            pool.dma_start(w_r, dram["w_r"]).then_inc(s_par3, 16)
            pool.dma_start(b_r, bass.AP(tensor=dram["b_r"].tensor, offset=0, ap=[[0, P], [1, 36]])
                           ).then_inc(s_par3, 16)

        @block.scalar
        def _(act):
            n = [0]

            def link(ins):
                n[0] += 1
                ins.then_inc(act_chain, 1)
                act.wait_ge(act_chain, n[0])

            def square_input(norm, src):
                if norm:
                    act.wait_ge(sums, norm)
                for i in range(4):
                    act.activation(sq[:, 2 * i:2 * i + 2], src[:, 2 * i:2 * i + 2], ACT.Square).then_inc(squares, 1)

            def square_banks(norm, key, unit):
                act.wait_ge(sums, norm)
                for i in range(4):
                    act.wait_ge(used, UNIT_AT[unit(i)] + 1)
                    act.activation(sq[:, 2 * i:2 * i + 2].rearrange("p a t -> p (a t)"), pb.bank((key, i))[:],
                                   ACT.Square).then_inc(squares, 1)

            def copy_spread(norm):
                act.wait_ge(spread, norm + 1)
                act.copy(rb[:], STAT[:, T:2 * T]).then_inc(rb_ready, 1)

            def evict(key, unit, dst, scale=None):
                act.wait_ge(used, UNIT_AT[unit] + 1)
                if scale is None:
                    act.copy(dst, pb.bank(key)[:]).then_inc(p_freed["act"], 1)
                else:
                    act.mul(dst, pb.bank(key)[:], scale).then_inc(p_freed["act"], 1)

            def two(v, i):
                return v[:, 2 * i:2 * i + 2].rearrange("p a t -> p (a t)")

            act.wait_ge(s_x, 16)
            square_input(0, x)
            act.wait_ge(s_par, 16 * 19)
            act.activation(ssm[:, 3], ssm[:, 2], ACT.Exp).then_inc(ssm_trig, 1)
            act.wait_ge(ssm_args, 1)
            act.activation(ssm[:, 6], ssm[:, 4], ACT.Exp).then_inc(ssm_trig, 1)
            act.wait_ge(ssm_args, 2)
            act.activation(ssm[:, 10], ssm[:, 8], ACT.Sin).then_inc(ssm_trig, 1)
            act.activation(ssm[:, 11], ssm[:, 9], ACT.Sin).then_inc(ssm_trig, 1)
            act.wait_ge(s_mem, 16)
            square_input(1, mem)
            for i in range(2):
                evict(("u", i), ("u", 2 * i + 1), two(uT, i))
            for i in range(2):
                evict(("q", i), ("q", 2 * i + 1), two(qT, i), HD ** -0.5)
            for i in range(2):
                evict(("k", i), ("k", 2 * i + 1), two(kT, i))
            for i in range(2):
                evict(("v", i), ("v", 3), v1[:, i])

            def filler(slot):
                if slot == 0:
                    act.wait_ge(ssm_ready, 2)
                if slot < 4:
                    evict(("xk", slot), ("xk", 2 * slot + 1), two(xkT, slot))
                elif slot < 8:
                    if slot % 2:
                        half = (slot - 4) // 2
                        for tt in range(TT):
                            evict(("xv", 2 * half + tt), ("xv", 4 * half + 3), xv[:, tt, half * 512:half * 512 + 512])
                else:
                    i = slot - 8
                    if i == 0:
                        act.wait_ge(dve_halves, 1)
                    act.wait_ge(used, UNIT_AT[("gate", 2 * i + 1)] + 1)
                    for c in range(2):
                        ins = act.activation(gates[:, 2 * i + c], pb.bank(("gate", i))[:, c * T:c * T + T], ACT.Identity,
                                             bias=hb[:, 2 * i + c:2 * i + c + 1], scale=0.5)
                    ins.then_inc(p_freed["act"], 1)

            for r in range(HEADS + 1):
                if r < HEADS:
                    act.wait_ge(*xb.read(("z", r)))
                    if r:
                        act.wait_ge(sp_ready, r)
                    link(act.activation(az, zm[r % 2], ACT.Abs))
                    link(act.activation(az, az, ACT.Exp, scale=-1.0))
                    act.activation(az, az, ACT.Ln, bias=1.0).then_inc(sp_ln, 1)
                    filler(2 * r)
                if r:
                    act.wait_ge(*xb.read(("cum", r - 1)))
                    act.activation(w1, w1, ACT.Exp).then_inc(w_exp, 1)
                if r < HEADS:
                    filler(2 * r + 1)
                if r:
                    hd = r - 1
                    lo = HD * (hd % 2)
                    act.wait_ge(pv_done, r)
                    act.copy(oT[lo:lo + HD, hd // 2], xb.bank(("pv", hd))[lo:lo + HD, 0:T]).then_inc(x_freed["act"], 1)

            act.wait_ge(y_freed, 4)
            act.activation(gt, yT, ACT.Square).then_inc(gelu_sq, 1)
            act.wait_ge(gelu_in, 1)
            act.activation(gt, gt, ACT.Tanh, scale=GELU_K * GELU_C).then_inc(gelu_th, 1)
            act.activation(gates, gates, ACT.Tanh).then_inc(gates_th, 1)
            for i in range(2):
                act.wait_ge(used, UNIT_AT[("glu", i)] + 1)
                if i == 0:
                    act.wait_ge(y_ready, 1)
                for c in range(2):
                    ins = act.activation(gt[:, 2 * i + c], pb.bank(("glu", i))[:, c * T:c * T + T], ACT.Tanh,
                                         bias=hb[:, 16 + 2 * i + c:17 + 2 * i + c], scale=0.5)
                ins.then_inc(p_freed["act"], 1)
            square_banks(2, "out", lambda i: ("out", 2 * i + 1))
            copy_spread(2)

            act.wait_ge(x_ready, 4)
            square_input(3, x)
            for i in range(4):
                evict(("xq", i), ("xq", 2 * i + 1), two(xqT, i), (D // XH) ** -0.5)
            for i in range(8 + 1):
                if i < 8:
                    act.wait_ge(max_ready, i + 1)
                    if i >= 2:
                        act.wait_ge(pt_done, i - 1)
                    act.activation(prob[:, i % 2], xb.bank(("sc", i))[:, 0:T], ACT.Exp, bias=sm[:, 0, i:i + 1],
                                   accum_out=sm[:, 1, i:i + 1]).then_inc(x_freed["act"], 1)
                if i:
                    hh, tt = (i - 1) // 2, (i - 1) % 2
                    act.wait_ge(pt_done, i)
                    if hh >= 2 and tt == 0:
                        act.wait_ge(xo_done, hh - 1)
                    act.copy(probT[:, hh % 2, :, tt * P:tt * P + P],
                             xb.bank(("pt", i - 1))[:, 0:T].rearrange("p (m t) -> p m t", m=TT)
                             ).then_inc(x_freed["act"], 1)
                    if tt:
                        act.wait_ge(xo_done, hh + 1)
                        act.copy(two(xoT, hh), pb.bank(("xav", hh))[:]).then_inc(p_freed["act"], 1)
            square_banks(4, "xo", lambda i: ("xo", 2 * i + 1))
            copy_spread(4)

            act.wait_ge(x_ready, 8)
            square_input(5, x)
            for j in range(FT):
                b = j % 3
                act.wait_ge(used, UNIT_AT[("fv", j)] + 1)
                if j >= 3:
                    act.wait_ge(hid_ready, j - 2)
                bank = xb.bank(("up", j))
                act.copy(up[:, b, :, 4:4 + T], bank[:].rearrange("p (c t) -> p c t", c=2))
                for c in range(2):
                    ins = act.activation(acc[:, b, c], bank[:, c * T:c * T + T], ACT.Identity,
                                         bias=col("conv_b", FT * c + j), scale=col("conv2", FT * c + j))
                ins.then_inc(x_freed["act"], 1)
                act.wait_ge(conv_g, j + 1)
                act.activation(fs[:, b, 0], acc[:, b, 0], ACT.Square).then_inc(gelu_sq, 1)
                act.wait_ge(gelu_in, j + 2)
                act.activation(fs[:, b, 0], fs[:, b, 0], ACT.Tanh, scale=GELU_K * GELU_C).then_inc(gelu_th, 1)
            square_banks(6, "dn", lambda i: ("dn", FT - 1))
            copy_spread(6)
            act.wait_ge(x_ready, 12)
            square_input(7, x)

            act.wait_ge(if_ready, 1)
            link(act.activation(ifr[:, 2], ifr[:, 1], ACT.Abs))
            link(act.activation(ifr[:, 2], ifr[:, 2], ACT.Exp, scale=-1.0))
            act.activation(ifr[:, 2], ifr[:, 2], ACT.Ln, bias=1.0).then_inc(if_ln, 1)
            for i in range(2):
                evict(("v2", i), ("v2", 3), v2[:, i])
            act.wait_ge(if_rows, 1)
            act.activation(ifr[:, 7], ifr[:, 7], ACT.Exp).then_inc(em_ready, 1)
            act.wait_ge(gt_done, 1)
            act.copy(gT, xb.bank(("gT", 0))[:, 0:TT * MH].rearrange("p (a b) -> p a b", a=TT)
                     ).then_inc(x_freed["act"], 1)
            for i in range(4):
                act.wait_ge(used, UNIT_AT[("qk2", 2 * i + 1)] + 1)
                if i >= 2:
                    act.wait_ge(qk_ready, i - 1)
                bank = pb.bank(("qk2", i))
                act.copy(qraw[:, i % 2, :, 4:4 + T], bank[:].rearrange("p (c t) -> p c t", c=2))
                for c in range(2):
                    ins = act.mul(qs[:, i % 2, c], bank[:, c * T:c * T + T], col("qk3", 2 * i + c))
                ins.then_inc(p_freed["act"], 1)
                act.wait_ge(qk_conv, i + 1)
                act.activation(qt[:, i % 2], qs[:, i % 2], ACT.Tanh, scale=0.5).then_inc(qk_th, 1)

            def gelu2(g, key, unit, keep, scratch):
                act.wait_ge(used, UNIT_AT[unit] + 1)
                act.copy(keep, pb.bank(key)[:])
                act.activation(scratch, pb.bank(key)[:], ACT.Square).then_inc(p_freed["act"], 1)
                act.wait_ge(gelu_in, g + 1)
                act.activation(scratch, scratch, ACT.Tanh, scale=GELU_K * GELU_C).then_inc(gelu_th, 1)

            for tt in range(TT):
                gelu2(FT + 1 + tt, ("vg", tt), ("vg", 3), gv[:, tt], gvs[:, tt])
            for tt in range(TT):
                act.wait_ge(vb_ready, tt + 1)
                act.activation(gvs[:, tt], gv[:, tt], ACT.Square, accum_out=vsum[:, tt:tt + 1]).then_inc(vsq, 1)
            for i in range(2):
                gelu2(FT + 3 + i, ("ug", i), ("ug", 2 * i + 1), two(ug, i), two(ugs, i))
            for i in range(2):
                act.wait_ge(used, UNIT_AT[("o2", 2 * i + 1)] + 1)
                act.activation(two(so, i), pb.bank(("o2", i))[:], ACT.Tanh, scale=0.5).then_inc(p_freed["act"], 1)
            for i in range(MH):
                act.wait_ge(dec_in, i + 1)
                act.activation(decay, decay, ACT.Exp, scale=-1.0).then_inc(dec_exp, 1)
                if i:
                    act.wait_ge(hm_ready, i)
                act.copy(emb, xb.bank(("rows", i))[:, T:2 * T]).then_inc(x_freed["act"], 1)
            act.wait_ge(hm_ready, MH)
            act.activation(sq[:, 0:4], hm, ACT.Square).then_inc(hsq, 1)
            act.wait_ge(gm_ready, 1)
            act.activation(sq[:, 4:8], gm, ACT.Square).then_inc(hsq, 1)
            act.wait_ge(hsum, 1)
            act.wait_ge(x_ready, 16)
            square_input(8, x)

            for i in range(4):
                act.wait_ge(tr_done, i + 1)
                act.copy(xtok[:, i // 2, (i % 2) * 512:(i % 2) * 512 + 512], xb.bank(("tr", i))[:]
                         ).then_inc(x_freed["act"], 1)
            for tt in range(TT):
                act.wait_ge(rt_max, tt + 1)
                act.activation(rsm[:, tt, 8:12], lg[:, tt, 0:NG], ACT.Exp, bias=rsm[:, tt, 0:1],
                               accum_out=rsm[:, tt, 1:2]).then_inc(rt_exp, 1)
            for tt in range(TT):
                act.wait_ge(rt_max, TT + tt + 1)
                act.activation(rsm[:, tt, 4:5], rsm[:, tt, 3:4], ACT.Exp).then_inc(rt_exp, 1)
            act.wait_ge(rounds_ready, 1)
            n_pairs = act.value_load(rounds[0:1, 0:1], min_val=1, max_val=MAXR) * PAIRS
            act.wait_ge(gath_done, 1)
            act.copy(xg[:, 0].rearrange("p k c -> p (k c)"), psum[4][:]).then_inc(xg_ready, 1)
            with act.Fori(0, n_pairs) as it:
                for e in range(2):
                    act.wait_ge(used, it * (2 * PER_EXPERT) + (DENSE + PER_EXPERT * e + 8))
                    act.wait_ge(hx_ready, 2 * it + (e + 1))
                    act.activation(ht[:, 0], psum[5][:, 0:4 * CAP].rearrange("p (f c) -> p f c", f=4), ACT.Tanh,
                                   scale=0.5).then_inc(hid_th, 1)
                    act.wait_ge(gath_done, 2 * it + (2 + e))
                    act.copy(xg[:, 1 - e].rearrange("p k c -> p (k c)"), psum[4][:]).then_inc(xg_ready, 1)
                act.wait_ge(used, it * (2 * PER_EXPERT) + (DENSE + 2 * PER_EXPERT))
                act.wait_ge(scat_done, it + 1)
                for c in range(2):
                    act.copy(yg[:, c * 512:c * 512 + 512], psum[6 + c][:]).then_inc(yg_ready, 1)
            act.wait_ge(x_ready, 20)
            square_input(9, x)

        @block.vector
        def _(dve):
            n = [0]

            def link(ins):
                n[0] += 1
                ins.then_inc(dve_chain, 1)
                dve.wait_ge(dve_chain, n[0])

            def two(v, i):
                return v[:, 2 * i:2 * i + 2].rearrange("p a t -> p (a t)")

            def ts(o, a, s1, op0, s2=None, op1=None):
                if op1 is None:
                    return dve.tensor_scalar(o, a, s1, None, op0)
                return dve.tensor_scalar(o, a, s1, s2, op0, op1)

            def tt_(o, a, b, op):
                return dve.tensor_tensor(o, a, b, op)

            def stt(o, a, s1, b, op0, op1):
                return dve.scalar_tensor_tensor(out=o, in0=a, scalar=s1, in1=b, op0=op0, op1=op1)

            def rsqrt(w):
                a, y, t = ms[:, 0:w], rstd[:, 0:w], rt[:, 0:w]
                link(ts(ri[:, 0:w], a.bitcast(I32), 1, ALU.logical_shift_right))
                link(ts(y.bitcast(I32), ri[:, 0:w], -1, ALU.mult, RSQRT_SEED, ALU.add))
                for step in range(4):
                    link(tt_(t, y, y, ALU.mult))
                    link(tt_(t, t, a, ALU.mult))
                    link(ts(t, t, -0.5, ALU.mult, 1.5, ALU.add))
                    if step < 3:
                        link(tt_(y, y, t, ALU.mult))
                return tt_(y, y, t, ALU.mult)

            def norm_scale(norm):
                dve.wait_ge(sums, norm + 1)
                link(ts(ms[:, 0:TT], STAT[:, 0:TT], 1.0 / D, ALU.mult, EPS, ALU.add))
                rsqrt(TT).then_inc(scales, 1)

            def normed(norm, src, dst, done):
                dve.wait_ge(spread, norm + 1)
                for k in range(KT):
                    stt(dst[:, k], src[:, k], col(NORMS[norm], k), STAT[:, T:2 * T], ALU.mult, ALU.mult
                        ).then_inc(done, 1)

            def add_normed(norm, key, copied):
                dve.wait_ge(rb_ready, copied)
                for i in range(4):
                    bank = pb.bank((key, i))
                    if i:
                        dve.wait_ge(x_ready, done_x[0])
                    for c in range(2):
                        ins = stt(post[:, c], bank[:, c * T:c * T + T], col(NORMS[norm], 2 * i + c), rb[:],
                                  ALU.mult, ALU.mult)
                    ins.then_inc(p_freed["dve"], 1)
                    dve.wait_ge(*pb.read((key, i)))
                    tt_(x[:, 2 * i:2 * i + 2], x[:, 2 * i:2 * i + 2], post, ALU.add).then_inc(x_ready, 1)
                    done_x[0] += 1

            done_x = [0]

            norm_scale(0)
            dve.wait_ge(s_par, 16 * 19)
            normed(0, x, h, h_ready)
            ts(hb[:, 0:16], cols[:, COLS["b_gate"][0]:COLS["b_gate"][0] + 16], 0.5, ALU.mult)
            ts(hb[:, 16:20], cols[:, COLS["b_glu"][0]:COLS["b_glu"][0] + 4], 0.5, ALU.mult).then_inc(dve_halves, 1)
            are, aim, dt, adt, th = ssm[:, 0], ssm[:, 1], ssm[:, 3], ssm[:, 4], ssm[:, 5]
            rad, turns, ang, cang, sin, cos = ssm[:, 6], ssm[:, 7], ssm[:, 8], ssm[:, 9], ssm[:, 10], ssm[:, 11]
            lr, li, den, num = ssm[:, 12], ssm[:, 13], ssm[:, 15], ssm[:, 16]
            t1, t2, fre, fim = ssm[:, 17], ssm[:, 18], ssm[:, 19], ssm[:, 20]
            dve.wait_ge(ssm_trig, 1)
            tt_(adt, are, dt, ALU.mult).then_inc(ssm_args, 1)
            link(tt_(th, aim, dt, ALU.mult))
            link(ts(turns, th, 1.0 / (2 * np.pi), ALU.mult, ROUND, ALU.add))
            link(ts(turns, turns, -ROUND, ALU.add))
            link(stt(ang, turns, -TWO_PI_HI, th, ALU.mult, ALU.add))
            link(stt(ang, turns, -TWO_PI_LO, ang, ALU.mult, ALU.add))
            link(ts(ang, ang, 3.1415925, ALU.min, -3.1415925, ALU.max))
            link(ts(t1, ang, -1.0, ALU.mult))
            link(tt_(t1, t1, ang, ALU.max))
            ts(cang, t1, -1.0, ALU.mult, np.pi / 2, ALU.add).then_inc(ssm_args, 1)
            norm_scale(1)
            normed(1, mem, mem, h_ready)
            dve.wait_ge(ssm_trig, 4)
            link(tt_(lr, rad, cos, ALU.mult))
            link(tt_(li, rad, sin, ALU.mult))
            link(ts(num, lr, -1.0, ALU.add))
            link(tt_(t1, are, are, ALU.mult))
            link(tt_(t2, aim, aim, ALU.mult))
            link(tt_(den, t1, t2, ALU.add))
            link(dve.reciprocal(den, den))
            link(tt_(t1, num, are, ALU.mult))
            link(tt_(t2, li, aim, ALU.mult))
            link(tt_(t1, t1, t2, ALU.add))
            link(tt_(fre, t1, den, ALU.mult))
            link(tt_(t1, li, are, ALU.mult))
            link(tt_(t2, num, aim, ALU.mult))
            link(tt_(t1, t1, t2, ALU.subtract))
            link(tt_(fim, t1, den, ALU.mult))
            link(dve.tensor_copy(powers[:, 0, 0], cos))
            link(dve.tensor_copy(powers[:, 0, 1], sin))
            link(dve.memset(rot[:, 0, :, 0:1], 1.0))
            link(dve.memset(rot[:, 1, :, 0:1], 0.0))
            k, w = 0, 1
            while w < T:
                c_, s_ = powers[:, k % 2, 0], powers[:, k % 2, 1]
                cb, sbb = (v.unsqueeze(2).to_broadcast([P, STILES, w]) for v in (c_, s_))
                a3 = ta[:, 0:STILES * w].rearrange("p (j t) -> p j t", j=STILES)
                b3 = tb[:, 0:STILES * w].rearrange("p (j t) -> p j t", j=STILES)
                tt_(a3, rot[:, 0, :, 0:w], cb, ALU.mult)
                link(tt_(b3, rot[:, 1, :, 0:w], sbb, ALU.mult))
                link(tt_(rot[:, 0, :, w:2 * w], a3, b3, ALU.subtract))
                tt_(a3, rot[:, 0, :, 0:w], sbb, ALU.mult)
                link(tt_(b3, rot[:, 1, :, 0:w], cb, ALU.mult))
                link(tt_(rot[:, 1, :, w:2 * w], a3, b3, ALU.add))
                if 2 * w < T:
                    tt_(ptmp[:, 0], c_, c_, ALU.mult)
                    tt_(ptmp[:, 1], s_, s_, ALU.mult)
                    link(tt_(ptmp[:, 2], c_, s_, ALU.mult))
                    tt_(powers[:, (k + 1) % 2, 0], ptmp[:, 0], ptmp[:, 1], ALU.subtract)
                    link(ts(powers[:, (k + 1) % 2, 1], ptmp[:, 2], 2.0, ALU.mult))
                k, w = k + 1, 2 * w
            fr, fi = (v.unsqueeze(2).to_broadcast([P, STILES, 16]) for v in (fre, fim))
            a3 = ta[:, 0:256].rearrange("p (j t) -> p j t", j=STILES)
            b3 = tb[:, 0:256].rearrange("p (j t) -> p j t", j=STILES)
            tt_(a3, craw[:, 0], fr, ALU.mult)
            link(tt_(b3, craw[:, 1], fi, ALU.mult))
            for g in range(2):
                link(tt_(cbd[64 * g:64 * g + 64, 0, :, 16 * g:16 * g + 16], a3[64 * g:64 * g + 64],
                         b3[64 * g:64 * g + 64], ALU.subtract))
            tt_(a3, craw[:, 0], fi, ALU.mult)
            link(tt_(b3, craw[:, 1], fr, ALU.mult))
            for g in range(2):
                stt(cbd[64 * g:64 * g + 64, 1, :, 16 * g:16 * g + 16], a3[64 * g:64 * g + 64], -1.0,
                    b3[64 * g:64 * g + 64], ALU.mult, ALU.subtract).then_inc(ssm_ready, 1)
            dve.wait_ge(ssm_ready, 2)

            def turned(j, which):
                return rot[:, which, j].unsqueeze(1).to_broadcast([P, 2, T])

            def recurrence(j):
                dve.wait_ge(bu_done, j + 1)
                bank = xb.bank(("bu", j))[:].rearrange("p (c t) -> p c t", c=2)
                tt_(m1, bank, turned(j, 0), ALU.mult)
                tt_(m2, bank, turned(j, 1), ALU.mult).then_inc(x_freed["dve"], 1)
                dve.wait_ge(*xb.read(("bu", j)))
                tt_(vr[:, 0], m1[:, 0], m2[:, 1], ALU.add)
                link(tt_(vr[:, 1], m1[:, 1], m2[:, 0], ALU.subtract))
                r_ = rad[:, j:j + 1].to_broadcast([P, T])
                for c in range(2):
                    ins = dve.tensor_tensor_scan(wr[:, c], r_, vr[:, c], 0.0, ALU.mult, ALU.add)
                link(ins)
                tt_(m1, wr, turned(j, 0), ALU.mult)
                link(tt_(m2, wr, turned(j, 1), ALU.mult))
                if j >= 2:
                    dve.wait_ge(y_done, j - 1)
                tt_(st[:, j % 2, 0], m1[:, 0], m2[:, 1], ALU.subtract)
                tt_(st[:, j % 2, 1], m1[:, 1], m2[:, 0], ALU.add).then_inc(st_ready, 1)
                dve.wait_ge(st_ready, j + 1)

            def y_out(i):
                dve.wait_ge(y_done, 4 * i + 4)
                stt(yT[:, i], uT[:, i], col("d", i), STAT[:, 0:T], ALU.mult, ALU.add).then_inc(y_freed, 1)

            for r in range(HEADS + 1):
                if r >= 3 and r % 2:
                    y_out((r - 3) // 2)
                if r < HEADS:
                    recurrence(2 * r)
                    dve.wait_ge(z_done, r + 1)
                    tt_(zm[r % 2], xb.bank(("z", r))[:, 0:384], mask_lt[:].rearrange("p a t -> p (a t)"), ALU.mult
                        ).then_inc(x_freed["dve"], 1)
                    dve.wait_ge(*xb.read(("z", r)))
                if r:
                    dve.wait_ge(cum_done, r)
                    if r >= 2:
                        dve.wait_ge(pv_done, r - 1)
                    tt_(w1, zm[(r - 1) % 2], xb.bank(("cum", r - 1))[:, 0:384], ALU.subtract
                        ).then_inc(x_freed["dve"], 1)
                if r < HEADS:
                    recurrence(2 * r + 1)
                    dve.wait_ge(sp_ln, r + 1)
                    link(stt(sp, zm[r % 2], 0.0, az, ALU.max, ALU.add))
                    tt_(sp, sp, mask_lt[:].rearrange("p a t -> p (a t)"), ALU.mult).then_inc(sp_ready, 1)
                if r:
                    dve.wait_ge(w_exp, r)
                    tt_(w1, w1, mask_lt[:].rearrange("p a t -> p (a t)"), ALU.mult).then_inc(w_ready, 1)
            y_out(3)
            dve.wait_ge(y_freed, 4)
            dve.wait_ge(gelu_sq, 1)
            stt(gt, gt, 1.0 / GELU_C, yT, ALU.add, ALU.mult).then_inc(gelu_in, 1)
            dve.wait_ge(gelu_th, 1)
            link(ts(gt, gt, 0.5, ALU.mult, 0.5, ALU.add))
            tt_(yT, gt, yT, ALU.mult).then_inc(y_ready, 1)
            dve.wait_ge(gates_th, 1)
            link(ts(gates, gates, 0.5, ALU.mult, 0.5, ALU.add))
            dve.wait_ge(*pb.read(("glu", 1)))
            link(ts(gt, gt, 0.5, ALU.mult, 0.5, ALU.add))
            tt_(gt, gt, yT, ALU.mult).then_inc(ossm_ready, 1)
            for i in range(4):
                for c, key in enumerate(("ba", "bs")):
                    dve.wait_ge(used, UNIT_AT[(key, i)] + 1)
                    if i and c == 0:
                        dve.wait_ge(merged_ready, i)
                    tt_(mg[:, c], two(gates, 4 * c + i), pb.bank((key, i))[:], ALU.mult).then_inc(p_freed["dve"], 1)
                    dve.wait_ge(*pb.read((key, i)))
                tt_(two(merged, i), mg[:, 0], mg[:, 1], ALU.add).then_inc(merged_ready, 1)
            norm_scale(2)
            add_normed(2, "out", 1)

            norm_scale(3)
            normed(3, x, h, h_ready)
            for i in range(8 + 1):
                if i < 8:
                    dve.wait_ge(sc_done, i + 1)
                    link(dve.tensor_reduce(sm[:, 2, i:i + 1], xb.bank(("sc", i))[:, 0:T], AX.X, ALU.max))
                    ts(sm[:, 0, i:i + 1], sm[:, 2, i:i + 1], -1.0, ALU.mult).then_inc(max_ready, 1)
                if i:
                    dve.wait_ge(*xb.read(("sc", i - 1)))
                    link(dve.reciprocal(sm[:, 3, i - 1:i], sm[:, 1, i - 1:i]))
                    ts(prob[:, (i - 1) % 2], prob[:, (i - 1) % 2], sm[:, 3, i - 1:i], ALU.mult
                       ).then_inc(prob_ready, 1)
            norm_scale(4)
            add_normed(4, "xo", 2)

            norm_scale(5)
            normed(5, x, h, h_ready)
            link(dve.memset(up[:, :, :, 0:4], 0.0))
            for j in range(FT):
                b = j % 3
                dve.wait_ge(*xb.read(("up", j)))
                for tap, lag in ((1, 1), (0, 2)):
                    for c in range(2):
                        ins = stt(acc[:, b, c], up[:, b, c, 4 - lag:4 - lag + T], col(f"conv{tap}", FT * c + j),
                                  acc[:, b, c], ALU.mult, ALU.add)
                    if tap:
                        link(ins)
                ins.then_inc(conv_g, 1)
                dve.wait_ge(conv_g, j + 1)
                dve.wait_ge(gelu_sq, j + 2)
                stt(fs[:, b, 0], fs[:, b, 0], 1.0 / GELU_C, acc[:, b, 0], ALU.add, ALU.mult).then_inc(gelu_in, 1)
                dve.wait_ge(gelu_th, j + 2)
                link(stt(fs[:, b, 1], fs[:, b, 0], 1.0, acc[:, b, 0], ALU.add, ALU.mult))
                if j >= 3:
                    dve.wait_ge(used, UNIT_AT[("dn", j - 3)] + 1)
                stt(hid[:, b], fs[:, b, 1], 0.5, acc[:, b, 1], ALU.mult, ALU.mult).then_inc(hid_ready, 1)
            norm_scale(6)
            add_normed(6, "dn", 3)

            norm_scale(7)
            normed(7, x, h, h_ready)
            dve.wait_ge(s_par2, 16 * 5)
            dve.wait_ge(if_done, 1)
            bank = xb.bank(("if", 0))
            ts(ifr[:, 1], bank[0:MH, T:2 * T], b_if[:, 1:2], ALU.add).then_inc(if_ready, 1)
            link(ts(ifr[:, 0], bank[0:MH, 0:T], b_if[:, 0:1], ALU.add))
            link(dve.memset(ifr[:, 9], 1.0))
            tt_(mixw, mixw, mask_le[:, 0].unsqueeze(1).to_broadcast([P, GG, P]), ALU.mult).then_inc(x_freed["dve"], 1)
            dve.wait_ge(*xb.read(("if", 0)))
            dve.wait_ge(if_ln, 1)
            link(stt(ifr[:, 3], ifr[:, 1], 0.0, ifr[:, 2], ALU.min, ALU.subtract))
            link(dve.tensor_tensor_scan(ifr[:, 4], ifr[:, 9], ifr[:, 3], 0.0, ALU.mult, ALU.add))
            link(tt_(ifr[:, 5], ifr[:, 0], ifr[:, 4], ALU.subtract))
            link(dve.tensor_tensor_scan(ifr[:, 6], ifr[:, 5], ifr[:, 5], 0.0, ALU.max, ALU.max))
            link(tt_(ifr[:, 7], ifr[:, 4], ifr[:, 6], ALU.add))
            ts(ifr[:, 7], ifr[:, 7], -1.0, ALU.mult, 87.0, ALU.min).then_inc(if_rows, 1)
            link(dve.memset(qraw[:, :, :, 0:4], 0.0))
            dve.wait_ge(if_rows, 1)
            dve.nop().then_inc(qpad, 1)
            for i in range(4):
                b = i % 2
                dve.wait_ge(*pb.read(("qk2", i)))
                for tap in (2, 1, 0):
                    for c in range(2):
                        ins = stt(qs[:, b, c], qraw[:, b, c, 1 + tap:1 + tap + T], col(f"qk{tap}", 2 * i + c),
                                  qs[:, b, c], ALU.mult, ALU.add)
                    if tap:
                        link(ins)
                ins.then_inc(qk_conv, 1)
                dve.wait_ge(qk_th, i + 1)
                stt(qk2[:, 2 * i:2 * i + 2], qt[:, b], 1.0, qs[:, b], ALU.add, ALU.mult).then_inc(qk_ready, 1)

            def gelu2(g, keep, scratch):
                stt(scratch, scratch, 1.0 / GELU_C, keep, ALU.add, ALU.mult).then_inc(gelu_in, 1)
                dve.wait_ge(gelu_th, g + 1)
                link(ts(scratch, scratch, 0.5, ALU.mult, 0.5, ALU.add))
                return tt_(keep, keep, scratch, ALU.mult)

            for tt in range(TT):
                dve.wait_ge(*pb.read(("vg", tt)))
                gelu2(FT + 1 + tt, gv[:, tt], gvs[:, tt]).then_inc(vb_ready, 1)
            for tt in range(TT):
                dve.wait_ge(vsq, tt + 1)
            link(ts(ms[:, 0:TT], vsum, 1.0 / 512, ALU.mult, EPS, ALU.add))
            link(rsqrt(TT))
            for tt in range(TT):
                ts(gv[:, tt], gv[:, tt], rstd[:, tt:tt + 1], ALU.mult).then_inc(vb_ready, 1)
            for i in range(2):
                dve.wait_ge(*pb.read(("ug", i)))
                link(gelu2(FT + 3 + i, two(ug, i), two(ugs, i)))
            dve.wait_ge(*pb.read(("o2", 1)))
            link(ts(so, so, 0.5, ALU.mult, 0.5, ALU.add))
            c2 = 0.25 * P ** -0.5
            for i in range(MH):
                dve.wait_ge(rows_done, i + 1)
                bank = xb.bank(("rows", i))
                ts(decay[:, 0:T], bank[:, 0:T], gT[:, 0, i:i + 1], ALU.subtract, 0.0, ALU.max)
                ts(decay[:, T:384], bank[:, P:T], gT[:, 1, i:i + 1], ALU.subtract, 0.0, ALU.max).then_inc(dec_in, 1)
                dve.wait_ge(dec_exp, i + 1)
                link(tt_(decay, decay, mask_le[:].rearrange("p a t -> p (a t)"), ALU.mult))
                dve.wait_ge(s2_done, i + 1)
                stt(st2, xb.bank(("s2", i))[:, 0:384], c2, decay, ALU.mult, ALU.mult).then_inc(x_freed["dve"], 1)
                dve.wait_ge(*xb.read(("rows", i)))
                dve.wait_ge(num_done, i + 1)
                bank = xb.bank(("num", i))
                link(stt(hden, bank[:, T:2 * T], -1.0, emb, ALU.mult, ALU.max))
                link(tt_(hden, bank[:, T:2 * T], hden, ALU.max))
                link(dve.reciprocal(hden, hden))
                tt_(hden, bank[:, 0:T], hden, ALU.mult).then_inc(x_freed["dve"], 1)
                dve.wait_ge(*xb.read(("num", i)))
                tt_(hm[:, i], hden, so[:, i], ALU.mult).then_inc(hm_ready, 1)
                dve.wait_ge(hm_ready, i + 1)
            for i in range(2):
                dve.wait_ge(mix_done, i + 1)
                bank = xb.bank(("mix", i))
                for c in range(2):
                    t_ = 2 * i + c
                    ins = stt(gm[:, t_].rearrange("p (n t) -> p n t", n=TT),
                              bank[:, c * T:c * T + T].rearrange("p (n t) -> p n t", n=TT), col("g_v", t_),
                              bsp[:, t_].unsqueeze(1).to_broadcast([P, TT, P]), ALU.mult, ALU.add)
                ins.then_inc(x_freed["dve"], 1)
            dve.wait_ge(*xb.read(("mix", 1)))
            tt_(gm, gm, ug, ALU.mult).then_inc(gm_ready, 1)
            dve.wait_ge(hsum, 1)
            bank = xb.bank(("hsum", 0))
            ts(ms[:, 0:8], bank[:, 0:8], 1.0 / P, ALU.mult, EPS, ALU.add)
            ts(ms[:, 8:24], bank[:, 8:24], 1.0 / 64, ALU.mult, EPS, ALU.add).then_inc(x_freed["dve"], 1)
            dve.wait_ge(*xb.read(("hsum", 0)))
            rsqrt(24).then_inc(hscale, 1)
            for i in range(4):
                dve.wait_ge(hspread, i + 1)
                bank = xb.bank(("hspread", i))
                for c in range(2):
                    t_ = 2 * i + c
                    src, g_ = (hm[:, t_], col("g_mlstm", t_)) if t_ < 4 else (gm[:, t_ - 4], col("g_gmlp", t_ - 4))
                    ins = stt(ycat[:, t_], src, g_, bank[:, c * T:c * T + T], ALU.mult, ALU.mult)
                ins.then_inc(x_freed["dve"], 1)
            for i in range(4):
                dve.wait_ge(used, UNIT_AT[("out2", 2 * i + 1)] + 1)
                if i == 0:
                    dve.wait_ge(x_ready, done_x[0])
                tt_(two(x, i), two(x, i), pb.bank(("out2", i))[:], ALU.add).then_inc(x_ready, 1)
            norm_scale(8)
            normed(8, x, h, h_ready)

            dve.wait_ge(s_par3, 32)
            link(ts(first, slots[:, 0:EG], -1.0, ALU.mult, float(EG), ALU.add))
            link(dve.memset(rank, -1.0))
            link(dve.memset(wall, 0.0))
            dve.memset(zero, 0.0).then_inc(y_zeroed, 1)
            dve.memset(scwT, 0.0).then_inc(scwT_ready, 1)
            for c in range(2):
                dve.memset(yg[:, c * 512:c * 512 + 512], 0.0).then_inc(yg_ready, 1)
            dve.memset(hx, 0.0).then_inc(hx_ready, 1)
            dve.wait_ge(lg_done, 1)
            bank = xb.bank(("lg", 0))
            for tt in range(TT):
                ins = tt_(lg[:, tt], bank[:, 64 * tt:64 * tt + 36], b_r, ALU.add)
            ins.then_inc(x_freed["dve"], 1)
            dve.wait_ge(*xb.read(("lg", 0)))

            def pick(values, w, where, best, tmp):
                link(dve.tensor_reduce(best, values, AX.X, ALU.max))
                link(ts(where, values, best, ALU.is_equal))
                link(tt_(where, where, first[:, 0:w], ALU.mult))
                link(dve.tensor_reduce(tmp, where, AX.X, ALU.max))
                link(ts(where, where, tmp, ALU.is_equal))

            for tt in range(TT):
                r_ = rsm[:, tt]
                pick(lg[:, tt, 0:NG], NG, gsel[:, tt], r_[:, 5:6], r_[:, 6:7])
                ts(r_[:, 0:1], r_[:, 5:6], -1.0, ALU.mult).then_inc(rt_max, 1)
            dve.wait_ge(rt_max, TT)
            for tt in range(TT):
                r_ = rsm[:, tt]
                le = lsel[:, 0, tt]
                link(ts(le, lg[:, tt, NG:NG + EG], gsel[:, tt, 0:1], ALU.mult))
                for g in range(1, NG):
                    link(stt(le, lg[:, tt, NG + EG * g:NG + EG * g + EG], gsel[:, tt, g:g + 1], le,
                             ALU.mult, ALU.add))
                pick(le, EG, sel1[:, tt], r_[:, 7:8], r_[:, 6:7])
                rest = lsel[:, 1, tt]
                link(stt(rest, sel1[:, tt], -3.0e38, le, ALU.mult, ALU.add))
                pick(rest, EG, sel2[:, tt], r_[:, 12:13], r_[:, 6:7])
                tt_(r_[:, 3:4], r_[:, 12:13], r_[:, 7:8], ALU.subtract).then_inc(rt_max, 1)
            for tt in range(TT):
                r_ = rsm[:, tt]
                dve.wait_ge(rt_exp, TT + tt + 1)
                link(ts(r_[:, 13:14], r_[:, 4:5], 1.0, ALU.add))
                link(tt_(r_[:, 13:14], r_[:, 13:14], r_[:, 1:2], ALU.mult))
                link(dve.reciprocal(r_[:, 14:15], r_[:, 13:14]))
                link(tt_(r_[:, 15:16], r_[:, 14:15], r_[:, 4:5], ALU.mult))
                both, wts = lsel[:, 2, tt], lsel[:, 3, tt]
                link(tt_(both, sel1[:, tt], sel2[:, tt], ALU.add))
                link(ts(wts, sel1[:, tt], r_[:, 14:15], ALU.mult))
                link(stt(wts, sel2[:, tt], r_[:, 15:16], wts, ALU.mult, ALU.add))
                for g in range(NG):
                    ts(selw[:, tt, EG * g:EG * g + EG], wts, gsel[:, tt, g:g + 1], ALU.mult)
                    ins = ts(selm[:, tt, EG * g:EG * g + EG], both, gsel[:, tt, g:g + 1], ALU.mult)
                ins.then_inc(sel_ready, 1)
            dve.wait_ge(rank_done, 1)
            bank = xb.bank(("rank", 0))
            for tt in range(TT):
                link(tt_(lmask[:, tt], bank[:, NE * tt:NE * tt + NE], selm[:, tt], ALU.mult))
                link(stt(lmask[:, tt], selm[:, tt], -1.0, lmask[:, tt], ALU.add, ALU.add))
                for r in range(MAXR):
                    ts(rank[:, tt, NE * r:NE * r + NE], lmask[:, tt], float(-CAP * r), ALU.add)
                    ins = dve.tensor_copy(wall[:, tt, NE * r:NE * r + NE], selw[:, tt])
                link(ins)
            dve.tensor_reduce(cnt[:, 0:1], bank[:, 2 * NE:3 * NE], AX.X, ALU.max).then_inc(x_freed["dve"], 1)
            dve.wait_ge(*xb.read(("rank", 0)))
            link(ts(cnt[:, 1:2], cnt[:, 0:1], CAP + 0.5, ALU.is_gt, 1.0, ALU.add))
            for r in range(2, MAXR):
                link(ts(cnt[:, 2:3], cnt[:, 0:1], CAP * r + 0.5, ALU.is_gt))
                link(tt_(cnt[:, 1:2], cnt[:, 1:2], cnt[:, 2:3], ALU.add))
            dve.tensor_copy(rounds[0:1, 0:1], cnt[0:1, 1:2]).then_inc(rounds_ready, 1)

            dve.wait_ge(rounds_ready, 1)
            n_pairs = dve.value_load(rounds[0:1, 0:1], min_val=1, max_val=MAXR) * PAIRS

            def gather_matrix(buf, at):
                for tt in range(TT):
                    ins = ts(gat[:, buf, tt], slots[:], rank[:, tt, at], ALU.is_equal)
                ins.then_inc(g_ready, 1)

            gather_matrix(0, slice(0, 1))
            with dve.Fori(0, n_pairs) as it:
                dve.wait_ge(gath_done, 2 * it + 1)
                gather_matrix(1, bass.ds(2 * it + 1, 1))
                dve.wait_ge(scwT_ready, it + 1)
                for e in range(2):
                    for tt in range(TT):
                        ins = ts(scw[:, tt, CAP * e:CAP * e + CAP], slots[:], rank[:, tt, bass.ds(2 * it + e, 1)],
                                 ALU.is_equal, wall[:, tt, bass.ds(2 * it + e, 1)], ALU.mult)
                ins.then_inc(scw_ready, 1)
                for e in range(2):
                    dve.wait_ge(hid_th, 2 * it + (e + 1))
                    gu = psum[5]
                    stt(ht[:, 1], ht[:, 0], 1.0, gu[:, 0:4 * CAP].rearrange("p (f c) -> p f c", f=4),
                        ALU.add, ALU.mult).then_inc(silu_done, 1)
                    dve.wait_ge(silu_done, 2 * it + (e + 1))
                    stt(hx[:, e], ht[:, 1], 0.5, gu[:, 4 * CAP:8 * CAP].rearrange("p (f c) -> p f c", f=4),
                        ALU.mult, ALU.mult).then_inc(hx_ready, 1)
                    dve.wait_ge(hx_ready, 2 * it + (e + 2))
                    if e == 0:
                        dve.wait_ge(scwT_done, it + 1)
                        dve.wait_ge(scat_done, it + 1)
                        dve.tensor_copy(scwT, psum[4][:, 0:T]).then_inc(scwT_ready, 1)
                        dve.wait_ge(gath_done, 2 * it + 2)
                        gather_matrix(0, bass.ds(2 * it + 2, 1))
            dve.wait_ge(moe_done, 1)
            for i in range(4):
                tt_(two(x, i), two(x, i), psum[i][:], ALU.add).then_inc(x_ready, 1)
            norm_scale(9)
            dve.wait_ge(x_ready, 20)
            normed(9, x, res, res_ready)

        @block.tensor
        def _(pe):
            def unit(key):
                k = UNIT_AT[key]
                pe.wait_ge(landed[k % RING], 16 * (k // RING + 1))
                return ring[:, k % RING]

            def mm(o, a, b, start, stop):
                return pe.matmul(o, a, b, start=start, stop=stop, skip_group_check=True)

            def norm_sums(norm):
                for k in range(KT):
                    if k % 2 == 0:
                        pe.wait_ge(squares, 4 * norm + k // 2 + 1)
                    for tt in range(TT):
                        ins = mm(STAT[:, tt:tt + 1], sq[:, k, tt * P:tt * P + P], ones[:, 0:1],
                                 k == 0 and tt == 0, k == KT - 1)
                ins.then_inc(sums, 1)
                pe.wait_ge(scales, norm + 1)
                for tt in range(TT):
                    ins = mm(STAT[:, T + tt * P:T + tt * P + P], rstd[:, tt:tt + 1].to_broadcast([P, P]), ident[:],
                             True, True)
                ins.then_inc(spread, 1)

            def cols_pair(bank, key, i, src, ready, base):
                for c in range(2):
                    w = unit((key, 2 * i + c))
                    for k in range(KT):
                        if ready is not None and i == 0 and c == 0:
                            pe.wait_ge(ready, base + k + 1)
                        ins = mm(bank[:, c * T:c * T + T], w[:, k * P:k * P + P], src[:, k], k == 0, k == KT - 1)
                    ins.then_inc(used, 1)

            def rows_part(banks, key, first_unit, n_units, src, total, k0):
                for u in range(n_units):
                    w = unit((key, first_unit + u))
                    for kk in range(2):
                        k = k0 + 2 * u + kk
                        for tt in range(TT):
                            ins = mm(banks[tt][:], src[:, k, tt * P:tt * P + P], w[:, kk * 512:kk * 512 + 512],
                                     k == 0, k == total - 1)
                    ins.then_inc(used, 1)

            def pairs(key, n, src, ready=None, base=0):
                for i in range(n):
                    pb.claim(pe, (key, i))
                    cols_pair(pb.bank((key, i)), key, i, src, ready, base)

            pe.wait_ge(consts, 1)
            norm_sums(0)
            pairs("u", 2, h, h_ready, 0)
            norm_sums(1)
            pairs("q", 2, h)
            pairs("k", 2, h)
            for i in range(TT):
                pb.claim(pe, ("v", i))
            rows_part([pb.bank(("v", i)) for i in range(TT)], "v", 0, 4, h, KT, 0)

            def filler(slot):
                if slot < 4:
                    pb.claim(pe, ("xk", slot))
                    cols_pair(pb.bank(("xk", slot)), "xk", slot, mem, h_ready, 8)
                elif slot < 8:
                    half, part = (slot - 4) // 2, slot % 2
                    if part == 0:
                        for tt in range(TT):
                            pb.claim(pe, ("xv", 2 * half + tt))
                    rows_part([pb.bank(("xv", 2 * half + tt)) for tt in range(TT)], "xv", 4 * half + 2 * part, 2,
                              mem, KT, 4 * part)
                else:
                    pb.claim(pe, ("gate", slot - 8))
                    cols_pair(pb.bank(("gate", slot - 8)), "gate", slot - 8, h, None, 0)

            def inputs_of(j):
                i, q = j // 4, j % 4
                if j == 0:
                    pe.wait_ge(s_par, 16 * 19)
                    pe.wait_ge(*pb.read(("u", 1)))
                xb.claim(pe, ("bu", j))
                for c in range(2):
                    ins = mm(xb.bank(("bu", j))[:, c * T:c * T + T], bbd[32 * q:32 * q + 32, c, i],
                             uT[32 * q:32 * q + 32, i], True, True)
                ins.then_inc(bu_done, 1)

            def outputs_of(j):
                i, q = j // 4, j % 4
                pe.wait_ge(st_ready, j + 1)
                if q == 0 and i:
                    pe.wait_ge(y_freed, i)
                for c in range(2):
                    ins = mm(STAT[32 * q:32 * q + 32, 0:T], cbd[:, c, j], st[:, j % 2, c], c == 0, c == 1)
                ins.then_inc(y_done, 1)

            for r in range(HEADS + 1):
                lo = HD * (r % 2)
                if r < HEADS:
                    inputs_of(2 * r)
                    if r == 0:
                        pe.wait_ge(*pb.read(("v", 1)))
                    xb.claim(pe, ("z", r))
                    z = xb.bank(("z", r))
                    qh, kh = qT[lo:lo + HD, r // 2], kT[lo:lo + HD, r // 2]
                    mm(z[:, 0:T], kh[:, 0:P], qh, True, True)
                    mm(z[:, T:384], kh[:, P:T], qh[:, P:T], True, True).then_inc(z_done, 1)
                if r:
                    outputs_of(2 * r - 2)
                    outputs_of(2 * r - 1)
                if r < HEADS:
                    filler(2 * r)
                if r:
                    xb.claim(pe, ("cum", r - 1))
                    pe.wait_ge(sp_ready, r)
                    z = xb.bank(("cum", r - 1))
                    mm(z[:, 0:T], tri[:], sp[:, 0:T], True, False)
                    mm(z[:, P:T], ones[:], sp[:, T:384], False, True)
                    mm(z[:, T:384], tri[:], sp[:, T:384], True, True).then_inc(cum_done, 1)
                if r < HEADS:
                    inputs_of(2 * r + 1)
                    filler(2 * r + 1)
                if r:
                    hd = r - 1
                    lo = HD * (hd % 2)
                    xb.claim(pe, ("pv", hd))
                    pe.wait_ge(w_ready, r)
                    o = xb.bank(("pv", hd))[lo:lo + HD]
                    mm(o[:, 0:T], v1[:, 0, HD * hd:HD * hd + HD], w1[:, 0:T], True, False)
                    mm(o[:, P:T], v1[:, 1, HD * hd:HD * hd + HD], w1[:, T:384], False, True).then_inc(pv_done, 1)

            def half_depth(bank, key, i, src):
                w = unit((key, i))
                for c in range(2):
                    for k in range(4):
                        ins = mm(bank[:, c * T:c * T + T], w[:, (4 * c + k) * P:(4 * c + k + 1) * P], src[:, k],
                                 k == 0, k == 3)
                ins.then_inc(used, 1)

            pe.wait_ge(y_ready, 1)
            for i in range(2):
                pb.claim(pe, ("glu", i))
                half_depth(pb.bank(("glu", i)), "glu", i, yT)
            pe.wait_ge(*xb.read(("pv", HEADS - 1)))
            for i in range(4):
                pb.claim(pe, ("ba", i))
                half_depth(pb.bank(("ba", i)), "ba", i, oT)
                if i == 0:
                    pe.wait_ge(ossm_ready, 1)
                pb.claim(pe, ("bs", i))
                half_depth(pb.bank(("bs", i)), "bs", i, gt)
            pe.wait_ge(merged_ready, 4)
            pairs("out", 4, merged)
            norm_sums(2)

            norm_sums(3)
            pairs("xq", 4, h, h_ready, 16)
            pe.wait_ge(*pb.read(("xq", 3)))
            for i in range(8 + 1):
                if i < 8:
                    hh, tt = i // 2, i % 2
                    xb.claim(pe, ("sc", i))
                    for k in range(2):
                        ins = mm(xb.bank(("sc", i))[:, 0:T], xqT[:, 2 * hh + k, tt * P:tt * P + P], xkT[:, 2 * hh + k],
                                 k == 0, k == 1)
                    ins.then_inc(sc_done, 1)
                if i:
                    hh, tt = (i - 1) // 2, (i - 1) % 2
                    xb.claim(pe, ("pt", i - 1))
                    pe.wait_ge(prob_ready, i)
                    for m in range(2):
                        ins = pe.transpose(xb.bank(("pt", i - 1))[:, m * P:m * P + P],
                                           prob[:, (i - 1) % 2, m * P:m * P + P], ident[:])
                    ins.then_inc(pt_done, 1)
                    if tt:
                        pb.claim(pe, ("xav", hh))
                        pe.wait_ge(*xb.read(("pt", i - 1)))
                        for c in range(2):
                            for m in range(2):
                                ins = mm(pb.bank(("xav", hh))[:, c * T:c * T + T],
                                         xv[:, m, (2 * hh + c) * P:(2 * hh + c + 1) * P], probT[:, hh % 2, m],
                                         m == 0, m == 1)
                        ins.then_inc(xo_done, 1)
            pe.wait_ge(*pb.read(("xav", XH - 1)))
            pairs("xo", 4, xoT)
            norm_sums(4)

            norm_sums(5)
            for i in range(4):
                pb.claim(pe, ("dn", i))
            for j in range(FT + 2):
                if j < FT:
                    xb.claim(pe, ("up", j))
                    for c, key in enumerate(("fg", "fv")):
                        w = unit((key, j))
                        for k in range(KT):
                            if j == 0 and c == 0:
                                pe.wait_ge(h_ready, 24 + k + 1)
                            ins = mm(xb.bank(("up", j))[:, c * T:c * T + T], w[:, k * P:k * P + P], h[:, k], k == 0,
                                     k == KT - 1)
                        ins.then_inc(used, 1)
                if j >= 2:
                    w = unit(("dn", j - 2))
                    pe.wait_ge(hid_ready, j - 1)
                    for c in range(KT):
                        ins = mm(pb.bank(("dn", c // 2))[:, (c % 2) * T:(c % 2) * T + T], w[:, c * P:c * P + P],
                                 hid[:, (j - 2) % 3], j == 2 and c % 2 == 0, j == FT + 1)
                    ins.then_inc(used, 1)
            norm_sums(6)

            norm_sums(7)
            pe.wait_ge(s_par2, 16 * 5)
            xb.claim(pe, ("if", 0))
            for c in range(2):
                for k in range(KT):
                    if c == 0:
                        pe.wait_ge(h_ready, 32 + k + 1)
                    ins = mm(xb.bank(("if", 0))[0:MH, c * T:c * T + T], w_if[:, k, MH * c:MH * c + MH], h[:, k],
                             k == 0, k == KT - 1)
            ins.then_inc(if_done, 1)
            for i in range(TT):
                pb.claim(pe, ("v2", i))
            rows_part([pb.bank(("v2", i)) for i in range(TT)], "v2", 0, 4, h, KT, 0)
            xb.claim(pe, ("gT", 0))
            pe.wait_ge(if_rows, 1)
            for tt in range(TT):
                ins = pe.transpose(xb.bank(("gT", 0))[:, MH * tt:MH * tt + MH], ifr[:, 5, tt * P:tt * P + P],
                                   ident[0:MH, 0:MH])
            ins.then_inc(gt_done, 1)
            pe.wait_ge(qpad, 1)
            pairs("qk2", 4, h)
            for i in range(TT):
                pb.claim(pe, ("vg", i))
            rows_part([pb.bank(("vg", i)) for i in range(TT)], "vg", 0, 4, h, KT, 0)
            pairs("ug", 2, h)
            pairs("o2", 2, h)
            pe.wait_ge(em_ready, 1)
            pe.wait_ge(qk_ready, 4)
            for i in range(MH + 1):
                if i < MH:
                    xb.claim(pe, ("rows", i))
                    for c, row in enumerate((6, 7)):
                        ins = mm(xb.bank(("rows", i))[:, c * T:c * T + T], head_sel[:, i], ifr[:, row], True, True)
                    ins.then_inc(rows_done, 1)
                if i:
                    xb.claim(pe, ("num", i - 1))
                    pe.wait_ge(*xb.read(("s2", i - 1)))
                    o = xb.bank(("num", i - 1))
                    for c in range(2):
                        w0 = v2[:, 0, (i - 1) * P:i * P] if c == 0 else ones[:]
                        w1_ = v2[:, 1, (i - 1) * P:i * P] if c == 0 else ones[:]
                        mm(o[:, c * T:c * T + T], w0, st2[:, 0:T], True, False)
                        ins = mm(o[:, c * T + P:c * T + T], w1_, st2[:, T:384], False, True)
                    ins.then_inc(num_done, 1)
                if i < MH:
                    xb.claim(pe, ("s2", i))
                    z = xb.bank(("s2", i))
                    qh, kh = qk2[:, i], qk2[:, MH + i]
                    mm(z[:, 0:T], kh[:, 0:P], qh, True, True)
                    mm(z[:, T:384], kh[:, P:T], qh[:, P:T], True, True).then_inc(s2_done, 1)
            pe.wait_ge(vb_ready, 4)
            for i in range(2):
                xb.claim(pe, ("mix", i))
                for c in range(2):
                    for half in range(2):
                        g = 4 * i + 2 * c + half
                        for nb in range(TT):
                            ins = mm(xb.bank(("mix", i))[64 * half:64 * half + 64, c * T + nb * P:c * T + nb * P + P],
                                     gv[:, nb, 64 * g:64 * g + 64], mixw[:, g], True, True)
                ins.then_inc(mix_done, 1)
            xb.claim(pe, ("hsum", 0))
            pe.wait_ge(hsq, 2)
            o = xb.bank(("hsum", 0))
            for i in range(4):
                for tt in range(TT):
                    mm(o[:, 2 * i + tt:2 * i + tt + 1], sq[:, i, tt * P:tt * P + P], ones[:, 0:1], True, True)
            for i in range(4):
                for tt in range(TT):
                    a = 8 + 4 * i + 2 * tt
                    ins = mm(o[:, a:a + 2], sq[:, 4 + i, tt * P:tt * P + P], half_ones[:], True, True)
            ins.then_inc(hsum, 1)
            pe.wait_ge(hscale, 1)
            for i in range(4):
                xb.claim(pe, ("hspread", i))
                for c in range(2):
                    t_ = 2 * i + c
                    for tt in range(TT):
                        o = xb.bank(("hspread", i))[:, c * T + tt * P:c * T + tt * P + P]
                        if t_ < 4:
                            w = rstd[:, 2 * t_ + tt:2 * t_ + tt + 1].to_broadcast([P, P])
                            ins = mm(o, w, ident[:], True, True)
                        for half in range(2 if t_ >= 4 else 0):
                            a = 8 + 4 * (t_ - 4) + 2 * tt + half
                            ins = mm(o[64 * half:64 * half + 64], rstd[:, a:a + 1].to_broadcast([P, 64]), ident[:],
                                     True, True)
                ins.then_inc(hspread, 1)
            pe.wait_ge(*xb.read(("hspread", 3)))
            pairs("out2", 4, ycat)

            norm_sums(8)
            pe.wait_ge(h_ready, 48)
            for i in range(4):
                xb.claim(pe, ("tr", i))
                for k in range(4):
                    ins = pe.transpose(xb.bank(("tr", i))[:, k * P:k * P + P],
                                       h[:, 4 * (i % 2) + k, (i // 2) * P:(i // 2) * P + P], ident[:])
                ins.then_inc(tr_done, 1)
            xb.claim(pe, ("lg", 0))
            pe.wait_ge(s_par3, 32)
            for tt in range(TT):
                for k in range(KT):
                    ins = mm(xb.bank(("lg", 0))[:, 64 * tt:64 * tt + 36], h[:, k, tt * P:tt * P + P], w_r[:, k],
                             k == 0, k == KT - 1)
            ins.then_inc(lg_done, 1)
            pe.wait_ge(y_zeroed, 1)
            pe.wait_ge(x_ready, 16)
            for i in range(4):
                mm(psum[i][:], ident[:], zero, True, True)
            xb.claim(pe, ("rank", 0))
            pe.wait_ge(sel_ready, TT)
            o = xb.bank(("rank", 0))
            mm(o[:, 0:NE], before[:], selm[:, 0], True, True)
            mm(o[:, NE:2 * NE], before[:], selm[:, 1], True, False)
            mm(o[:, NE:2 * NE], ones[:], selm[:, 0], False, True)
            mm(o[:, 2 * NE:3 * NE], ones[:], selm[:, 0], True, False)
            mm(o[:, 2 * NE:3 * NE], ones[:], selm[:, 1], False, True).then_inc(rank_done, 1)
            pe.wait_ge(*xb.read(("tr", 3)))
            pe.wait_ge(*xb.read(("rank", 0)))
            pe.wait_ge(rounds_ready, 1)
            n_pairs = pe.value_load(rounds[0:1, 0:1], min_val=1, max_val=MAXR) * PAIRS

            def gather(buf):
                for k in range(KT):
                    for tt in range(TT):
                        ins = mm(psum[4][:, k * CAP:k * CAP + CAP], xtok[:, tt, k * P:k * P + P], gat[:, buf, tt],
                                 tt == 0, tt == 1)
                ins.then_inc(gath_done, 1)

            def scatter():
                for k in range(KT):
                    ins = mm(psum[k // 2][:, (k % 2) * T:(k % 2) * T + T], yg[:, k * P:k * P + P], scwT, False, True)
                return ins

            pe.wait_ge(g_ready, 1)
            gather(0)
            with pe.Fori(0, n_pairs) as it:
                for e in range(2):
                    if e:
                        pe.wait_ge(scw_ready, it + 1)
                        pe.wait_ge(xg_ready, 2 * it + 2)
                        for tt in range(TT):
                            ins = pe.transpose(psum[4][:, tt * P:tt * P + P], scw[:, tt], ident[:])
                        ins.then_inc(scwT_done, 1)
                    pe.wait_ge(xg_ready, 2 * it + (e + 1))
                    pe.wait_ge(hx_ready, 2 * it + (e + 1))
                    for u in range(8):
                        slot = u
                        pe.wait_ge(landed[slot], it * 32 + 16 * (DENSE // RING + e + 1))
                        for k in range(KT):
                            ins = mm(psum[5][:, u * CAP:u * CAP + CAP], ring[:, slot, k * P:k * P + P],
                                     xg[:, e, k], k == 0, k == KT - 1)
                        ins.then_inc(used, 1)
                    if e:
                        pe.wait_ge(scwT_ready, it + 2)
                    pe.wait_ge(g_ready, 2 * it + (2 + e))
                    gather(1 - e)
                    if e == 0:
                        pe.wait_ge(yg_ready, 2 * it + 2)
                        pe.wait_ge(scwT_ready, it + 1)
                        scatter().then_inc(scat_done, 1)
                    pe.wait_ge(hx_ready, 2 * it + (e + 2))
                    for u in range(4):
                        slot = 8 + u
                        pe.wait_ge(landed[slot], it * 32 + 16 * (DENSE // RING + e + 1))
                        for c in range(2):
                            ins = mm(psum[6 + c][CAP * e:CAP * e + CAP, :], hx[:, e, u],
                                     ring[:, slot, c * 512:c * 512 + 512], u == 0, u == 3)
                        ins.then_inc(used, 1)
            pe.wait_ge(yg_ready, 2 * n_pairs + 2)
            scatter().then_inc(moe_done, 1)
            norm_sums(9)


def tiles_of(w):
    k, n = w.shape
    return w.reshape(k // P, P, n // P, P).transpose(2, 1, 0, 3).reshape(n // P, P, k)


def half_tiles_of(w):
    t = tiles_of(w)
    return t.reshape(-1, 2, P, 512).transpose(0, 2, 1, 3).reshape(-1, P, UNIT)


def row_tiles_of(w):
    k, n = w.shape
    return w.reshape(k // 256, 2, P, n // 512, 512).transpose(3, 0, 2, 1, 4).reshape(-1, P, UNIT)


def lay_out(a):
    win, win2 = a["w_in"][0], a["w_in_2"][0]
    parts = {
        "q": tiles_of(win[:, 0:512]), "k": tiles_of(win[:, 512:1024]), "v": row_tiles_of(win[:, 1024:1536]),
        "u": tiles_of(win[:, 1536:2048]), "gate": tiles_of(win[:, 2048:4096]),
        "xk": tiles_of(a["xa_wk"][0]), "xv": row_tiles_of(a["xa_wv"][0]), "xq": tiles_of(a["xa_wq"][0]),
        "xo": tiles_of(a["xa_wo"][0]), "glu": half_tiles_of(a["ssm_w_glu"][0]),
        "ba": half_tiles_of(a["w_branch_attn"][0]), "bs": half_tiles_of(a["w_branch_ssm"][0]),
        "out": tiles_of(a["w_out"][0]), "fg": tiles_of(a["ffn_w_up"][0][:, :FT * P]),
        "fv": tiles_of(a["ffn_w_up"][0][:, FT * P:]), "dn": a["ffn_w_down"][0].reshape(FT, P, D),
        "qk2": tiles_of(win2[:, 0:1024]), "v2": row_tiles_of(win2[:, 1024:1536]), "o2": tiles_of(win2[:, 1536:2048]),
        "ug": tiles_of(win2[:, 2056:2568]), "vg": row_tiles_of(win2[:, 2568:3080]), "out2": tiles_of(a["w_out_2"][0]),
    }
    stream = np.empty((DENSE + NE * PER_EXPERT, P, UNIT), np.float32)
    for n, (key, i) in enumerate(UNITS):
        stream[n] = parts[key][i]
    for e in range(NE):
        n = DENSE + e * PER_EXPERT
        stream[n:n + 4] = tiles_of(a["w_gate_2"][0, e])
        stream[n + 4:n + 8] = tiles_of(a["w_up_2"][0, e])
        stream[n + 8:n + 12] = a["w_down_2"][0, e].reshape(4, P, D)

    def column(v):
        return v.reshape(-1, P).T

    vectors = {
        "mix_pre": a["norm_mix_pre"], "mix_post": a["norm_mix_post"], "xa_pre": a["norm_xa_pre"],
        "xa_post": a["norm_xa_post"], "mem": a["norm_mem"], "ffn_pre": a["norm_ffn_pre"],
        "ffn_post": a["norm_ffn_post"], "norm1": a["norm1_g_2"], "norm2": a["norm2_g_2"], "final": a["final_g_2"],
        "b_gate": a["b_gate"], "d": a["ssm_d"], "b_glu": a["ssm_b_glu"], "conv0": a["ffn_conv_w"][0, 0],
        "conv1": a["ffn_conv_w"][0, 1], "conv2": a["ffn_conv_w"][0, 2], "conv_b": a["ffn_conv_b"],
        "qk0": a["conv_qk_2"][0, 0], "qk1": a["conv_qk_2"][0, 1], "qk2": a["conv_qk_2"][0, 2],
        "qk3": a["conv_qk_2"][0, 3], "g_mlstm": a["g_mlstm_out_2"], "g_v": a["g_gmlp_v_2"],
        "g_gmlp": a["g_gmlp_out_2"],
    }

    def states(v):
        return v.reshape(STILES, P).T

    log_dt = np.broadcast_to(a["ssm_log_dt"][0][:, None], (2 * STILES, 64))
    b = np.stack([a["ssm_b_re"][0], a["ssm_b_im"][0]])
    c = np.stack([a["ssm_c_re"][0], a["ssm_c_im"][0]])
    return {
        "stream": stream,
        "xT": a["x"][0].T.reshape(KT, P, T).transpose(1, 0, 2),
        "memT": a["mem"][0].T.reshape(KT, P, T).transpose(1, 0, 2),
        "cols": np.concatenate([column(vectors[name]) for name in COLS], axis=1),
        "ssm_a": np.stack([states(a["ssm_a_re"][0]), states(a["ssm_a_im"][0]), states(log_dt)], axis=1),
        "ssm_b": b.reshape(2, 4, 8, 64, 16).transpose(2, 4, 0, 1, 3).reshape(P, 2, 4, 64),
        "ssm_c": c.reshape(2, STILES, 2, 16, 64).transpose(2, 4, 0, 1, 3).reshape(P, 2, STILES, 16),
        "mixw": a["w_spatial_2"][0].transpose(2, 0, 1),
        "bsp": a["b_spatial_2"][0],
        "w_if": win2[:, 2048:2056].reshape(KT, P, 8).transpose(1, 0, 2),
        "b_if": np.stack([a["b_igate_2"][0], a["b_fgate_2"][0]], axis=1),
        "w_r": np.concatenate([a["w_router_group_2"][0], a["w_router_expert_2"][0]], axis=1
                              ).reshape(KT, P, 36).transpose(1, 0, 2),
        "b_r": np.concatenate([a["b_router_group_2"][0], a["b_router_expert_2"][0]]),
    }


def kernel(**inputs):
    import concourse.bacc as bacc
    from concourse.bass_utils import run_bass_kernel_spmd

    laid = {k: np.ascontiguousarray(v) for k, v in lay_out({k: np.asarray(v) for k, v in inputs.items()}).items()}
    nc = bacc.Bacc("TRN2", target_bir_lowering=False, num_devices=1)
    dram = {k: nc.dram_tensor(f"in_{k}", v.shape, mybir.dt.from_np(v.dtype), kind="ExternalInput").ap()
            for k, v in laid.items()}
    out = nc.dram_tensor("out_y", (P, KT, T), F32, kind="ExternalOutput").ap()
    program(nc, dram, out)
    got = run_bass_kernel_spmd(nc, [{f"in_{k}": v for k, v in laid.items()}], core_ids=[0]).results[0]["out_y"]
    return got.reshape(P, KT, T).transpose(2, 1, 0).reshape(1, T, D)
```

```python
from contextlib import ExitStack

import numpy as np

import concourse.bass as bass
from concourse import mybir

ALU = mybir.AluOpType
ACT = mybir.ActivationFunctionType
F32 = mybir.dt.float32
I32 = mybir.dt.int32
F32R = mybir.dt.float32r
AX = mybir.AxisListType

P = 128
D = 1024
T = 256
KT = D // P
TT = T // P
RING = 12
UNIT = 8 * P
EPS = 1e-6
HEADS = 8
HD = 64
STILES = 16
XH = 4
FT = 22
MH = 4
GG = 8
NE = 32
EG = 8
NG = 4
CAP = 64
MAXR = T // CAP
PAIRS = NE // 2
FE = 512
TWO_PI_HI = 6.28125
TWO_PI_LO = 2 * np.pi - 6.28125
ROUND = 12582912.0
GELU_C = 0.044715
GELU_K = float(np.sqrt(2 / np.pi))
RSQRT_SEED = float(0x5F3759DF + 0x40000000 - 0x00400000)

UNITS = []
UNITS += [("u", i) for i in range(4)] + [("q", i) for i in range(4)] + [("k", i) for i in range(4)]
UNITS += [("v", i) for i in range(4)] + [("xk", i) for i in range(8)] + [("xv", i) for i in range(8)]
UNITS += [("gate", i) for i in range(16)] + [("glu", i) for i in range(2)]
for i in range(4):
    UNITS += [("ba", i), ("bs", i)]
UNITS += [("out", i) for i in range(8)] + [("xq", i) for i in range(8)] + [("xo", i) for i in range(8)]
for i in range(FT + 2):
    if i < FT:
        UNITS += [("fg", i), ("fv", i)]
    if i >= 2:
        UNITS += [("dn", i - 2)]
UNITS += [("v2", i) for i in range(4)] + [("qk2", i) for i in range(8)] + [("vg", i) for i in range(4)]
UNITS += [("ug", i) for i in range(4)] + [("o2", i) for i in range(4)] + [("out2", i) for i in range(8)]
UNIT_AT = {key: n for n, key in enumerate(UNITS)}
DENSE = len(UNITS)
SPLIT = UNIT_AT[("xq", 0)]
SPLIT_RING = 3
PER_EXPERT = 12
PAIR = 2 * PER_EXPERT
assert DENSE % RING == 0 and PAIR % RING == 0

COLS = {}
for name, width in (("mix_pre", 8), ("mix_post", 8), ("xa_pre", 8), ("xa_post", 8), ("mem", 8), ("ffn_pre", 8),
                    ("ffn_post", 8), ("norm1", 8), ("norm2", 8), ("final", 8), ("b_gate", 16), ("d", 4),
                    ("b_glu", 4), ("conv0", 44), ("conv1", 44), ("conv2", 44), ("conv_b", 44), ("qk0", 8),
                    ("qk1", 8), ("qk2", 8), ("qk3", 8), ("g_mlstm", 4), ("g_v", 4), ("g_gmlp", 4)):
    COLS[name] = sum(w for _, w in COLS.values()), width
NCOLS = sum(w for _, w in COLS.values())

NORMS = ["mix_pre", "mem", "mix_post", "xa_pre", "xa_post", "ffn_pre", "ffn_post", "norm1", "norm2", "final"]


class BankRing:

    def __init__(self, banks, plan, freed):
        self.banks, self.plan, self.freed = banks, plan, freed
        self.at = {key: n for n, (key, _) in enumerate(plan)}

    def bank(self, key):
        return self.banks[self.at[key] % len(self.banks)]

    def claim(self, pe, key):
        before = self.at[key] - len(self.banks)
        if before >= 0:
            pe.wait_ge(*self.read(self.plan[before][0]))

    def read(self, key):
        reader = self.plan[self.at[key]][1]
        semaphore, start, step = self.freed[reader]
        return semaphore, start + step * sum(r == reader for _, r in self.plan[:self.at[key] + 1])


def program(nc, dram, out):
    with ExitStack() as ctx:
        def sb(name, shape, dt=F32):
            return ctx.enter_context(nc.sbuf_tensor(name, shape, dt))

        def sem(name):
            return ctx.enter_context(nc.semaphore(name))

        ring = sb("ring", [P, RING, UNIT])
        x = sb("x", [P, KT, T])
        h = sb("h", [P, KT, T])
        sq = sb("sq", [P, KT, T])
        ident = sb("ident", [P, P])
        ones = sb("ones", [P, P])
        tri = sb("tri", [P, P])
        before = sb("before", [P, P])
        mask_lt = sb("mask_lt", [P, 3, P])
        mask_le = sb("mask_le", [P, 3, P])
        half_ones = sb("half_ones", [P, 2])
        head_sel = sb("head_sel", [MH, MH, P])
        slots = sb("slots", [P, CAP])
        cols = sb("cols", [P, NCOLS])
        hb = sb("hb", [P, 24])
        ms = sb("ms", [P, 24])
        ri = sb("ri", [P, 24], I32)
        rstd = sb("rstd", [P, 24])
        rt = sb("rt", [P, 24])
        rb = sb("rb", [P, T])
        arena_at = nc.sbuf_base + -nc.sbuf_base % 32
        arena = sb("arena", [P, 31136])
        bbd = sb("bbd", [P, 2, 4, P])

        def view(start, *shape, parts=P):
            n = int(np.prod(shape))
            v = arena[0:parts, start:start + n]
            if len(shape) == 1:
                return v
            names = "abcd"[:len(shape)]
            sizes = {names[i]: shape[i] for i in range(len(shape))}
            return v.rearrange(f"p ({' '.join(names)}) -> p {' '.join(names)}", **sizes)

        def rounded(name, start, shape):
            return nc.alloc_sbuf_tensor_at(name, shape, F32R, offset=arena_at + 4 * start)

        hh, hl = rounded("h_high", 8192, [P, KT, T]), rounded("h_low", 10240, [P, KT, T])
        yh, yl = rounded("y_high", 12288, [P, KT, T]), rounded("y_low", 14336, [P, KT, T])
        wh = rounded("w_high", 24576, [P, SPLIT_RING, UNIT])
        wl = rounded("w_low", 24576 + SPLIT_RING * UNIT, [P, SPLIT_RING, UNIT])

        rot = view(0, 2, STILES, T)
        uT, qT, kT = view(8192, 4, T), view(9216, 4, T), view(10240, 4, T)
        v1 = view(11264, TT, 512)
        gates = view(12288, 16, T)
        xkT, xv = view(16384, KT, T), view(18432, TT, D)
        oT = view(20480, 4, T)
        yT = view(21504, 4, T)
        m1, m2, vr, wr = view(22528, 2, T), view(23040, 2, T), view(23552, 2, T), view(24064, 2, T)
        st = view(24576, 2, 2, T)
        zm, az, sp, w1 = view(25600, 384), view(25984, 384), view(26368, 384), view(26752, 384)
        zm = (zm, view(30752, 384))
        gt = view(22528, 4, T)
        cbd = view(27136, 2, STILES, 32)
        craw = view(24576, 2, STILES, 16)
        ta, tb = view(16384, STILES * 128), view(18432, STILES * 128)
        mem = view(28160, KT, T)
        powers = view(30208, 2, 2, STILES)
        ptmp = view(30272, 6, STILES)
        ssm = view(30368, 24, STILES)
        merged = view(0, KT, T)
        mg = view(2048, 2, 512)
        xqT = view(3072, KT, T)
        prob = view(5120, 2, T)
        probT = view(5632, 2, TT, T)
        post = view(22528, KT, T)
        sm = view(8000, 4, 8)
        up = view(0, 3, 2, T + 4)
        acc = view(1560, 3, 2, T)
        fs = view(3096, 3, 2, T)
        hid32 = view(4632, 3, T)
        v2 = view(0, TT, 512)
        qk2 = view(1024, 8, T)
        qraw = view(3072, 2, 2, T + 4)
        qs = view(4112, 2, 2, T)
        gv = view(5136, TT, 512)
        gvs = view(6160, TT, 512)
        ugs = view(6160, 4, T)
        gm = view(4112, 4, T)
        decay = view(7184, 384)
        st2 = view(7568, 384)
        gT = view(7952, TT, MH)
        b_if = view(7960, 2, parts=MH)
        vsum = view(7964, 2)
        ug = view(16384, 4, T)
        so = view(17408, 4, T)
        hm = view(18432, 4, T)
        qt = view(18432, 2, 2, T)
        mixw = view(19456, GG, P)
        bsp = view(20480, 4, P)
        ifr = view(20992, 10, T, parts=MH)
        emb = view(23552, T)
        hden = view(23808, T)
        w_if = view(24064, KT, 8)
        xtok = view(0, TT, D)
        w_r = view(2048, KT, 36)
        b_r = view(2336, 36)
        lg = view(2400, TT, 36)
        rsm = view(2480, TT, 16)
        gsel = view(2512, TT, NG)
        lsel = view(2520, 4, TT, EG)
        lmask = view(2584, TT, NE)
        sel1, sel2 = view(2648, TT, EG), view(2664, TT, EG)
        first = view(2680, EG)
        selw = view(2688, TT, NE)
        selm = view(2752, TT, NE)
        rank = view(2816, TT, MAXR * NE + 4)
        wall = view(3080, TT, MAXR * NE + 4)
        gat = view(3344, TT, 2 * CAP)
        scw = view(3600, TT, 2 * CAP)
        scwT = view(3856, T)
        xg = view(4112, KT, 2 * CAP)
        gate_th = view(5136, FE)
        act_ = view(5648, FE)
        hx = view(6160, FE)
        hT = view(6672, FE // P, 2 * CAP)
        yg = view(7184, D)
        cnt = view(8208, 4)
        zero = view(8212, 512)
        res = view(8724, KT, T)
        rounds = sb("rounds", [1, 1], I32)

        psum = [ctx.enter_context(nc.psum_tensor(f"psum{i}", [P, 512], F32)) for i in range(8)]
        STAT = psum[7]

        landed = [sem(f"landed{i}") for i in range(RING)]
        used = sem("used")
        s_x, s_mem, s_cols, s_par = sem("x_in"), sem("mem_in"), sem("vectors_in"), sem("ssm_matrices_in")
        s_par2, s_par3 = sem("mixer2_params_in"), sem("router_params_in")
        s_out = sem("out_stored")
        consts = sem("consts_ready")
        hi_ready, lo_ready = sem("weights_high"), sem("weights_low")
        op32, op_high, op_low = sem("operand_ready"), sem("operand_high"), sem("operand_low")
        squares, sums, scales, spread = sem("squares_ready"), sem("sums_ready"), sem("scales_ready"), sem("spread_ready")
        scaled, rb_ready = sem("post_scaled"), sem("spread_copied")
        h_ready, x_ready = sem("h_ready"), sem("x_ready")
        act_chain, dve_chain, pool_chain = sem("act_chain"), sem("dve_chain"), sem("pool_chain")
        p_freed = {"act": sem("pbank_freed_act"), "dve": sem("pbank_freed_dve")}
        x_freed = {"act": sem("xbank_freed_act"), "dve": sem("xbank_freed_dve")}
        dve_halves = sem("bias_halves")
        ssm_args, ssm_trig, ssm_ready = sem("ssm_args"), sem("ssm_trig"), sem("ssm_ready")
        bu_done, st_ready, y_done, y_freed = sem("bu_done"), sem("states_ready"), sem("y_done"), sem("y_freed")
        z_done, sp_ln, sp_ready = sem("z_done"), sem("softplus_ln"), sem("softplus_ready")
        cum_done, w_exp, w_ready = sem("cum_done"), sem("w_exp"), sem("w_ready")
        pv_done = sem("pv_done")
        gelu_sq, gelu_in, gelu_th = sem("gelu_squares"), sem("gelu_inner"), sem("gelu_tanh")
        y_ready, glu_th, ossm_ready = sem("y_ready"), sem("glu_tanh"), sem("ossm_ready")
        gates_th, merged_ready = sem("gates_tanh"), sem("merged_ready")
        sc_done, max_ready, prob_exp, prob_ready = sem("scores_done"), sem("max_ready"), sem("prob_exp"), sem("prob_ready")
        pt_done, pt_ready, xo_done = sem("probT_done"), sem("probT_ready"), sem("xo_done")
        xo_high = sem("attended_high")
        up_ready, conv_g, hid_ready = sem("up_ready"), sem("conv_ready"), sem("hid_ready")
        if_done, if_ready, if_ln, if_rows, em_ready = (sem("if_done"), sem("if_ready"), sem("if_ln"),
                                                       sem("if_rows"), sem("em_ready"))
        gt_done, qpad = sem("gT_done"), sem("qk_padded")
        qk_raw, qk_conv, qk_th, qk_ready = sem("qk_raw"), sem("qk_conv"), sem("qk_tanh"), sem("qk_ready")
        rows_done, dec_in, dec_exp, s2_done, s2_ready = (sem("rows_done"), sem("decay_in"), sem("decay_exp"),
                                                         sem("scores2_done"), sem("scores2_ready"))
        em_copied, num_done, hm_ready, hsq = sem("em_copied"), sem("num_done"), sem("hm_ready"), sem("head_squares")
        vsq, vb_ready, mix_done, gm_ready = sem("v_squares"), sem("vb_ready"), sem("mix_done"), sem("gm_ready")
        so_th, hsum, hscale, hspread, ycat_ready = (sem("o_tanh"), sem("head_sums"), sem("head_scales"),
                                                    sem("head_spread"), sem("ycat_ready"))
        tr_done, tr_ready, lg_done = sem("tok_turned"), sem("tok_ready"), sem("logits_done")
        rt_max, rt_exp, sel_ready, rank_done, rank_ready = (sem("router_max"), sem("router_exp"), sem("sel_ready"),
                                                            sem("rank_done"), sem("rank_ready"))
        rounds_ready, y_zeroed = sem("rounds_ready"), sem("y_zeroed")
        g_ready, gath_done, xg_low, xg_high = sem("gather_ready"), sem("gather_done"), sem("xg_low"), sem("xg_high")
        hid_th, hx_ready, hT_done, hT_ready = sem("expert_tanh"), sem("hx_ready"), sem("hT_done"), sem("hT_ready")
        scw_ready, scwT_done, scwT_ready = sem("scatter_ready"), sem("scatterT_done"), sem("scatterT_ready")
        yg_low, yg_high = sem("yg_low"), sem("yg_high")
        silu_done = sem("silu_done")
        moe_done, res_ready = sem("moe_done"), sem("result_ready")

        pplan = [(("u", i), "act") for i in range(2)] + [(("q", i), "act") for i in range(2)]
        pplan += [(("k", i), "act") for i in range(2)] + [(("v", i), "act") for i in range(2)]
        pplan += [(("xk", i), "act") for i in range(4)] + [(("xv", i), "act") for i in range(4)]
        pplan += [(("gate", i), "act") for i in range(8)] + [(("glu", i), "act") for i in range(2)]
        for i in range(4):
            pplan += [(("ba", i), "dve"), (("bs", i), "dve")]
        pplan += [(("out", i), "act") for i in range(4)] + [(("xq", i), "act") for i in range(4)]
        pplan += [(("xav", i), "dve") for i in range(XH)]
        pplan += [(("xo", i), "act") for i in range(4)] + [(("dn", i), "act") for i in range(4)]
        pplan += [(("v2", i), "act") for i in range(2)] + [(("qk2", i), "act") for i in range(4)]
        pplan += [(("vg", i), "act") for i in range(2)] + [(("ug", i), "act") for i in range(2)]
        pplan += [(("o2", i), "act") for i in range(2)] + [(("out2", i), "dve") for i in range(4)]
        pb = BankRing(psum[0:4], pplan, {who: (s, 0, 1) for who, s in p_freed.items()})

        xplan = []
        for r in range(HEADS + 1):
            if r < HEADS:
                xplan += [(("bu", 2 * r), "dve"), (("z", r), "dve")]
            if r >= 1:
                xplan += [(("cum", r - 1), "dve")]
            if r < HEADS:
                xplan += [(("bu", 2 * r + 1), "dve")]
            if r >= 1:
                xplan += [(("pv", r - 1), "act")]
        for i in range(8 + 1):
            if i < 8:
                xplan += [(("sc", i), "act")]
            if i >= 1:
                xplan += [(("pt", i - 1), "act")]
        xplan += [(("up", i), "act") for i in range(FT)]
        xplan += [(("if", 0), "dve"), (("gT", 0), "act")]
        for i in range(MH + 1):
            if i < MH:
                xplan += [(("rows", i), "act")]
            if i >= 1:
                xplan += [(("num", i - 1), "dve")]
            if i < MH:
                xplan += [(("s2", i), "dve")]
        xplan += [(("mix", i), "dve") for i in range(2)] + [(("hsum", 0), "dve")]
        xplan += [(("hspread", i), "op32") for i in range(4)]
        xplan += [(("tr", i), "act") for i in range(4)]
        xplan += [(("lg", 0), "dve"), (("rank", 0), "dve")]
        xb = BankRing(psum[4:7], xplan, {"act": (x_freed["act"], 0, 1), "dve": (x_freed["dve"], 0, 1),
                                         "op32": (op32, 3 * KT, 2)})

        def col(name, i=0):
            start = COLS[name][0] + i
            return cols[:, start:start + 1]

        block = ctx.enter_context(nc.Block())

        @block.sync
        def _(sp):
            sp.dma_start(x[:], dram["xT"]).then_inc(s_x, 16)
            for n in range(RING):
                sp.dma_start(ring[:, n], dram["stream"][n]).then_inc(landed[n], 16)
            stream = dram["stream"]
            with sp.Fori(1, (DENSE + NE * PER_EXPERT) // RING) as i:
                for s in range(RING):
                    sp.wait_ge(used, RING * i + (s + 1 - RING))
                    sp.dma_start(ring[:, s], stream[bass.ds(RING * i + s, 1)].rearrange("a p n -> p (a n)")
                                 ).then_inc(landed[s], 16)
            sp.wait_ge(rounds_ready, 1)
            n_rounds = sp.value_load(rounds[0:1, 0:1], min_val=1, max_val=MAXR)
            with sp.If(n_rounds > 1):
                with sp.Fori(1, n_rounds) as r:
                    with sp.Fori(0, NE) as i:
                        for s in range(RING):
                            sp.wait_ge(used, r * (NE * PER_EXPERT) + RING * i + (DENSE + s + 1 - RING))
                            sp.dma_start(ring[:, s], stream[bass.ds(RING * i + (DENSE + s), 1)].rearrange(
                                "a p n -> p (a n)")).then_inc(landed[s], 16)
            sp.wait_ge(res_ready, KT)
            sp.dma_start(out, res).then_inc(s_out, 16)
            sp.wait_ge(s_out, 16)

        @block.gpsimd
        def _(pool):
            n = [0]

            def link(ins):
                n[0] += 1
                ins.then_inc(pool_chain, 1)
                pool.wait_ge(pool_chain, n[0])

            link(pool.memset(ones[:], 1.0))
            pool.affine_select(out=ident[:], in_=ones[:], compare_op=ALU.is_equal, fill=0.0, base=0,
                               pattern=[[-1, P]], channel_multiplier=1).then_inc(consts, 1)
            pool.dma_start(mem, dram["memT"]).then_inc(s_mem, 16)
            link(pool.memset(mask_lt[:], 1.0))
            link(pool.memset(mask_le[:], 1.0))
            link(pool.memset(head_sel[:], 1.0))
            link(pool.memset(half_ones[:], 1.0))
            link(pool.affine_select(out=tri[:], in_=ones[:], compare_op=ALU.is_ge, fill=0.0, base=0,
                                    pattern=[[-1, P]], channel_multiplier=1))
            link(pool.affine_select(out=before[:], in_=ones[:], compare_op=ALU.is_gt, fill=0.0, base=0,
                                    pattern=[[1, P]], channel_multiplier=-1))
            for b in (0, 2):
                link(pool.affine_select(out=mask_lt[:, b], in_=mask_lt[:, b], compare_op=ALU.is_gt, fill=0.0,
                                        base=0, pattern=[[1, P]], channel_multiplier=-1))
                link(pool.affine_select(out=mask_le[:, b], in_=mask_le[:, b], compare_op=ALU.is_ge, fill=0.0,
                                        base=0, pattern=[[1, P]], channel_multiplier=-1))
            link(pool.affine_select(out=head_sel[:], in_=head_sel[:], compare_op=ALU.is_equal, fill=0.0, base=0,
                                    pattern=[[-1, MH], [0, P]], channel_multiplier=1))
            link(pool.affine_select(out=half_ones[:, 0:1], in_=half_ones[:, 0:1], compare_op=ALU.is_gt, fill=0.0,
                                    base=64, pattern=[[0, 1]], channel_multiplier=-1))
            link(pool.affine_select(out=half_ones[:, 1:2], in_=half_ones[:, 1:2], compare_op=ALU.is_ge, fill=0.0,
                                    base=-64, pattern=[[0, 1]], channel_multiplier=1))
            link(pool.memset(bbd[:], 0.0))
            link(pool.memset(cbd[:], 0.0))
            for g in range(8):
                for c in range(2):
                    pool.dma_start(bbd[16 * g:16 * g + 16, c, :, (g % 2) * 64:(g % 2) * 64 + 64],
                                   dram["ssm_b"][16 * g:16 * g + 16, c]).then_inc(s_par, 16)
            pool.dma_start(craw[:], dram["ssm_c"]).then_inc(s_par, 16)
            pool.iota(slots[:], pattern=[[1, CAP]], base=0, channel_multiplier=0,
                      allow_small_or_imprecise_dtypes=True).then_inc(consts, 1)
            def weights_low(first, end):
                for n_ in range(first, end):
                    m = n_ - SPLIT
                    pool.wait_ge(hi_ready, m + 1)
                    pool.tensor_tensor(wl[:, m % SPLIT_RING], ring[:, n_ % RING],
                                       wh[:, m % SPLIT_RING].bitcast(F32), ALU.subtract).then_inc(lo_ready, 1)

            weights_low(SPLIT, UNIT_AT[("v2", 0)])
            pool.wait_ge(used, UNIT_AT["dn", FT - 1] + 1)
            pool.wait_ge(x_ready, 12)
            pool.dma_start(mixw, dram["mixw"]).then_inc(s_par2, 16)
            for g in range(2):
                pool.dma_start(bsp[64 * g:64 * g + 64], bass.AP(
                    tensor=dram["bsp"].tensor, offset=g * P, ap=[[0, 64], [2 * P, 4], [1, P]])).then_inc(s_par2, 16)
            pool.dma_start(w_if, dram["w_if"]).then_inc(s_par2, 16)
            pool.dma_start(b_if, dram["b_if"]).then_inc(s_par2, 16)
            weights_low(UNIT_AT[("v2", 0)], DENSE)
            pool.wait_ge(used, UNIT_AT["out2", 7] + 1)
            pool.dma_start(w_r, dram["w_r"]).then_inc(s_par3, 16)
            pool.dma_start(b_r, bass.AP(tensor=dram["b_r"].tensor, offset=0, ap=[[0, P], [1, 36]])
                           ).then_inc(s_par3, 16)

        @block.scalar
        def _(act):
            n = [0]

            def link(ins):
                n[0] += 1
                ins.then_inc(act_chain, 1)
                act.wait_ge(act_chain, n[0])

            def square_input(norm, src, ready=None):
                if norm:
                    act.wait_ge(sums, norm)
                for i in range(4):
                    if ready is not None:
                        act.wait_ge(x_ready, ready + i + 1)
                    act.activation(sq[:, 2 * i:2 * i + 2], src[:, 2 * i:2 * i + 2], ACT.Square).then_inc(squares, 1)

            def square_banks(norm, key, unit):
                act.wait_ge(sums, norm)
                for i in range(4):
                    unit_used(unit(i))
                    bank = pb.bank((key, i))
                    act.activation(two(sq, i), bank[:], ACT.Square).then_inc(squares, 1)
                    for c in range(2):
                        ins = act.mul(post[:, 2 * i + c], bank[:, c * T:c * T + T], col(NORMS[norm], 2 * i + c))
                    ins.then_inc(p_freed["act"], 1)
                weights_high(UNIT_AT[unit(3)] + 1 + SPLIT_RING)
                act.wait_ge(spread, norm + 1)
                act.copy(rb[:], STAT[:, T:2 * T]).then_inc(rb_ready, 1)

            def evict(key, unit, dst, scale=None):
                unit_used(unit)
                if scale is None:
                    act.copy(dst, pb.bank(key)[:]).then_inc(p_freed["act"], 1)
                else:
                    act.mul(dst, pb.bank(key)[:], scale).then_inc(p_freed["act"], 1)
                weights_high(UNIT_AT[unit] + 1 + SPLIT_RING)

            def two(v, i):
                return v[:, 2 * i:2 * i + 2].rearrange("p a t -> p (a t)")

            split = [SPLIT]

            def weights_high(end):
                while split[0] < min(end, DENSE):
                    n_, m = split[0], split[0] - SPLIT
                    act.wait_ge(landed[n_ % RING], 16 * (n_ // RING + 1))
                    act.wait_ge(used, max(n_ - SPLIT_RING + 1, SPLIT))
                    act.copy(wh[:, m % SPLIT_RING], ring[:, n_ % RING]).then_inc(hi_ready, 1)
                    split[0] += 1

            def unit_used(key):
                weights_high(UNIT_AT[key] + SPLIT_RING)
                act.wait_ge(used, UNIT_AT[key] + 1)

            highs = [0]

            def operand_high(dst, src, n_):
                for k in range(n_):
                    highs[0] += 1
                    act.wait_ge(op32, highs[0])
                    act.copy(dst[:, k], src[:, k]).then_inc(op_high, 1)

            act.dma_start(cols[:], dram["cols"]).then_inc(s_cols, 16)
            act.dma_start(ssm[:, 0:3], dram["ssm_a"]).then_inc(s_cols, 16)
            act.wait_ge(s_x, 16)
            square_input(0, x)
            act.wait_ge(s_cols, 32)
            act.activation(ssm[:, 3], ssm[:, 2], ACT.Exp).then_inc(ssm_trig, 1)
            act.wait_ge(ssm_args, 1)
            act.activation(ssm[:, 6], ssm[:, 4], ACT.Exp).then_inc(ssm_trig, 1)
            act.wait_ge(ssm_args, 2)
            act.activation(ssm[:, 10], ssm[:, 8], ACT.Sin).then_inc(ssm_trig, 1)
            act.activation(ssm[:, 11], ssm[:, 9], ACT.Sin).then_inc(ssm_trig, 1)
            act.wait_ge(s_mem, 16)
            square_input(1, mem)
            for i in range(2):
                evict(("u", i), ("u", 2 * i + 1), two(uT, i))
            for i in range(2):
                evict(("q", i), ("q", 2 * i + 1), two(qT, i), HD ** -0.5)
            for i in range(2):
                evict(("k", i), ("k", 2 * i + 1), two(kT, i))
            for i in range(2):
                evict(("v", i), ("v", 3), v1[:, i])

            def filler(slot):
                if slot == 0:
                    act.wait_ge(ssm_ready, 2)
                if slot < 4:
                    evict(("xk", slot), ("xk", 2 * slot + 1), two(xkT, slot))
                elif slot < 8:
                    if slot % 2:
                        half = (slot - 4) // 2
                        for tt in range(TT):
                            evict(("xv", 2 * half + tt), ("xv", 4 * half + 3), xv[:, tt, half * 512:half * 512 + 512])
                else:
                    i = slot - 8
                    if i == 0:
                        act.wait_ge(dve_halves, 1)
                    unit_used(("gate", 2 * i + 1))
                    for c in range(2):
                        ins = act.activation(gates[:, 2 * i + c], pb.bank(("gate", i))[:, c * T:c * T + T], ACT.Identity,
                                             bias=hb[:, 2 * i + c:2 * i + c + 1], scale=0.5)
                    ins.then_inc(p_freed["act"], 1)

            for r in range(HEADS + 1):
                if r < HEADS:
                    act.wait_ge(*xb.read(("z", r)))
                    if r:
                        act.wait_ge(sp_ready, r)
                    link(act.activation(az, zm[r % 2], ACT.Abs))
                    link(act.activation(az, az, ACT.Exp, scale=-1.0))
                    act.activation(az, az, ACT.Ln, bias=1.0).then_inc(sp_ln, 1)
                    filler(2 * r)
                if r:
                    act.wait_ge(*xb.read(("cum", r - 1)))
                    act.activation(w1, w1, ACT.Exp).then_inc(w_exp, 1)
                if r < HEADS:
                    filler(2 * r + 1)
                if r:
                    hd = r - 1
                    lo = HD * (hd % 2)
                    act.wait_ge(pv_done, r)
                    act.copy(oT[lo:lo + HD, hd // 2], xb.bank(("pv", hd))[lo:lo + HD, 0:T]).then_inc(x_freed["act"], 1)

            act.wait_ge(y_freed, 4)
            act.activation(gt, yT, ACT.Square).then_inc(gelu_sq, 1)
            act.wait_ge(gelu_in, 1)
            act.activation(gt, gt, ACT.Tanh, scale=GELU_K * GELU_C).then_inc(gelu_th, 1)
            act.activation(gates, gates, ACT.Tanh).then_inc(gates_th, 1)
            for i in range(2):
                unit_used(("glu", i))
                if i == 0:
                    act.wait_ge(y_ready, 1)
                for c in range(2):
                    ins = act.activation(gt[:, 2 * i + c], pb.bank(("glu", i))[:, c * T:c * T + T], ACT.Tanh,
                                         bias=hb[:, 16 + 2 * i + c:17 + 2 * i + c], scale=0.5)
                ins.then_inc(p_freed["act"], 1)
            square_banks(2, "out", lambda i: ("out", 2 * i + 1))

            square_input(3, x, 0)
            operand_high(hh, h, KT)
            for i in range(4):
                evict(("xq", i), ("xq", 2 * i + 1), two(xqT, i), (D // XH) ** -0.5)
            for i in range(8 + 1):
                if i < 8:
                    act.wait_ge(max_ready, i + 1)
                    if i >= 2:
                        act.wait_ge(pt_done, i - 1)
                    act.activation(prob[:, i % 2], xb.bank(("sc", i))[:, 0:T], ACT.Exp, bias=sm[:, 0, i:i + 1],
                                   accum_out=sm[:, 1, i:i + 1]).then_inc(x_freed["act"], 1)
                if i:
                    head, tt = (i - 1) // 2, (i - 1) % 2
                    act.wait_ge(pt_done, i)
                    if head >= 2 and tt == 0:
                        act.wait_ge(xo_done, head - 1)
                    act.copy(probT[:, head % 2, :, tt * P:tt * P + P],
                             xb.bank(("pt", i - 1))[:, 0:T].rearrange("p (m t) -> p m t", m=TT)
                             ).then_inc(x_freed["act"], 1)
                    if tt:
                        act.wait_ge(xo_done, head + 1)
                        act.copy(two(yh, head), pb.bank(("xav", head))[:]).then_inc(xo_high, 1)
            square_banks(4, "xo", lambda i: ("xo", 2 * i + 1))

            square_input(5, x, 4)
            operand_high(hh, h, KT)
            for j in range(FT):
                b = j % 3
                unit_used(("fv", j))
                if j >= 3:
                    act.wait_ge(hid_ready, j - 2)
                bank = xb.bank(("up", j))
                act.copy(up[:, b, :, 4:4 + T], bank[:].rearrange("p (c t) -> p c t", c=2))
                for c in range(2):
                    ins = act.activation(acc[:, b, c], bank[:, c * T:c * T + T], ACT.Identity,
                                         bias=col("conv_b", FT * c + j), scale=col("conv2", FT * c + j))
                ins.then_inc(x_freed["act"], 1)
                weights_high(UNIT_AT[("fv", j)] + 1 + SPLIT_RING)
                act.wait_ge(conv_g, j + 1)
                act.activation(fs[:, b, 0], acc[:, b, 0], ACT.Square).then_inc(gelu_sq, 1)
                weights_high(UNIT_AT[("fv", j)] + 2 + SPLIT_RING)
                act.wait_ge(gelu_in, j + 2)
                act.activation(fs[:, b, 0], fs[:, b, 0], ACT.Tanh, scale=GELU_K * GELU_C).then_inc(gelu_th, 1)
            square_banks(6, "dn", lambda i: ("dn", FT - 1))
            square_input(7, x, 8)
            operand_high(hh, h, KT)

            act.wait_ge(if_ready, 1)
            link(act.activation(ifr[:, 2], ifr[:, 1], ACT.Abs))
            link(act.activation(ifr[:, 2], ifr[:, 2], ACT.Exp, scale=-1.0))
            act.activation(ifr[:, 2], ifr[:, 2], ACT.Ln, bias=1.0).then_inc(if_ln, 1)
            for i in range(2):
                evict(("v2", i), ("v2", 3), v2[:, i])
            act.wait_ge(if_rows, 1)
            act.activation(ifr[:, 7], ifr[:, 7], ACT.Exp).then_inc(em_ready, 1)
            act.wait_ge(gt_done, 1)
            act.copy(gT, xb.bank(("gT", 0))[:, 0:TT * MH].rearrange("p (a b) -> p a b", a=TT)
                     ).then_inc(x_freed["act"], 1)
            for i in range(4):
                unit_used(("qk2", 2 * i + 1))
                if i >= 2:
                    act.wait_ge(qk_ready, i - 1)
                bank = pb.bank(("qk2", i))
                act.copy(qraw[:, i % 2, :, 4:4 + T], bank[:].rearrange("p (c t) -> p c t", c=2))
                for c in range(2):
                    ins = act.mul(qs[:, i % 2, c], bank[:, c * T:c * T + T], col("qk3", 2 * i + c))
                ins.then_inc(p_freed["act"], 1)
                act.wait_ge(qk_conv, i + 1)
                act.activation(qt[:, i % 2], qs[:, i % 2], ACT.Tanh, scale=0.5).then_inc(qk_th, 1)

            def gelu2(g, key, unit, keep, scratch):
                unit_used(unit)
                act.copy(keep, pb.bank(key)[:])
                act.activation(scratch, pb.bank(key)[:], ACT.Square).then_inc(p_freed["act"], 1)
                act.wait_ge(gelu_in, g + 1)
                act.activation(scratch, scratch, ACT.Tanh, scale=GELU_K * GELU_C).then_inc(gelu_th, 1)

            for tt in range(TT):
                gelu2(FT + 1 + tt, ("vg", tt), ("vg", 3), gv[:, tt], gvs[:, tt])
            for tt in range(TT):
                act.wait_ge(vb_ready, tt + 1)
                act.activation(gvs[:, tt], gv[:, tt], ACT.Square, accum_out=vsum[:, tt:tt + 1]).then_inc(vsq, 1)
            act.wait_ge(vsq, TT)
            for i in range(2):
                gelu2(FT + 3 + i, ("ug", i), ("ug", 2 * i + 1), two(ug, i), two(ugs, i))
            for i in range(2):
                unit_used(("o2", 2 * i + 1))
                act.activation(two(so, i), pb.bank(("o2", i))[:], ACT.Tanh, scale=0.5).then_inc(p_freed["act"], 1)
            for i in range(MH):
                act.wait_ge(dec_in, i + 1)
                act.activation(decay, decay, ACT.Exp, scale=-1.0).then_inc(dec_exp, 1)
                if i:
                    act.wait_ge(hm_ready, i)
                act.copy(emb, xb.bank(("rows", i))[:, T:2 * T]).then_inc(x_freed["act"], 1)
            act.wait_ge(hm_ready, MH)
            act.activation(sq[:, 0:4], hm, ACT.Square).then_inc(hsq, 1)
            act.wait_ge(gm_ready, 1)
            act.activation(sq[:, 4:8], gm, ACT.Square).then_inc(hsq, 1)
            act.wait_ge(hsum, 1)
            operand_high(yh, h, KT)
            act.wait_ge(sums, 8)
            for i in range(4):
                weights_high(UNIT_AT[("out2", 2 * i + 1)] + 1 + SPLIT_RING)
                act.wait_ge(x_ready, 12 + i + 1)
                act.activation(two(sq, i), two(x, i), ACT.Square).then_inc(squares, 1)

            for i in range(4):
                act.wait_ge(tr_done, i + 1)
                act.copy(xtok[:, i // 2, (i % 2) * 512:(i % 2) * 512 + 512], xb.bank(("tr", i))[:]
                         ).then_inc(x_freed["act"], 1)
            for tt in range(TT):
                act.wait_ge(rt_max, tt + 1)
                act.activation(rsm[:, tt, 8:12], lg[:, tt, 0:NG], ACT.Exp, bias=rsm[:, tt, 0:1],
                               accum_out=rsm[:, tt, 1:2]).then_inc(rt_exp, 1)
            for tt in range(TT):
                act.wait_ge(rt_max, TT + tt + 1)
                act.activation(rsm[:, tt, 4:5], rsm[:, tt, 3:4], ACT.Exp).then_inc(rt_exp, 1)
            act.wait_ge(rounds_ready, 1)
            n_pairs = act.value_load(rounds[0:1, 0:1], min_val=1, max_val=MAXR) * PAIRS
            xg0 = xg[:, 0:4].rearrange("p k c -> p (k c)")
            act.wait_ge(gath_done, 1)
            act.copy(xg0, psum[6][:]).then_inc(xg_low, 1)
            with act.Fori(0, n_pairs) as it:
                act.wait_ge(used, it * PAIR + (DENSE + 2 * KT))
                act.wait_ge(hx_ready, it + 1)
                act.activation(gate_th, psum[4][:], ACT.Tanh, scale=0.5).then_inc(hid_th, 1)
                act.wait_ge(gath_done, 2 * it + 3)
                act.copy(xg0, psum[6][:]).then_inc(xg_low, 1)
                act.wait_ge(hT_done, it + 1)
                act.copy(hT.rearrange("p f c -> p (f c)"), psum[4][:]).then_inc(hT_ready, 1)
                act.wait_ge(used, it * PAIR + (DENSE + PAIR))
                act.copy(yg[:, 0:512], psum[6][:]).then_inc(yg_low, 1)
            square_input(9, x, 16)

        @block.vector
        def _(dve):
            n = [0]

            def link(ins):
                n[0] += 1
                ins.then_inc(dve_chain, 1)
                dve.wait_ge(dve_chain, n[0])

            def two(v, i):
                return v[:, 2 * i:2 * i + 2].rearrange("p a t -> p (a t)")

            def ts(o, a, s1, op0, s2=None, op1=None):
                if op1 is None:
                    return dve.tensor_scalar(o, a, s1, None, op0)
                return dve.tensor_scalar(o, a, s1, s2, op0, op1)

            def tt_(o, a, b, op):
                return dve.tensor_tensor(o, a, b, op)

            def stt(o, a, s1, b, op0, op1):
                return dve.scalar_tensor_tensor(out=o, in0=a, scalar=s1, in1=b, op0=op0, op1=op1)

            def rsqrt(w):
                a, y, t = ms[:, 0:w], rstd[:, 0:w], rt[:, 0:w]
                link(ts(ri[:, 0:w], a.bitcast(I32), 1, ALU.logical_shift_right))
                link(ts(y.bitcast(I32), ri[:, 0:w], -1, ALU.mult, RSQRT_SEED, ALU.add))
                for step in range(3):
                    link(tt_(t, a, y, ALU.mult))
                    link(tt_(t, t, y, ALU.mult))
                    ins = stt(y, t, 1.5, y, ALU.add, ALU.mult)
                    if step < 2:
                        link(ins)
                return ins

            def norm_scale(norm):
                dve.wait_ge(sums, norm + 1)
                link(ts(ms[:, 0:TT], STAT[:, 0:TT], -0.5 / D, ALU.mult, -0.5 * EPS, ALU.add))
                rsqrt(TT).then_inc(scales, 1)

            def normed(norm, src, dst, done):
                dve.wait_ge(spread, norm + 1)
                for k in range(KT):
                    stt(dst[:, k], src[:, k], col(NORMS[norm], k), STAT[:, T:2 * T], ALU.mult, ALU.mult
                        ).then_inc(done, 1)

            def add_normed(norm, key):
                dve.wait_ge(rb_ready, norm // 2)
                rms = rb[:].unsqueeze(1).to_broadcast([P, 2, T])
                for i in range(5):
                    if i < 4:
                        dve.wait_ge(*pb.read((key, i)))
                        tt_(post[:, 2 * i:2 * i + 2], post[:, 2 * i:2 * i + 2], rms, ALU.mult).then_inc(scaled, 1)
                    if i:
                        done_x[0] += 1
                        dve.wait_ge(scaled, done_x[0])
                        tt_(x[:, 2 * i - 2:2 * i], x[:, 2 * i - 2:2 * i], post[:, 2 * i - 2:2 * i], ALU.add
                            ).then_inc(x_ready, 1)

            lows = [0]

            def operand_lows(dst_high, dst_low, src, made, n_, done):
                for k in range(n_ + 2):
                    if k < n_:
                        made(k).then_inc(op32, 1)
                    if k >= 2:
                        lows[0] += 1
                        dve.wait_ge(op_high, lows[0])
                        tt_(dst_low[:, k - 2], src[:, k - 2], dst_high[:, k - 2].bitcast(F32), ALU.subtract
                            ).then_inc(done, 1)

            def normed_split(norm):
                dve.wait_ge(spread, norm + 1)
                operand_lows(hh, hl, h, lambda k: stt(h[:, k], x[:, k], col(NORMS[norm], k), STAT[:, T:2 * T],
                                                      ALU.mult, ALU.mult), KT, h_ready)

            done_x = [0]

            norm_scale(0)
            dve.wait_ge(s_cols, 32)
            normed(0, x, h, h_ready)
            ts(hb[:, 0:16], cols[:, COLS["b_gate"][0]:COLS["b_gate"][0] + 16], 0.5, ALU.mult)
            ts(hb[:, 16:20], cols[:, COLS["b_glu"][0]:COLS["b_glu"][0] + 4], 0.5, ALU.mult).then_inc(dve_halves, 1)
            are, aim, dt, adt, th = ssm[:, 0], ssm[:, 1], ssm[:, 3], ssm[:, 4], ssm[:, 5]
            rad, turns, ang, cang, sin, cos = ssm[:, 6], ssm[:, 7], ssm[:, 8], ssm[:, 9], ssm[:, 10], ssm[:, 11]
            lr, li, den, num = ssm[:, 12], ssm[:, 13], ssm[:, 15], ssm[:, 16]
            t1, t2, fre, fim = ssm[:, 17], ssm[:, 18], ssm[:, 19], ssm[:, 20]
            dve.wait_ge(ssm_trig, 1)
            tt_(adt, are, dt, ALU.mult).then_inc(ssm_args, 1)
            link(tt_(th, aim, dt, ALU.mult))
            link(ts(turns, th, 1.0 / (2 * np.pi), ALU.mult, ROUND, ALU.add))
            link(ts(turns, turns, -ROUND, ALU.add))
            link(stt(ang, turns, -TWO_PI_HI, th, ALU.mult, ALU.add))
            link(stt(ang, turns, -TWO_PI_LO, ang, ALU.mult, ALU.add))
            link(ts(ang, ang, 3.1415925, ALU.min, -3.1415925, ALU.max))
            link(ts(t1, ang, -1.0, ALU.mult))
            link(tt_(t1, t1, ang, ALU.max))
            ts(cang, t1, -1.0, ALU.mult, np.pi / 2, ALU.add).then_inc(ssm_args, 1)
            norm_scale(1)
            normed(1, mem, mem, h_ready)
            dve.wait_ge(ssm_trig, 4)
            link(tt_(lr, rad, cos, ALU.mult))
            link(tt_(li, rad, sin, ALU.mult))
            link(ts(num, lr, -1.0, ALU.add))
            link(tt_(t1, are, are, ALU.mult))
            link(tt_(t2, aim, aim, ALU.mult))
            link(tt_(den, t1, t2, ALU.add))
            link(dve.reciprocal(den, den))
            link(tt_(t1, num, are, ALU.mult))
            link(tt_(t2, li, aim, ALU.mult))
            link(tt_(t1, t1, t2, ALU.add))
            link(tt_(fre, t1, den, ALU.mult))
            link(tt_(t1, li, are, ALU.mult))
            link(tt_(t2, num, aim, ALU.mult))
            link(tt_(t1, t1, t2, ALU.subtract))
            link(tt_(fim, t1, den, ALU.mult))
            link(dve.tensor_copy(powers[:, 0, 0], cos))
            link(dve.tensor_copy(powers[:, 0, 1], sin))
            link(dve.memset(rot[:, 0, :, 0:1], 1.0))
            link(dve.memset(rot[:, 1, :, 0:1], 0.0))
            k, w = 0, 1
            while w < T:
                c_, s_ = powers[:, k % 2, 0], powers[:, k % 2, 1]
                cb, sbb = (v.unsqueeze(2).to_broadcast([P, STILES, w]) for v in (c_, s_))
                a3 = ta[:, 0:STILES * w].rearrange("p (j t) -> p j t", j=STILES)
                b3 = tb[:, 0:STILES * w].rearrange("p (j t) -> p j t", j=STILES)
                tt_(a3, rot[:, 0, :, 0:w], cb, ALU.mult)
                link(tt_(b3, rot[:, 1, :, 0:w], sbb, ALU.mult))
                link(tt_(rot[:, 0, :, w:2 * w], a3, b3, ALU.subtract))
                tt_(a3, rot[:, 0, :, 0:w], sbb, ALU.mult)
                link(tt_(b3, rot[:, 1, :, 0:w], cb, ALU.mult))
                link(tt_(rot[:, 1, :, w:2 * w], a3, b3, ALU.add))
                if 2 * w < T:
                    tt_(ptmp[:, 0], c_, c_, ALU.mult)
                    tt_(ptmp[:, 1], s_, s_, ALU.mult)
                    link(tt_(ptmp[:, 2], c_, s_, ALU.mult))
                    tt_(powers[:, (k + 1) % 2, 0], ptmp[:, 0], ptmp[:, 1], ALU.subtract)
                    link(ts(powers[:, (k + 1) % 2, 1], ptmp[:, 2], 2.0, ALU.mult))
                k, w = k + 1, 2 * w
            dve.wait_ge(s_par, 16 * 17)
            dve.wait_ge(consts, 2)
            fr, fi = (v.unsqueeze(2).to_broadcast([P, STILES, 16]) for v in (fre, fim))
            a3 = ta[:, 0:256].rearrange("p (j t) -> p j t", j=STILES)
            b3 = tb[:, 0:256].rearrange("p (j t) -> p j t", j=STILES)
            tt_(a3, craw[:, 0], fr, ALU.mult)
            link(tt_(b3, craw[:, 1], fi, ALU.mult))
            for g in range(2):
                link(tt_(cbd[64 * g:64 * g + 64, 0, :, 16 * g:16 * g + 16], a3[64 * g:64 * g + 64],
                         b3[64 * g:64 * g + 64], ALU.subtract))
            tt_(a3, craw[:, 0], fi, ALU.mult)
            link(tt_(b3, craw[:, 1], fr, ALU.mult))
            for g in range(2):
                stt(cbd[64 * g:64 * g + 64, 1, :, 16 * g:16 * g + 16], a3[64 * g:64 * g + 64], -1.0,
                    b3[64 * g:64 * g + 64], ALU.mult, ALU.subtract).then_inc(ssm_ready, 1)
            dve.wait_ge(ssm_ready, 2)

            def turned(j, which):
                return rot[:, which, j].unsqueeze(1).to_broadcast([P, 2, T])

            def recurrence(j):
                dve.wait_ge(bu_done, j + 1)
                bank = xb.bank(("bu", j))[:].rearrange("p (c t) -> p c t", c=2)
                tt_(m1, bank, turned(j, 0), ALU.mult)
                tt_(m2, bank, turned(j, 1), ALU.mult).then_inc(x_freed["dve"], 1)
                dve.wait_ge(*xb.read(("bu", j)))
                tt_(vr[:, 0], m1[:, 0], m2[:, 1], ALU.add)
                link(tt_(vr[:, 1], m1[:, 1], m2[:, 0], ALU.subtract))
                r_ = rad[:, j:j + 1].to_broadcast([P, T])
                for c in range(2):
                    ins = dve.tensor_tensor_scan(wr[:, c], r_, vr[:, c], 0.0, ALU.mult, ALU.add)
                link(ins)
                tt_(m1, wr, turned(j, 0), ALU.mult)
                link(tt_(m2, wr, turned(j, 1), ALU.mult))
                if j >= 2:
                    dve.wait_ge(y_done, j - 1)
                tt_(st[:, j % 2, 0], m1[:, 0], m2[:, 1], ALU.subtract)
                tt_(st[:, j % 2, 1], m1[:, 1], m2[:, 0], ALU.add).then_inc(st_ready, 1)
                dve.wait_ge(st_ready, j + 1)

            def y_out(i):
                dve.wait_ge(y_done, 4 * i + 4)
                stt(yT[:, i], uT[:, i], col("d", i), STAT[:, 0:T], ALU.mult, ALU.add).then_inc(y_freed, 1)

            for r in range(HEADS + 1):
                if r >= 3 and r % 2:
                    y_out((r - 3) // 2)
                if r < HEADS:
                    recurrence(2 * r)
                    dve.wait_ge(z_done, r + 1)
                    tt_(zm[r % 2], xb.bank(("z", r))[:, 0:384], mask_lt[:].rearrange("p a t -> p (a t)"), ALU.mult
                        ).then_inc(x_freed["dve"], 1)
                    dve.wait_ge(*xb.read(("z", r)))
                if r:
                    dve.wait_ge(cum_done, r)
                    if r >= 2:
                        dve.wait_ge(pv_done, r - 1)
                    tt_(w1, zm[(r - 1) % 2], xb.bank(("cum", r - 1))[:, 0:384], ALU.subtract
                        ).then_inc(x_freed["dve"], 1)
                if r < HEADS:
                    recurrence(2 * r + 1)
                    dve.wait_ge(sp_ln, r + 1)
                    link(stt(sp, zm[r % 2], 0.0, az, ALU.max, ALU.add))
                    tt_(sp, sp, mask_lt[:].rearrange("p a t -> p (a t)"), ALU.mult).then_inc(sp_ready, 1)
                if r:
                    dve.wait_ge(w_exp, r)
                    tt_(w1, w1, mask_lt[:].rearrange("p a t -> p (a t)"), ALU.mult).then_inc(w_ready, 1)
            y_out(3)
            dve.wait_ge(y_freed, 4)
            dve.wait_ge(gelu_sq, 1)
            stt(gt, gt, 1.0 / GELU_C, yT, ALU.add, ALU.mult).then_inc(gelu_in, 1)
            dve.wait_ge(gelu_th, 1)
            link(ts(gt, gt, 0.5, ALU.mult, 0.5, ALU.add))
            tt_(yT, gt, yT, ALU.mult).then_inc(y_ready, 1)
            dve.wait_ge(gates_th, 1)
            link(ts(gates, gates, 0.5, ALU.mult, 0.5, ALU.add))
            dve.wait_ge(*pb.read(("glu", 1)))
            link(ts(gt, gt, 0.5, ALU.mult, 0.5, ALU.add))
            tt_(gt, gt, yT, ALU.mult).then_inc(ossm_ready, 1)
            for i in range(4):
                for c, key in enumerate(("ba", "bs")):
                    dve.wait_ge(used, UNIT_AT[(key, i)] + 1)
                    if i and c == 0:
                        dve.wait_ge(merged_ready, i)
                    tt_(mg[:, c], two(gates, 4 * c + i), pb.bank((key, i))[:], ALU.mult).then_inc(p_freed["dve"], 1)
                    dve.wait_ge(*pb.read((key, i)))
                tt_(two(merged, i), mg[:, 0], mg[:, 1], ALU.add).then_inc(merged_ready, 1)
            norm_scale(2)
            add_normed(2, "out")

            norm_scale(3)
            normed_split(3)

            def attended(hh_):
                dve.wait_ge(xo_high, hh_ + 1)
                tt_(two(yl, hh_), pb.bank(("xav", hh_))[:], two(yh, hh_).bitcast(F32), ALU.subtract
                    ).then_inc(p_freed["dve"], 1)

            for i in range(8 + 1):
                if i < 8:
                    dve.wait_ge(sc_done, i + 1)
                    link(dve.tensor_reduce(sm[:, 2, i:i + 1], xb.bank(("sc", i))[:, 0:T], AX.X, ALU.max))
                    ts(sm[:, 0, i:i + 1], sm[:, 2, i:i + 1], -1.0, ALU.mult).then_inc(max_ready, 1)
                if i:
                    dve.wait_ge(*xb.read(("sc", i - 1)))
                    link(dve.reciprocal(sm[:, 3, i - 1:i], sm[:, 1, i - 1:i]))
                    ts(prob[:, (i - 1) % 2], prob[:, (i - 1) % 2], sm[:, 3, i - 1:i], ALU.mult
                       ).then_inc(prob_ready, 1)
                if i >= 3 and i % 2:
                    attended(i // 2 - 1)
            attended(XH - 1)
            norm_scale(4)
            add_normed(4, "xo")

            norm_scale(5)
            normed_split(5)
            link(dve.memset(up[:, :, :, 0:4], 0.0))
            for j in range(FT):
                b = j % 3
                dve.wait_ge(*xb.read(("up", j)))
                for tap, lag in ((1, 1), (0, 2)):
                    for c in range(2):
                        ins = stt(acc[:, b, c], up[:, b, c, 4 - lag:4 - lag + T], col(f"conv{tap}", FT * c + j),
                                  acc[:, b, c], ALU.mult, ALU.add)
                    if tap:
                        link(ins)
                ins.then_inc(conv_g, 1)
                dve.wait_ge(conv_g, j + 1)
                dve.wait_ge(gelu_sq, j + 2)
                stt(fs[:, b, 0], fs[:, b, 0], 1.0 / GELU_C, acc[:, b, 0], ALU.add, ALU.mult).then_inc(gelu_in, 1)
                dve.wait_ge(gelu_th, j + 2)
                link(stt(fs[:, b, 1], fs[:, b, 0], 1.0, acc[:, b, 0], ALU.add, ALU.mult))
                if j >= 3:
                    dve.wait_ge(used, UNIT_AT[("dn", j - 3)] + 1)
                link(stt(hid32[:, b], fs[:, b, 1], 0.5, acc[:, b, 1], ALU.mult, ALU.mult))
                link(dve.tensor_copy(yh[:, b], hid32[:, b]))
                tt_(yl[:, b], hid32[:, b], yh[:, b].bitcast(F32), ALU.subtract).then_inc(hid_ready, 1)
            norm_scale(6)
            add_normed(6, "dn")

            norm_scale(7)
            normed_split(7)
            dve.wait_ge(s_par2, 16 * 5)
            dve.wait_ge(if_done, 1)
            bank = xb.bank(("if", 0))
            ts(ifr[:, 1], bank[0:MH, T:2 * T], b_if[:, 1:2], ALU.add).then_inc(if_ready, 1)
            link(ts(ifr[:, 0], bank[0:MH, 0:T], b_if[:, 0:1], ALU.add))
            link(dve.memset(ifr[:, 9], 1.0))
            tt_(mixw, mixw, mask_le[:, 0].unsqueeze(1).to_broadcast([P, GG, P]), ALU.mult).then_inc(x_freed["dve"], 1)
            dve.wait_ge(*xb.read(("if", 0)))
            dve.wait_ge(if_ln, 1)
            link(stt(ifr[:, 3], ifr[:, 1], 0.0, ifr[:, 2], ALU.min, ALU.subtract))
            link(dve.tensor_tensor_scan(ifr[:, 4], ifr[:, 9], ifr[:, 3], 0.0, ALU.mult, ALU.add))
            link(tt_(ifr[:, 5], ifr[:, 0], ifr[:, 4], ALU.subtract))
            link(dve.tensor_tensor_scan(ifr[:, 6], ifr[:, 5], ifr[:, 5], 0.0, ALU.max, ALU.max))
            link(tt_(ifr[:, 7], ifr[:, 4], ifr[:, 6], ALU.add))
            ts(ifr[:, 7], ifr[:, 7], -1.0, ALU.mult, 87.0, ALU.min).then_inc(if_rows, 1)
            link(dve.memset(qraw[:, :, :, 0:4], 0.0))
            dve.wait_ge(if_rows, 1)
            dve.nop().then_inc(qpad, 1)
            for i in range(4):
                b = i % 2
                dve.wait_ge(*pb.read(("qk2", i)))
                for tap in (2, 1, 0):
                    for c in range(2):
                        ins = stt(qs[:, b, c], qraw[:, b, c, 1 + tap:1 + tap + T], col(f"qk{tap}", 2 * i + c),
                                  qs[:, b, c], ALU.mult, ALU.add)
                    if tap:
                        link(ins)
                ins.then_inc(qk_conv, 1)
                dve.wait_ge(qk_th, i + 1)
                stt(qk2[:, 2 * i:2 * i + 2], qt[:, b], 1.0, qs[:, b], ALU.add, ALU.mult).then_inc(qk_ready, 1)

            def gelu2(g, keep, scratch):
                stt(scratch, scratch, 1.0 / GELU_C, keep, ALU.add, ALU.mult).then_inc(gelu_in, 1)
                dve.wait_ge(gelu_th, g + 1)
                link(ts(scratch, scratch, 0.5, ALU.mult, 0.5, ALU.add))
                return tt_(keep, keep, scratch, ALU.mult)

            for tt in range(TT):
                dve.wait_ge(*pb.read(("vg", tt)))
                gelu2(FT + 1 + tt, gv[:, tt], gvs[:, tt]).then_inc(vb_ready, 1)
            for tt in range(TT):
                dve.wait_ge(vsq, tt + 1)
            link(ts(ms[:, 0:TT], vsum, -0.5 / 512, ALU.mult, -0.5 * EPS, ALU.add))
            link(rsqrt(TT))
            for tt in range(TT):
                ts(gv[:, tt], gv[:, tt], rstd[:, tt:tt + 1], ALU.mult).then_inc(vb_ready, 1)
            for i in range(2):
                dve.wait_ge(*pb.read(("ug", i)))
                link(gelu2(FT + 3 + i, two(ug, i), two(ugs, i)))
            dve.wait_ge(*pb.read(("o2", 1)))
            link(ts(so, so, 0.5, ALU.mult, 0.5, ALU.add))
            c2 = 0.25 * P ** -0.5
            for i in range(MH):
                dve.wait_ge(rows_done, i + 1)
                bank = xb.bank(("rows", i))
                ts(decay[:, 0:T], bank[:, 0:T], gT[:, 0, i:i + 1], ALU.subtract, 0.0, ALU.max)
                ts(decay[:, T:384], bank[:, P:T], gT[:, 1, i:i + 1], ALU.subtract, 0.0, ALU.max).then_inc(dec_in, 1)
                dve.wait_ge(dec_exp, i + 1)
                link(tt_(decay, decay, mask_le[:].rearrange("p a t -> p (a t)"), ALU.mult))
                dve.wait_ge(s2_done, i + 1)
                stt(st2, xb.bank(("s2", i))[:, 0:384], c2, decay, ALU.mult, ALU.mult).then_inc(x_freed["dve"], 1)
                dve.wait_ge(*xb.read(("rows", i)))
                dve.wait_ge(num_done, i + 1)
                bank = xb.bank(("num", i))
                link(stt(hden, bank[:, T:2 * T], -1.0, emb, ALU.mult, ALU.max))
                link(tt_(hden, bank[:, T:2 * T], hden, ALU.max))
                link(dve.reciprocal(hden, hden))
                tt_(hden, bank[:, 0:T], hden, ALU.mult).then_inc(x_freed["dve"], 1)
                dve.wait_ge(*xb.read(("num", i)))
                tt_(hm[:, i], hden, so[:, i], ALU.mult).then_inc(hm_ready, 1)
                dve.wait_ge(hm_ready, i + 1)
            for i in range(2):
                dve.wait_ge(mix_done, i + 1)
                bank = xb.bank(("mix", i))
                for c in range(2):
                    t_ = 2 * i + c
                    ins = stt(gm[:, t_].rearrange("p (n t) -> p n t", n=TT),
                              bank[:, c * T:c * T + T].rearrange("p (n t) -> p n t", n=TT), col("g_v", t_),
                              bsp[:, t_].unsqueeze(1).to_broadcast([P, TT, P]), ALU.mult, ALU.add)
                ins.then_inc(x_freed["dve"], 1)
            dve.wait_ge(*xb.read(("mix", 1)))
            tt_(gm, gm, ug, ALU.mult).then_inc(gm_ready, 1)
            dve.wait_ge(hsum, 1)
            bank = xb.bank(("hsum", 0))
            ts(ms[:, 0:8], bank[:, 0:8], -0.5 / P, ALU.mult, -0.5 * EPS, ALU.add)
            ts(ms[:, 8:24], bank[:, 8:24], -0.5 / 64, ALU.mult, -0.5 * EPS, ALU.add).then_inc(x_freed["dve"], 1)
            dve.wait_ge(*xb.read(("hsum", 0)))
            rsqrt(24).then_inc(hscale, 1)

            def headed(t_):
                i, c = t_ // 2, t_ % 2
                if c == 0:
                    dve.wait_ge(hspread, i + 1)
                src, g_ = (hm[:, t_], col("g_mlstm", t_)) if t_ < 4 else (gm[:, t_ - 4], col("g_gmlp", t_ - 4))
                return stt(h[:, t_], src, g_, xb.bank(("hspread", i))[:, c * T:c * T + T], ALU.mult, ALU.mult)

            operand_lows(yh, yl, h, headed, KT, op_low)
            for i in range(4):
                dve.wait_ge(used, UNIT_AT[("out2", 2 * i + 1)] + 1)
                if i == 0:
                    dve.wait_ge(x_ready, done_x[0])
                tt_(two(x, i), two(x, i), pb.bank(("out2", i))[:], ALU.add).then_inc(x_ready, 1)
            norm_scale(8)
            normed(8, x, h, h_ready)

            dve.wait_ge(s_par3, 32)
            link(ts(first, slots[:, 0:EG], -1.0, ALU.mult, float(EG), ALU.add))
            link(dve.memset(rank, -1.0))
            link(dve.memset(wall, 0.0))
            dve.memset(zero, 0.0).then_inc(y_zeroed, 1)
            dve.memset(scwT, 0.0).then_inc(scwT_ready, 1)
            dve.memset(yg[:, 0:512], 0.0).then_inc(yg_low, 1)
            dve.memset(yg[:, 512:D], 0.0).then_inc(yg_high, 1)
            dve.memset(hT, 0.0).then_inc(hT_ready, 1)
            dve.memset(hx, 0.0).then_inc(hx_ready, 1)
            dve.wait_ge(lg_done, 1)
            bank = xb.bank(("lg", 0))
            for tt in range(TT):
                ins = tt_(lg[:, tt], bank[:, 64 * tt:64 * tt + 36], b_r, ALU.add)
            ins.then_inc(x_freed["dve"], 1)
            dve.wait_ge(*xb.read(("lg", 0)))

            def pick(values, w, where, best, tmp):
                link(dve.tensor_reduce(best, values, AX.X, ALU.max))
                link(ts(where, values, best, ALU.is_equal))
                link(tt_(where, where, first[:, 0:w], ALU.mult))
                link(dve.tensor_reduce(tmp, where, AX.X, ALU.max))
                link(ts(where, where, tmp, ALU.is_equal))

            for tt in range(TT):
                r_ = rsm[:, tt]
                pick(lg[:, tt, 0:NG], NG, gsel[:, tt], r_[:, 5:6], r_[:, 6:7])
                ts(r_[:, 0:1], r_[:, 5:6], -1.0, ALU.mult).then_inc(rt_max, 1)
            dve.wait_ge(rt_max, TT)
            for tt in range(TT):
                r_ = rsm[:, tt]
                le = lsel[:, 0, tt]
                link(ts(le, lg[:, tt, NG:NG + EG], gsel[:, tt, 0:1], ALU.mult))
                for g in range(1, NG):
                    link(stt(le, lg[:, tt, NG + EG * g:NG + EG * g + EG], gsel[:, tt, g:g + 1], le,
                             ALU.mult, ALU.add))
                pick(le, EG, sel1[:, tt], r_[:, 7:8], r_[:, 6:7])
                rest = lsel[:, 1, tt]
                link(stt(rest, sel1[:, tt], -3.0e38, le, ALU.mult, ALU.add))
                pick(rest, EG, sel2[:, tt], r_[:, 12:13], r_[:, 6:7])
                tt_(r_[:, 3:4], r_[:, 12:13], r_[:, 7:8], ALU.subtract).then_inc(rt_max, 1)
            for tt in range(TT):
                r_ = rsm[:, tt]
                dve.wait_ge(rt_exp, TT + tt + 1)
                link(ts(r_[:, 13:14], r_[:, 4:5], 1.0, ALU.add))
                link(tt_(r_[:, 13:14], r_[:, 13:14], r_[:, 1:2], ALU.mult))
                link(dve.reciprocal(r_[:, 14:15], r_[:, 13:14]))
                link(tt_(r_[:, 15:16], r_[:, 14:15], r_[:, 4:5], ALU.mult))
                both, wts = lsel[:, 2, tt], lsel[:, 3, tt]
                link(tt_(both, sel1[:, tt], sel2[:, tt], ALU.add))
                link(ts(wts, sel1[:, tt], r_[:, 14:15], ALU.mult))
                link(stt(wts, sel2[:, tt], r_[:, 15:16], wts, ALU.mult, ALU.add))
                for g in range(NG):
                    ts(selw[:, tt, EG * g:EG * g + EG], wts, gsel[:, tt, g:g + 1], ALU.mult)
                    ins = ts(selm[:, tt, EG * g:EG * g + EG], both, gsel[:, tt, g:g + 1], ALU.mult)
                ins.then_inc(sel_ready, 1)
            dve.wait_ge(rank_done, 1)
            bank = xb.bank(("rank", 0))
            for tt in range(TT):
                link(tt_(lmask[:, tt], bank[:, NE * tt:NE * tt + NE], selm[:, tt], ALU.mult))
                link(stt(lmask[:, tt], selm[:, tt], -1.0, lmask[:, tt], ALU.add, ALU.add))
                for r in range(MAXR):
                    ts(rank[:, tt, NE * r:NE * r + NE], lmask[:, tt], float(-CAP * r), ALU.add)
                    ins = dve.tensor_copy(wall[:, tt, NE * r:NE * r + NE], selw[:, tt])
                link(ins)
            dve.tensor_reduce(cnt[:, 0:1], bank[:, 2 * NE:3 * NE], AX.X, ALU.max).then_inc(x_freed["dve"], 1)
            dve.wait_ge(*xb.read(("rank", 0)))
            link(ts(cnt[:, 1:2], cnt[:, 0:1], CAP + 0.5, ALU.is_gt, 1.0, ALU.add))
            for r in range(2, MAXR):
                link(ts(cnt[:, 2:3], cnt[:, 0:1], CAP * r + 0.5, ALU.is_gt))
                link(tt_(cnt[:, 1:2], cnt[:, 1:2], cnt[:, 2:3], ALU.add))
            dve.tensor_copy(rounds[0:1, 0:1], cnt[0:1, 1:2]).then_inc(rounds_ready, 1)

            dve.wait_ge(rounds_ready, 1)
            n_pairs = dve.value_load(rounds[0:1, 0:1], min_val=1, max_val=MAXR) * PAIRS

            def gather_matrix(first_column):
                for e in range(2):
                    for tt in range(TT):
                        ins = ts(gat[:, tt, CAP * e:CAP * e + CAP], slots[:],
                                 rank[:, tt, bass.ds(first_column + e, 1)], ALU.is_equal)
                ins.then_inc(g_ready, 1)

            xg1 = xg[:, 4:8].rearrange("p k c -> p (k c)")
            gather_matrix(0)
            dve.wait_ge(gath_done, 2)
            dve.tensor_copy(xg1, psum[7][:]).then_inc(xg_high, 1)
            with dve.Fori(0, n_pairs) as it:
                dve.wait_ge(gath_done, 2 * it + 2)
                gather_matrix(2 * it + 2)
                dve.wait_ge(scwT_ready, it + 1)
                for e in range(2):
                    for tt in range(TT):
                        ins = ts(scw[:, tt, CAP * e:CAP * e + CAP], slots[:], rank[:, tt, bass.ds(2 * it + e, 1)],
                                 ALU.is_equal, wall[:, tt, bass.ds(2 * it + e, 1)], ALU.mult)
                ins.then_inc(scw_ready, 1)
                dve.wait_ge(hid_th, it + 1)
                stt(act_, gate_th, 1.0, psum[4][:], ALU.add, ALU.mult).then_inc(silu_done, 1)
                dve.wait_ge(silu_done, it + 1)
                stt(hx, act_, 0.5, psum[5][:], ALU.mult, ALU.mult).then_inc(hx_ready, 1)
                dve.wait_ge(gath_done, 2 * it + 4)
                dve.tensor_copy(xg1, psum[7][:]).then_inc(xg_high, 1)
                dve.wait_ge(scwT_done, it + 1)
                dve.tensor_copy(scwT, psum[5][:, 0:T]).then_inc(scwT_ready, 1)
                dve.wait_ge(used, it * PAIR + (DENSE + PAIR))
                dve.tensor_copy(yg[:, 512:D], psum[7][:]).then_inc(yg_high, 1)
            dve.wait_ge(moe_done, 1)
            for i in range(4):
                tt_(two(x, i), two(x, i), psum[i][:], ALU.add).then_inc(x_ready, 1)
            norm_scale(9)
            dve.wait_ge(x_ready, 20)
            normed(9, x, res, res_ready)

        @block.tensor
        def _(pe):
            def unit(key):
                k = UNIT_AT[key]
                pe.wait_ge(landed[k % RING], 16 * (k // RING + 1))
                return ring[:, k % RING]

            def mm(o, a, b, start, stop):
                return pe.matmul(o, a, b, start=start, stop=stop, skip_group_check=True)

            def split_unit(key):
                m = UNIT_AT[key] - SPLIT
                pe.wait_ge(lo_ready, m + 1)
                return wh[:, m % SPLIT_RING], wl[:, m % SPLIT_RING]

            def mm_split(o, a_parts, b_parts, start, stop):
                (ah, al), (bh, bl) = a_parts, b_parts
                mm(o, ah, bh, start, False)
                mm(o, ah, bl, False, False)
                return mm(o, al, bh, False, stop)

            def norm_sum(norm, i):
                pe.wait_ge(squares, 4 * norm + i + 1)
                for k in range(2 * i, 2 * i + 2):
                    for tt in range(TT):
                        ins = mm(STAT[:, tt:tt + 1], sq[:, k, tt * P:tt * P + P], ones[:, 0:1],
                                 k == 0 and tt == 0, k == KT - 1)
                if i == 3:
                    ins.then_inc(sums, 1)

            def norm_sums(norm, first=0):
                for i in range(first, 4):
                    norm_sum(norm, i)
                pe.wait_ge(scales, norm + 1)
                for tt in range(TT):
                    ins = mm(STAT[:, T + tt * P:T + tt * P + P], rstd[:, tt:tt + 1].to_broadcast([P, P]), ident[:],
                             True, True)
                ins.then_inc(spread, 1)

            def cols_pair(bank, key, i, src, ready, base):
                for c in range(2):
                    w = unit((key, 2 * i + c))
                    for k in range(KT):
                        if ready is not None and i == 0 and c == 0:
                            pe.wait_ge(ready, base + k + 1)
                        ins = mm(bank[:, c * T:c * T + T], w[:, k * P:k * P + P], src[:, k], k == 0, k == KT - 1)
                    ins.then_inc(used, 1)

            def rows_part(banks, key, first_unit, n_units, src, total, k0):
                for u in range(n_units):
                    w = unit((key, first_unit + u))
                    for kk in range(2):
                        k = k0 + 2 * u + kk
                        for tt in range(TT):
                            ins = mm(banks[tt][:], src[:, k, tt * P:tt * P + P], w[:, kk * 512:kk * 512 + 512],
                                     k == 0, k == total - 1)
                    ins.then_inc(used, 1)

            def split_cols_pair(bank, key, i, src, ready, base):
                for c in range(2):
                    w_high, w_low = split_unit((key, 2 * i + c))
                    for k in range(KT):
                        if ready is not None and i == 0 and c == 0:
                            pe.wait_ge(ready, base + k + 1)
                        tile = slice(k * P, k * P + P)
                        ins = mm_split(bank[:, c * T:c * T + T], (w_high[:, tile], w_low[:, tile]),
                                       (src[0][:, k], src[1][:, k]), k == 0, k == KT - 1)
                    ins.then_inc(used, 1)

            def split_rows(key, src):
                for i in range(TT):
                    pb.claim(pe, (key, i))
                for u in range(KT // 2):
                    w_high, w_low = split_unit((key, u))
                    for kk in range(2):
                        k = 2 * u + kk
                        for tt in range(TT):
                            tile, columns = slice(tt * P, tt * P + P), slice(kk * 512, kk * 512 + 512)
                            ins = mm_split(pb.bank((key, tt))[:], (src[0][:, k, tile], src[1][:, k, tile]),
                                           (w_high[:, columns], w_low[:, columns]), k == 0, k == KT - 1)
                    ins.then_inc(used, 1)

            def pairs(key, n, src, ready=None, base=0, norm=None):
                for i in range(n):
                    pb.claim(pe, (key, i))
                    pair = cols_pair if UNIT_AT[(key, 0)] < SPLIT else split_cols_pair
                    pair(pb.bank((key, i)), key, i, src, ready, base)
                    if norm is not None and i:
                        norm_sum(norm, i - 1)

            pe.wait_ge(consts, 1)
            norm_sums(0)
            pairs("u", 2, h, h_ready, 0)
            norm_sums(1)
            pairs("q", 2, h)
            pairs("k", 2, h)
            for i in range(TT):
                pb.claim(pe, ("v", i))
            rows_part([pb.bank(("v", i)) for i in range(TT)], "v", 0, 4, h, KT, 0)

            def filler(slot):
                if slot < 4:
                    pb.claim(pe, ("xk", slot))
                    cols_pair(pb.bank(("xk", slot)), "xk", slot, mem, h_ready, 8)
                elif slot < 8:
                    half, part = (slot - 4) // 2, slot % 2
                    if part == 0:
                        for tt in range(TT):
                            pb.claim(pe, ("xv", 2 * half + tt))
                    rows_part([pb.bank(("xv", 2 * half + tt)) for tt in range(TT)], "xv", 4 * half + 2 * part, 2,
                              mem, KT, 4 * part)
                else:
                    pb.claim(pe, ("gate", slot - 8))
                    cols_pair(pb.bank(("gate", slot - 8)), "gate", slot - 8, h, None, 0)

            def inputs_of(j):
                i, q = j // 4, j % 4
                if j == 0:
                    pe.wait_ge(s_par, 16 * 17)
                    pe.wait_ge(*pb.read(("u", 1)))
                xb.claim(pe, ("bu", j))
                for c in range(2):
                    ins = mm(xb.bank(("bu", j))[:, c * T:c * T + T], bbd[32 * q:32 * q + 32, c, i],
                             uT[32 * q:32 * q + 32, i], True, True)
                ins.then_inc(bu_done, 1)

            def outputs_of(j):
                i, q = j // 4, j % 4
                pe.wait_ge(st_ready, j + 1)
                if q == 0 and i:
                    pe.wait_ge(y_freed, i)
                for c in range(2):
                    ins = mm(STAT[32 * q:32 * q + 32, 0:T], cbd[:, c, j], st[:, j % 2, c], c == 0, c == 1)
                ins.then_inc(y_done, 1)

            for r in range(HEADS + 1):
                lo = HD * (r % 2)
                if r < HEADS:
                    inputs_of(2 * r)
                    if r == 0:
                        pe.wait_ge(*pb.read(("v", 1)))
                    xb.claim(pe, ("z", r))
                    z = xb.bank(("z", r))
                    qh, kh = qT[lo:lo + HD, r // 2], kT[lo:lo + HD, r // 2]
                    mm(z[:, 0:T], kh[:, 0:P], qh, True, True)
                    mm(z[:, T:384], kh[:, P:T], qh[:, P:T], True, True).then_inc(z_done, 1)
                if r:
                    outputs_of(2 * r - 2)
                    outputs_of(2 * r - 1)
                if r < HEADS:
                    filler(2 * r)
                if r:
                    xb.claim(pe, ("cum", r - 1))
                    pe.wait_ge(sp_ready, r)
                    z = xb.bank(("cum", r - 1))
                    mm(z[:, 0:T], tri[:], sp[:, 0:T], True, False)
                    mm(z[:, P:T], ones[:], sp[:, T:384], False, True)
                    mm(z[:, T:384], tri[:], sp[:, T:384], True, True).then_inc(cum_done, 1)
                if r < HEADS:
                    inputs_of(2 * r + 1)
                    filler(2 * r + 1)
                if r:
                    hd = r - 1
                    lo = HD * (hd % 2)
                    xb.claim(pe, ("pv", hd))
                    pe.wait_ge(w_ready, r)
                    o = xb.bank(("pv", hd))[lo:lo + HD]
                    mm(o[:, 0:T], v1[:, 0, HD * hd:HD * hd + HD], w1[:, 0:T], True, False)
                    mm(o[:, P:T], v1[:, 1, HD * hd:HD * hd + HD], w1[:, T:384], False, True).then_inc(pv_done, 1)

            def half_depth(bank, key, i, src):
                w = unit((key, i))
                for c in range(2):
                    for k in range(4):
                        ins = mm(bank[:, c * T:c * T + T], w[:, (4 * c + k) * P:(4 * c + k + 1) * P], src[:, k],
                                 k == 0, k == 3)
                ins.then_inc(used, 1)

            pe.wait_ge(y_ready, 1)
            for i in range(2):
                pb.claim(pe, ("glu", i))
                half_depth(pb.bank(("glu", i)), "glu", i, yT)
            pe.wait_ge(*xb.read(("pv", HEADS - 1)))
            for i in range(4):
                pb.claim(pe, ("ba", i))
                half_depth(pb.bank(("ba", i)), "ba", i, oT)
                if i == 0:
                    pe.wait_ge(ossm_ready, 1)
                pb.claim(pe, ("bs", i))
                half_depth(pb.bank(("bs", i)), "bs", i, gt)
            pe.wait_ge(merged_ready, 4)
            pairs("out", 4, merged, norm=2)
            norm_sums(2, 3)

            norm_sums(3)
            pairs("xq", 4, (hh, hl), h_ready, 16)
            pe.wait_ge(*pb.read(("xq", 3)))
            for i in range(8 + 1):
                if i < 8:
                    head, tt = i // 2, i % 2
                    xb.claim(pe, ("sc", i))
                    for k in range(2):
                        ins = mm(xb.bank(("sc", i))[:, 0:T], xqT[:, 2 * head + k, tt * P:tt * P + P], xkT[:, 2 * head + k],
                                 k == 0, k == 1)
                    ins.then_inc(sc_done, 1)
                if i:
                    head, tt = (i - 1) // 2, (i - 1) % 2
                    xb.claim(pe, ("pt", i - 1))
                    pe.wait_ge(prob_ready, i)
                    for m in range(2):
                        ins = pe.transpose(xb.bank(("pt", i - 1))[:, m * P:m * P + P],
                                           prob[:, (i - 1) % 2, m * P:m * P + P], ident[:])
                    ins.then_inc(pt_done, 1)
                    if tt:
                        pb.claim(pe, ("xav", head))
                        pe.wait_ge(*xb.read(("pt", i - 1)))
                        for c in range(2):
                            for m in range(2):
                                ins = mm(pb.bank(("xav", head))[:, c * T:c * T + T],
                                         xv[:, m, (2 * head + c) * P:(2 * head + c + 1) * P], probT[:, head % 2, m],
                                         m == 0, m == 1)
                        ins.then_inc(xo_done, 1)
            pe.wait_ge(*pb.read(("xav", XH - 1)))
            pairs("xo", 4, (yh, yl), norm=4)
            norm_sums(4, 3)

            norm_sums(5)
            for i in range(4):
                pb.claim(pe, ("dn", i))
            for j in range(FT + 2):
                if j < FT:
                    xb.claim(pe, ("up", j))
                    for c, key in enumerate(("fg", "fv")):
                        w_high, w_low = split_unit((key, j))
                        for k in range(KT):
                            if j == 0 and c == 0:
                                pe.wait_ge(h_ready, 24 + k + 1)
                            tile = slice(k * P, k * P + P)
                            ins = mm_split(xb.bank(("up", j))[:, c * T:c * T + T], (w_high[:, tile], w_low[:, tile]),
                                           (hh[:, k], hl[:, k]), k == 0, k == KT - 1)
                        ins.then_inc(used, 1)
                if j >= 2:
                    w_high, w_low = split_unit(("dn", j - 2))
                    pe.wait_ge(hid_ready, j - 1)
                    b = (j - 2) % 3
                    for c in range(KT):
                        tile = slice(c * P, c * P + P)
                        ins = mm_split(pb.bank(("dn", c // 2))[:, (c % 2) * T:(c % 2) * T + T],
                                       (w_high[:, tile], w_low[:, tile]), (yh[:, b], yl[:, b]),
                                       j == 2 and c % 2 == 0, j == FT + 1)
                    ins.then_inc(used, 1)
            norm_sums(6)

            norm_sums(7)
            pe.wait_ge(s_par2, 16 * 5)
            xb.claim(pe, ("if", 0))
            for c in range(2):
                for k in range(KT):
                    if c == 0:
                        pe.wait_ge(h_ready, 32 + k + 1)
                    ins = mm(xb.bank(("if", 0))[0:MH, c * T:c * T + T], w_if[:, k, MH * c:MH * c + MH], h[:, k],
                             k == 0, k == KT - 1)
            ins.then_inc(if_done, 1)
            split_rows("v2", (hh, hl))
            xb.claim(pe, ("gT", 0))
            pe.wait_ge(if_rows, 1)
            for tt in range(TT):
                ins = pe.transpose(xb.bank(("gT", 0))[:, MH * tt:MH * tt + MH], ifr[:, 5, tt * P:tt * P + P],
                                   ident[0:MH, 0:MH])
            ins.then_inc(gt_done, 1)
            pe.wait_ge(qpad, 1)
            pairs("qk2", 4, (hh, hl))
            split_rows("vg", (hh, hl))
            pairs("ug", 2, (hh, hl))
            pairs("o2", 2, (hh, hl))
            pe.wait_ge(em_ready, 1)
            pe.wait_ge(qk_ready, 4)
            for i in range(MH + 1):
                if i < MH:
                    xb.claim(pe, ("rows", i))
                    for c, row in enumerate((6, 7)):
                        ins = mm(xb.bank(("rows", i))[:, c * T:c * T + T], head_sel[:, i], ifr[:, row], True, True)
                    ins.then_inc(rows_done, 1)
                if i:
                    xb.claim(pe, ("num", i - 1))
                    pe.wait_ge(*xb.read(("s2", i - 1)))
                    o = xb.bank(("num", i - 1))
                    for c in range(2):
                        w0 = v2[:, 0, (i - 1) * P:i * P] if c == 0 else ones[:]
                        w1_ = v2[:, 1, (i - 1) * P:i * P] if c == 0 else ones[:]
                        mm(o[:, c * T:c * T + T], w0, st2[:, 0:T], True, False)
                        ins = mm(o[:, c * T + P:c * T + T], w1_, st2[:, T:384], False, True)
                    ins.then_inc(num_done, 1)
                if i < MH:
                    xb.claim(pe, ("s2", i))
                    z = xb.bank(("s2", i))
                    qh, kh = qk2[:, i], qk2[:, MH + i]
                    mm(z[:, 0:T], kh[:, 0:P], qh, True, True)
                    mm(z[:, T:384], kh[:, P:T], qh[:, P:T], True, True).then_inc(s2_done, 1)
            pe.wait_ge(vb_ready, 4)
            for i in range(2):
                xb.claim(pe, ("mix", i))
                for c in range(2):
                    for half in range(2):
                        g = 4 * i + 2 * c + half
                        for nb in range(TT):
                            ins = mm(xb.bank(("mix", i))[64 * half:64 * half + 64, c * T + nb * P:c * T + nb * P + P],
                                     gv[:, nb, 64 * g:64 * g + 64], mixw[:, g], True, True)
                ins.then_inc(mix_done, 1)
            xb.claim(pe, ("hsum", 0))
            pe.wait_ge(hsq, 2)
            o = xb.bank(("hsum", 0))
            for i in range(4):
                for tt in range(TT):
                    mm(o[:, 2 * i + tt:2 * i + tt + 1], sq[:, i, tt * P:tt * P + P], ones[:, 0:1], True, True)
            for i in range(4):
                for tt in range(TT):
                    a = 8 + 4 * i + 2 * tt
                    ins = mm(o[:, a:a + 2], sq[:, 4 + i, tt * P:tt * P + P], half_ones[:], True, True)
            ins.then_inc(hsum, 1)
            pe.wait_ge(hscale, 1)
            for i in range(4):
                xb.claim(pe, ("hspread", i))
                for c in range(2):
                    t_ = 2 * i + c
                    for tt in range(TT):
                        o = xb.bank(("hspread", i))[:, c * T + tt * P:c * T + tt * P + P]
                        if t_ < 4:
                            w = rstd[:, 2 * t_ + tt:2 * t_ + tt + 1].to_broadcast([P, P])
                            ins = mm(o, w, ident[:], True, True)
                        for half in range(2 if t_ >= 4 else 0):
                            a = 8 + 4 * (t_ - 4) + 2 * tt + half
                            ins = mm(o[64 * half:64 * half + 64], rstd[:, a:a + 1].to_broadcast([P, 64]), ident[:],
                                     True, True)
                ins.then_inc(hspread, 1)
            pairs("out2", 4, (yh, yl), op_low, 0, norm=8)

            norm_sums(8, 3)
            pe.wait_ge(h_ready, 48)
            for i in range(4):
                xb.claim(pe, ("tr", i))
                for k in range(4):
                    ins = pe.transpose(xb.bank(("tr", i))[:, k * P:k * P + P],
                                       h[:, 4 * (i % 2) + k, (i // 2) * P:(i // 2) * P + P], ident[:])
                ins.then_inc(tr_done, 1)
            xb.claim(pe, ("lg", 0))
            pe.wait_ge(s_par3, 32)
            for tt in range(TT):
                for k in range(KT):
                    ins = mm(xb.bank(("lg", 0))[:, 64 * tt:64 * tt + 36], h[:, k, tt * P:tt * P + P], w_r[:, k],
                             k == 0, k == KT - 1)
            ins.then_inc(lg_done, 1)
            pe.wait_ge(y_zeroed, 1)
            pe.wait_ge(x_ready, 16)
            for i in range(4):
                mm(psum[i][:], ident[:], zero, True, True)
            xb.claim(pe, ("rank", 0))
            pe.wait_ge(sel_ready, TT)
            o = xb.bank(("rank", 0))
            mm(o[:, 0:NE], before[:], selm[:, 0], True, True)
            mm(o[:, NE:2 * NE], before[:], selm[:, 1], True, False)
            mm(o[:, NE:2 * NE], ones[:], selm[:, 0], False, True)
            mm(o[:, 2 * NE:3 * NE], ones[:], selm[:, 0], True, False)
            mm(o[:, 2 * NE:3 * NE], ones[:], selm[:, 1], False, True).then_inc(rank_done, 1)
            pe.wait_ge(*xb.read(("tr", 3)))
            pe.wait_ge(*xb.read(("rank", 0)))
            pe.wait_ge(rounds_ready, 1)
            n_pairs = pe.value_load(rounds[0:1, 0:1], min_val=1, max_val=MAXR) * PAIRS

            def gather():
                for k in range(KT):
                    c = (k % 4) * 2 * CAP
                    for tt in range(TT):
                        ins = mm(psum[6 + k // 4][:, c:c + 2 * CAP], xtok[:, tt, k * P:k * P + P], gat[:, tt],
                                 tt == 0, tt == 1)
                    if k % 4 == 3:
                        ins.then_inc(gath_done, 1)

            def scatter():
                for k in range(KT):
                    ins = mm(psum[k // 2][:, (k % 2) * T:(k % 2) * T + T], yg[:, k * P:k * P + P], scwT, False, True)
                return ins

            def pair_unit(it, n):
                pe.wait_ge(landed[n % RING], it * (16 * PAIR // RING) + 16 * ((DENSE + n) // RING + 1))
                return ring[:, n % RING]

            half = (slice(0, CAP), slice(CAP, 2 * CAP))
            pe.wait_ge(g_ready, 1)
            gather()
            with pe.Fori(0, n_pairs) as it:
                pe.wait_ge(xg_low, it + 1)
                pe.wait_ge(xg_high, it + 1)
                pe.wait_ge(hT_ready, it + 1)
                pe.wait_ge(scwT_ready, it + 1)
                for k in range(KT):
                    w = [pair_unit(it, 2 * k + e) for e in range(2)]
                    for c in range(2):
                        for e in range(2):
                            ins = mm(psum[4 + c][half[e]], xg[:, k, half[e]], w[e][:, c * FE:c * FE + FE],
                                     k == 0, k == KT - 1)
                            if c:
                                ins.then_inc(used, 1)
                pe.wait_ge(g_ready, it + 2)
                pe.wait_ge(yg_low, it + 1)
                pe.wait_ge(yg_high, it + 1)
                gather()
                scatter()
                pe.wait_ge(hx_ready, it + 2)
                for f in range(FE // P):
                    ins = pe.transpose(psum[4][:, f * P:f * P + P], hx[:, f * P:f * P + P], ident[:])
                ins.then_inc(hT_done, 1)
                pe.wait_ge(scw_ready, it + 1)
                for tt in range(TT):
                    ins = pe.transpose(psum[5][:, tt * P:tt * P + P], scw[:, tt], ident[:])
                ins.then_inc(scwT_done, 1)
                pe.wait_ge(xg_low, it + 2)
                pe.wait_ge(xg_high, it + 2)
                pe.wait_ge(hT_ready, it + 2)
                for f in range(FE // P):
                    w = [pair_unit(it, 2 * KT + 2 * f + e) for e in range(2)]
                    for c in range(2):
                        for e in range(2):
                            ins = mm(psum[6 + c][half[e]], hT[:, f, half[e]], w[e][:, c * 512:c * 512 + 512],
                                     f == 0, f == FE // P - 1)
                            if c:
                                ins.then_inc(used, 1)
            pe.wait_ge(yg_low, n_pairs + 1)
            pe.wait_ge(yg_high, n_pairs + 1)
            pe.wait_ge(scwT_ready, n_pairs + 1)
            scatter().then_inc(moe_done, 1)
            norm_sums(9)


def tiles_of(w):
    k, n = w.shape
    return w.reshape(k // P, P, n // P, P).transpose(2, 1, 0, 3).reshape(n // P, P, k)


def half_tiles_of(w):
    t = tiles_of(w)
    return t.reshape(-1, 2, P, 512).transpose(0, 2, 1, 3).reshape(-1, P, UNIT)


def row_tiles_of(w):
    k, n = w.shape
    return w.reshape(k // 256, 2, P, n // 512, 512).transpose(3, 0, 2, 1, 4).reshape(-1, P, UNIT)


def lay_out(a):
    win, win2 = a["w_in"][0], a["w_in_2"][0]
    parts = {
        "q": tiles_of(win[:, 0:512]), "k": tiles_of(win[:, 512:1024]), "v": row_tiles_of(win[:, 1024:1536]),
        "u": tiles_of(win[:, 1536:2048]), "gate": tiles_of(win[:, 2048:4096]),
        "xk": tiles_of(a["xa_wk"][0]), "xv": row_tiles_of(a["xa_wv"][0]), "xq": tiles_of(a["xa_wq"][0]),
        "xo": tiles_of(a["xa_wo"][0]), "glu": half_tiles_of(a["ssm_w_glu"][0]),
        "ba": half_tiles_of(a["w_branch_attn"][0]), "bs": half_tiles_of(a["w_branch_ssm"][0]),
        "out": tiles_of(a["w_out"][0]), "fg": tiles_of(a["ffn_w_up"][0][:, :FT * P]),
        "fv": tiles_of(a["ffn_w_up"][0][:, FT * P:]), "dn": a["ffn_w_down"][0].reshape(FT, P, D),
        "qk2": tiles_of(win2[:, 0:1024]), "v2": row_tiles_of(win2[:, 1024:1536]), "o2": tiles_of(win2[:, 1536:2048]),
        "ug": tiles_of(win2[:, 2056:2568]), "vg": row_tiles_of(win2[:, 2568:3080]), "out2": tiles_of(a["w_out_2"][0]),
    }
    stream = np.empty((DENSE + NE * PER_EXPERT, P, UNIT), np.float32)
    for n, (key, i) in enumerate(UNITS):
        stream[n] = parts[key][i]
    for e in range(NE):
        n = DENSE + (e // 2) * PAIR + e % 2
        stream[n:n + 2 * KT:2, :, :FE] = a["w_gate_2"][0, e].reshape(KT, P, FE)
        stream[n:n + 2 * KT:2, :, FE:] = a["w_up_2"][0, e].reshape(KT, P, FE)
        stream[n + 2 * KT:n + PAIR:2] = a["w_down_2"][0, e].reshape(FE // P, P, D)

    def column(v):
        return v.reshape(-1, P).T

    vectors = {
        "mix_pre": a["norm_mix_pre"], "mix_post": a["norm_mix_post"], "xa_pre": a["norm_xa_pre"],
        "xa_post": a["norm_xa_post"], "mem": a["norm_mem"], "ffn_pre": a["norm_ffn_pre"],
        "ffn_post": a["norm_ffn_post"], "norm1": a["norm1_g_2"], "norm2": a["norm2_g_2"], "final": a["final_g_2"],
        "b_gate": a["b_gate"], "d": a["ssm_d"], "b_glu": a["ssm_b_glu"], "conv0": a["ffn_conv_w"][0, 0],
        "conv1": a["ffn_conv_w"][0, 1], "conv2": a["ffn_conv_w"][0, 2], "conv_b": a["ffn_conv_b"],
        "qk0": a["conv_qk_2"][0, 0], "qk1": a["conv_qk_2"][0, 1], "qk2": a["conv_qk_2"][0, 2],
        "qk3": a["conv_qk_2"][0, 3], "g_mlstm": a["g_mlstm_out_2"], "g_v": a["g_gmlp_v_2"],
        "g_gmlp": a["g_gmlp_out_2"],
    }

    def states(v):
        return v.reshape(STILES, P).T

    log_dt = np.broadcast_to(a["ssm_log_dt"][0][:, None], (2 * STILES, 64))
    b = np.stack([a["ssm_b_re"][0], a["ssm_b_im"][0]])
    c = np.stack([a["ssm_c_re"][0], a["ssm_c_im"][0]])
    return {
        "stream": stream,
        "xT": a["x"][0].T.reshape(KT, P, T).transpose(1, 0, 2),
        "memT": a["mem"][0].T.reshape(KT, P, T).transpose(1, 0, 2),
        "cols": np.concatenate([column(vectors[name]) for name in COLS], axis=1),
        "ssm_a": np.stack([states(a["ssm_a_re"][0]), states(a["ssm_a_im"][0]), states(log_dt)], axis=1),
        "ssm_b": b.reshape(2, 4, 8, 64, 16).transpose(2, 4, 0, 1, 3).reshape(P, 2, 4, 64),
        "ssm_c": c.reshape(2, STILES, 2, 16, 64).transpose(2, 4, 0, 1, 3).reshape(P, 2, STILES, 16),
        "mixw": a["w_spatial_2"][0].transpose(2, 0, 1),
        "bsp": a["b_spatial_2"][0],
        "w_if": win2[:, 2048:2056].reshape(KT, P, 8).transpose(1, 0, 2),
        "b_if": np.stack([a["b_igate_2"][0], a["b_fgate_2"][0]], axis=1),
        "w_r": np.concatenate([a["w_router_group_2"][0], a["w_router_expert_2"][0]], axis=1
                              ).reshape(KT, P, 36).transpose(1, 0, 2),
        "b_r": np.concatenate([a["b_router_group_2"][0], a["b_router_expert_2"][0]]),
    }


def kernel(**inputs):
    import concourse.bacc as bacc
    from concourse.bass_utils import run_bass_kernel_spmd

    laid = {k: np.ascontiguousarray(v) for k, v in lay_out({k: np.asarray(v) for k, v in inputs.items()}).items()}
    nc = bacc.Bacc("TRN2", target_bir_lowering=False, num_devices=1)
    dram = {k: nc.dram_tensor(f"in_{k}", v.shape, mybir.dt.from_np(v.dtype), kind="ExternalInput").ap()
            for k, v in laid.items()}
    out = nc.dram_tensor("out_y", (P, KT, T), F32, kind="ExternalOutput").ap()
    program(nc, dram, out)
    got = run_bass_kernel_spmd(nc, [{f"in_{k}": v for k, v in laid.items()}], core_ids=[0]).results[0]["out_y"]
    return got.reshape(P, KT, T).transpose(2, 1, 0).reshape(1, T, D)
```

```python
from contextlib import ExitStack

import numpy as np

import concourse.bass as bass
from concourse import mybir

ALU = mybir.AluOpType
ACT = mybir.ActivationFunctionType
F32 = mybir.dt.float32
I32 = mybir.dt.int32
F32R = mybir.dt.float32r
AX = mybir.AxisListType

P = 128
D = 1024
T = 256
KT = D // P
TT = T // P
RING = 6
SPLIT_RING = 4
UNIT = 8 * P
EPS = 1e-6
HEADS = 8
HD = 64
STILES = 16
XH = 4
FT = 22
MH = 4
GG = 8
NE = 32
EG = 8
NG = 4
CAP = 64
MAXR = T // CAP
PAIRS = NE // 2
FE = 512
TWO_PI_HI = 6.28125
TWO_PI_LO = 2 * np.pi - 6.28125
ROUND = 12582912.0
GELU_C = 0.044715
GELU_K = float(np.sqrt(2 / np.pi))
RSQRT_SEED = float(0x5F3759DF + 0x40000000 - 0x00400000)

UNITS = []
UNITS += [("u", i) for i in range(4)] + [("q", i) for i in range(4)] + [("k", i) for i in range(4)]
UNITS += [("v", i) for i in range(4)] + [("xk", i) for i in range(8)] + [("xv", i) for i in range(4)]
UNITS += [("gate", i) for i in range(16)] + [("glu", i) for i in range(2)]
for i in range(4):
    UNITS += [("ba", i), ("bs", i)]
UNITS += [("out", i) for i in range(8)] + [("xv", i) for i in range(4, 8)]
UNITS += [("xq", i) for i in range(8)] + [("xo", i) for i in range(8)]
for i in range(FT + 2):
    if i < FT:
        UNITS += [("fg", i), ("fv", i)]
    if i >= 2:
        UNITS += [("dn", i - 2)]
UNITS += [("v2", i) for i in range(4)] + [("qk2", i) for i in range(8)] + [("o2", i) for i in range(4)]
UNITS += [("vg", i) for i in range(4)] + [("ug", i) for i in range(4)] + [("out2", i) for i in range(8)]
LEFT = [("xk", i) for i in range(8)] + [("xv", i) for i in range(4)] + [("gate", i) for i in range(16)]
FILLERS = []
for width in (2, 2, 1, 2, 1, 2, 2, 1, 2, 1, 2, 2, 1, 2, 1, 2, 2):
    FILLERS.append(LEFT[:width])
    LEFT = LEFT[width:]
assert not LEFT
QUERIES_AT = {0: (2, 3), 1: (4,), 2: (5,), 3: (6,), 4: (7,)}
UNIT_AT = {key: n for n, key in enumerate(UNITS)}
DENSE = len(UNITS)
SPLITS = [key for key in UNITS if key[0] not in ("xk", "xv", "glu", "ba", "bs")]
SPLIT_AT = {key: m for m, key in enumerate(SPLITS)}
PER_EXPERT = 12
PAIR = 2 * PER_EXPERT
assert DENSE % RING == 0

COLS = {}
for name, width in (("mix_pre", 8), ("mix_post", 8), ("xa_pre", 8), ("xa_post", 8), ("mem", 8), ("ffn_pre", 8),
                    ("ffn_post", 8), ("norm1", 8), ("norm2", 8), ("final", 8), ("b_gate", 16), ("d", 4),
                    ("b_glu", 4), ("conv0", 44), ("conv1", 44), ("conv2", 44), ("conv_b", 44), ("qk0", 8),
                    ("qk1", 8), ("qk2", 8), ("qk3", 8), ("g_mlstm", 4), ("g_v", 4), ("g_gmlp", 4)):
    COLS[name] = sum(w for _, w in COLS.values()), width
NCOLS = sum(w for _, w in COLS.values())

NORMS = ["mix_pre", "mem", "mix_post", "xa_pre", "xa_post", "ffn_pre", "ffn_post", "norm1", "norm2", "final"]


class BankRing:

    def __init__(self, banks, plan, freed):
        self.banks, self.plan, self.freed = banks, plan, freed
        self.at = {key: n for n, (key, _) in enumerate(plan)}

    def bank(self, key):
        return self.banks[self.at[key] % len(self.banks)]

    def claim(self, pe, key):
        before = self.at[key] - len(self.banks)
        if before >= 0:
            pe.wait_ge(*self.read(self.plan[before][0]))

    def read(self, key):
        reader = self.plan[self.at[key]][1]
        semaphore, start, step = self.freed[reader]
        return semaphore, start + step * sum(r == reader for _, r in self.plan[:self.at[key] + 1])


def program(nc, dram, out):
    with ExitStack() as ctx:
        def sb(name, shape, dt=F32):
            return ctx.enter_context(nc.sbuf_tensor(name, shape, dt))

        def sem(name):
            return ctx.enter_context(nc.semaphore(name))

        ring_at = nc.sbuf_base + -nc.sbuf_base % 32
        ring = sb("ring", [P, RING, UNIT])
        parts_at = nc.sbuf_base + -nc.sbuf_base % 32
        parts = sb("parts", [P, SPLIT_RING * UNIT + KT * T])
        x = sb("x", [P, KT, T])
        h_at = nc.sbuf_base + -nc.sbuf_base % 32
        h = sb("h", [P, KT, T])
        sq = sb("sq", [P, KT, T])
        ident = sb("ident", [P, P])
        ones = sb("ones", [P, P])
        tri = sb("tri", [P, P])
        before = sb("before", [P, P])
        mask_lt = sb("mask_lt", [P, 3, P])
        mask_le = sb("mask_le", [P, 3, P])
        half_ones = sb("half_ones", [P, 2])
        head_sel = sb("head_sel", [MH, MH, P])
        slots = sb("slots", [P, CAP])
        cols = sb("cols", [P, NCOLS])
        hb = sb("hb", [P, 24])
        ms = sb("ms", [P, 24])
        ri = sb("ri", [P, 24], I32)
        rstd = sb("rstd", [P, 24])
        rt = sb("rt", [P, 24])
        rb = sb("rb", [P, T])
        arena_at = nc.sbuf_base + -nc.sbuf_base % 32
        arena = sb("arena", [P, 31136])
        bbd = sb("bbd", [P, 2, 4, P])

        def view(start, *shape, parts=P):
            n = int(np.prod(shape))
            v = arena[0:parts, start:start + n]
            if len(shape) == 1:
                return v
            names = "abcd"[:len(shape)]
            sizes = {names[i]: shape[i] for i in range(len(shape))}
            return v.rearrange(f"p ({' '.join(names)}) -> p {' '.join(names)}", **sizes)

        def rounded(name, start, shape, base=None):
            return nc.alloc_sbuf_tensor_at(name, shape, F32R, offset=(base or arena_at) + 4 * start)

        h0h, h0l = rounded("h0_high", SPLIT_RING * UNIT, [P, KT, T], parts_at), rounded("h0_low", 0, [P, KT, T], h_at)
        hh, hl = rounded("h_high", 8192, [P, KT, T]), rounded("h_low", 10240, [P, KT, T])
        yh, yl = rounded("y_high", 12288, [P, KT, T]), rounded("y_low", 14336, [P, KT, T])
        wh = rounded("w_high", 0, [P, SPLIT_RING, UNIT], parts_at)
        wl = rounded("w_low", 0, [P, RING, UNIT], ring_at)

        rot = view(0, 2, STILES, T)
        uT, qT, kT = view(8192, 4, T), view(9216, 4, T), view(10240, 4, T)
        v1 = view(11264, TT, 512)
        gates = view(12288, 16, T)
        xkT, xv = view(16384, KT, T), view(18432, TT, D)
        oT = view(20480, 4, T)
        yT = view(21504, 4, T)
        m1, m2, vr, wr = view(22528, 2, T), view(23040, 2, T), view(23552, 2, T), view(24064, 2, T)
        st = view(24576, 2, 2, T)
        zm, az, sp, w1 = view(25600, 384), view(25984, 384), view(26368, 384), view(26752, 384)
        zm = (zm, view(30752, 384))
        gt = view(22528, 4, T)
        cbd = view(27136, 2, STILES, 32)
        craw = view(24576, 2, STILES, 16)
        ta, tb = view(16384, STILES * 128), view(18432, STILES * 128)
        mem = view(28160, KT, T)
        powers = view(30208, 2, 2, STILES)
        ptmp = view(30272, 6, STILES)
        ssm = view(30368, 24, STILES)
        merged = view(0, KT, T)
        mg = view(2048, 2, 512)
        xqT = view(3072, KT, T)
        prob = view(5120, 2, T)
        probT = view(5632, 2, TT, T)
        post = view(22528, KT, T)
        sm = view(8000, 4, 8)
        up = view(0, 3, 2, T + 4)
        acc = view(1560, 3, 2, T)
        fs = view(3096, 3, 2, T)
        hid32 = view(4632, 3, T)
        v2 = view(0, TT, 512)
        qk2 = view(1024, 8, T)
        qraw = view(3072, 2, 2, T + 4)
        qs = view(4112, 2, 2, T)
        gv = view(5136, TT, 512)
        gvs = view(6160, TT, 512)
        ugs = view(6160, 4, T)
        gm = view(4112, 4, T)
        decay = view(7184, 384)
        st2 = view(7568, 384)
        gT = view(7952, TT, MH)
        b_if = view(7960, 2, parts=MH)
        vsum = view(7964, 2)
        ug = view(16384, 4, T)
        so = view(17408, 4, T)
        hm = view(18432, 4, T)
        qt = view(18432, 2, 2, T)
        mixw = view(19456, GG, P)
        bsp = view(20480, 4, P)
        ifr = view(20992, 10, T, parts=MH)
        emb = view(23552, T)
        hden = view(23808, T)
        w_if = view(24064, KT, 8)
        xtok = view(0, TT, D)
        w_r = view(30720, KT, 36)
        b_r = view(31008, 36)
        lg = view(2400, TT, 36)
        rsm = view(2480, TT, 16)
        gsel = view(2512, TT, NG)
        lsel = view(2520, 4, TT, EG)
        lmask = view(2584, TT, NE)
        lgrp = view(7712, TT, NG, EG)
        sel1, sel2 = view(2648, TT, EG), view(2664, TT, EG)
        first = view(2680, EG)
        selw = view(2688, TT, NE)
        selm = view(2752, TT, NE)
        rank = view(2816, TT, MAXR * NE + 4)
        wall = view(3080, TT, MAXR * NE + 4)
        gat = view(3344, TT, 2 * CAP)
        scw = view(3600, TT, 2 * CAP)
        scwT = view(3856, T)
        xg = view(4112, KT, 2 * CAP)
        gate_th = view(5136, FE)
        act_ = view(5648, FE)
        hx = view(6160, FE)
        hT = view(6672, FE // P, 2 * CAP)
        yg = view(12288, D)
        cnt = view(7696, 4)
        zero = view(7184, 512)
        res = view(13312, KT, T)
        pair_slot = [ring[:, n] for n in range(RING)]
        pair_slot += [view(start + UNIT * n, UNIT) for start, count in ((8192, 4), (24576, 6), (16384, 8))
                      for n in range(count)]
        rounds = sb("rounds", [1, 1], I32)

        psum = [ctx.enter_context(nc.psum_tensor(f"psum{i}", [P, 512], F32)) for i in range(8)]
        STAT = psum[7]

        landed = [sem(f"landed{i}") for i in range(RING)]
        landed += [sem(f"landed{i}") for i in range(RING, PAIR)]
        used = sem("used")
        s_x = sem("x_lower_in"), sem("x_upper_in")
        s_mem, s_cols, s_par = sem("mem_in"), sem("vectors_in"), sem("ssm_matrices_in")
        s_par2, s_par3 = sem("mixer2_params_in"), sem("router_params_in")
        s_out = sem("out_stored")
        consts = sem("consts_ready")
        hi_ready, lo_ready = sem("weights_high"), sem("weights_low")
        op32, op_high, op_low = sem("operand_ready"), sem("operand_high"), sem("operand_low")
        squares, sums, scales, spread = sem("squares_ready"), sem("sums_ready"), sem("scales_ready"), sem("spread_ready")
        scaled, rb_ready = sem("post_scaled"), sem("spread_copied")
        h_ready, x_ready = sem("h_ready"), sem("x_ready")
        act_chain, dve_chain, pool_chain = sem("act_chain"), sem("dve_chain"), sem("pool_chain")
        p_freed = {"act": sem("pbank_freed_act"), "dve": sem("pbank_freed_dve")}
        x_freed = {"act": sem("xbank_freed_act"), "dve": sem("xbank_freed_dve")}
        dve_halves = sem("bias_halves")
        ssm_args, ssm_trig, ssm_ready = sem("ssm_args"), sem("ssm_trig"), sem("ssm_ready")
        bu_done, st_ready, y_done, y_freed = sem("bu_done"), sem("states_ready"), sem("y_done"), sem("y_freed")
        z_done, sp_ln, sp_ready = sem("z_done"), sem("softplus_ln"), sem("softplus_ready")
        cum_done, w_exp, w_ready = sem("cum_done"), sem("w_exp"), sem("w_ready")
        pv_done = sem("pv_done")
        gelu_sq, gelu_in, gelu_th = sem("gelu_squares"), sem("gelu_inner"), sem("gelu_tanh")
        y_ready, ossm_ready = sem("y_ready"), sem("ossm_ready")
        gates_th, merged_ready = sem("gates_tanh"), sem("merged_ready")
        sc_done, max_ready, prob_ready = sem("scores_done"), sem("max_ready"), sem("prob_ready")
        pt_done, xo_done = sem("probT_done"), sem("xo_done")
        xo_high, bbd_zeroed = sem("attended_high"), sem("ssm_matrices_zeroed")
        merged_high, merged_low = sem("merged_high"), sem("merged_low")
        conv_g, hid_ready = sem("conv_ready"), sem("hid_ready")
        if_done, if_ready, if_ln, if_rows, em_ready = (sem("if_done"), sem("if_ready"), sem("if_ln"),
                                                       sem("if_rows"), sem("em_ready"))
        gt_done, qpad = sem("gT_done"), sem("qk_padded")
        qk_conv, qk_th, qk_ready = sem("qk_conv"), sem("qk_tanh"), sem("qk_ready")
        rows_done, dec_in, dec_exp, s2_done = (sem("rows_done"), sem("decay_in"), sem("decay_exp"),
                                               sem("scores2_done"))
        num_done, hm_ready, hsq = sem("num_done"), sem("hm_ready"), sem("head_squares")
        vsq, vb_ready, mix_done, gm_ready = sem("v_squares"), sem("vb_ready"), sem("mix_done"), sem("gm_ready")
        hsum, hscale, hspread = sem("head_sums"), sem("head_scales"), sem("head_spread")
        tr_done, lg_done = sem("tok_turned"), sem("logits_done")
        rt_max, rt_exp, sel_ready, rank_done = (sem("router_max"), sem("router_exp"), sem("sel_ready"),
                                                sem("rank_done"))
        rounds_ready, y_zeroed = sem("rounds_ready"), sem("y_zeroed")
        g_ready, gath_done, xg_low, xg_high = sem("gather_ready"), sem("gather_done"), sem("xg_low"), sem("xg_high")
        hid_th, hx_ready, hT_done, hT_ready = sem("expert_tanh"), sem("hx_ready"), sem("hT_done"), sem("hT_ready")
        scw_ready, scwT_done, scwT_ready = sem("scatter_ready"), sem("scatterT_done"), sem("scatterT_ready")
        yg_low, yg_high = sem("yg_low"), sem("yg_high")
        silu_done = sem("silu_done")
        moe_done, res_ready = sem("moe_done"), sem("result_ready")

        pplan = [(("u", i), "act") for i in range(2)] + [(("q", i), "act") for i in range(2)]
        pplan += [(("k", i), "act") for i in range(2)] + [(("v", i), "act") for i in range(2)]
        pplan += [(("xk", i), "act") for i in range(4)] + [(("xv", i), "act") for i in range(2)]
        pplan += [(("gate", i), "act") for i in range(8)] + [(("glu", i), "act") for i in range(2)]
        for i in range(4):
            pplan += [(("ba", i), "dve"), (("bs", i), "dve")]
        pplan += [(("out", i), "act") for i in range(4)] + [(("xv", i), "act") for i in range(2, 4)]
        pplan += [(("xq", i), "act") for i in range(3)] + [(("xav", 0), "dve"), (("xq", 3), "act")]
        pplan += [(("xav", i), "dve") for i in range(1, XH)]
        pplan += [(("xo", i), "act") for i in range(4)] + [(("dn", i), "act") for i in range(4)]
        pplan += [(("v2", i), "act") for i in range(2)] + [(("qk2", i), "act") for i in range(4)]
        pplan += [(("o2", i), "act") for i in range(2)] + [(("vg", i), "act") for i in range(2)]
        pplan += [(("ug", i), "act") for i in range(2)] + [(("out2", i), "dve") for i in range(4)]
        pb = BankRing(psum[0:4], pplan, {who: (s, 0, 1) for who, s in p_freed.items()})

        xplan = []
        for r in range(HEADS + 1):
            if r < HEADS:
                xplan += [(("bu", 2 * r), "dve"), (("z", r), "dve")]
            if r >= 1:
                xplan += [(("cum", r - 1), "dve")]
            if r < HEADS:
                xplan += [(("bu", 2 * r + 1), "dve")]
            if r >= 1:
                xplan += [(("pv", r - 1), "act")]
        for i in range(8 + 1):
            if i < 8:
                xplan += [(("sc", i), "act")]
            if i >= 1:
                xplan += [(("pt", i - 1), "act")]
        xplan += [(("up", i), "act") for i in range(FT)]
        xplan += [(("if", 0), "dve"), (("gT", 0), "act")]
        for i in range(MH + 1):
            if i < MH:
                xplan += [(("rows", i), "act")]
            if i >= 1:
                xplan += [(("num", i - 1), "dve")]
            if i < MH:
                xplan += [(("s2", i), "dve")]
        xplan += [(("mix", i), "dve") for i in range(2)] + [(("hsum", 0), "dve")]
        xplan += [(("hspread", i), "op32") for i in range(4)]
        xplan += [(("lg", 0), "dve")] + [(("tr", i), "act") for i in range(4)] + [(("rank", 0), "dve")]
        xb = BankRing(psum[4:7], xplan, {"act": (x_freed["act"], 0, 1), "dve": (x_freed["dve"], 0, 1),
                                         "op32": (op32, 4 * KT, 2)})

        def col(name, i=0):
            start = COLS[name][0] + i
            return cols[:, start:start + 1]

        block = ctx.enter_context(nc.Block())

        @block.sync
        def _(sp):
            for half in range(2):
                some = slice(half * KT // 2, (half + 1) * KT // 2)
                sp.dma_start(x[:, some], dram["xT"][:, some]).then_inc(s_x[half], 16)
            for n in range(RING):
                sp.dma_start(ring[:, n], dram["stream"][n]).then_inc(landed[n], 16)
            sp.wait_ge(bbd_zeroed, 1)
            for g in range(8):
                for c in range(2):
                    sp.dma_start(bbd[16 * g:16 * g + 16, c, :, (g % 2) * 64:(g % 2) * 64 + 64],
                                 dram["ssm_b"][16 * g:16 * g + 16, c]).then_inc(s_par, 16)
            sp.dma_start(craw[:], dram["ssm_c"]).then_inc(s_par, 16)
            stream = dram["stream"]
            with sp.Fori(1, DENSE // RING) as i:
                for s in range(RING):
                    sp.wait_ge(used, RING * i + (s + 1 - RING))
                    sp.dma_start(ring[:, s], stream[bass.ds(RING * i + s, 1)].rearrange("a p n -> p (a n)")
                                 ).then_inc(landed[s], 16)
            sp.wait_ge(op_low, KT)
            for s in range(RING, PAIR):
                sp.dma_start(pair_slot[s], stream[DENSE + s]).then_inc(landed[s], 16)
            for s in range(RING):
                sp.wait_ge(used, DENSE - RING + s + 1)
                sp.dma_start(pair_slot[s], stream[DENSE + s]).then_inc(landed[s], 16)
            with sp.Fori(1, PAIRS) as i:
                for s in range(PAIR):
                    sp.wait_ge(used, PAIR * i + (DENSE + s + 1 - PAIR))
                    sp.dma_start(pair_slot[s], stream[bass.ds(PAIR * i + (DENSE + s), 1)].rearrange(
                        "a p n -> p (a n)")).then_inc(landed[s], 16)
            sp.wait_ge(rounds_ready, 1)
            n_rounds = sp.value_load(rounds[0:1, 0:1], min_val=1, max_val=MAXR)
            with sp.If(n_rounds > 1):
                with sp.Fori(1, n_rounds) as r:
                    with sp.Fori(0, PAIRS) as i:
                        for s in range(PAIR):
                            sp.wait_ge(used, r * (NE * PER_EXPERT) + PAIR * i + (DENSE + s + 1 - PAIR))
                            sp.dma_start(pair_slot[s], stream[bass.ds(PAIR * i + (DENSE + s), 1)].rearrange(
                                "a p n -> p (a n)")).then_inc(landed[s], 16)
            for half in range(2):
                some = slice(half * KT // 2, (half + 1) * KT // 2)
                sp.wait_ge(res_ready, (half + 1) * KT // 2)
                sp.dma_start(out[:, some], res[:, some]).then_inc(s_out, 16)
            sp.wait_ge(s_out, 32)

        @block.gpsimd
        def _(pool):
            n = [0]

            def link(ins):
                n[0] += 1
                ins.then_inc(pool_chain, 1)
                pool.wait_ge(pool_chain, n[0])

            link(pool.memset(ones[:], 1.0))
            pool.affine_select(out=ident[:], in_=ones[:], compare_op=ALU.is_equal, fill=0.0, base=0,
                               pattern=[[-1, P]], channel_multiplier=1).then_inc(consts, 1)
            pool.dma_start(mem, dram["memT"]).then_inc(s_mem, 16)
            pool.memset(bbd[:], 0.0).then_inc(bbd_zeroed, 1)
            link(pool.memset(mask_lt[:], 1.0))
            link(pool.memset(mask_le[:], 1.0))
            link(pool.memset(head_sel[:], 1.0))
            link(pool.memset(half_ones[:], 1.0))
            link(pool.affine_select(out=tri[:], in_=ones[:], compare_op=ALU.is_ge, fill=0.0, base=0,
                                    pattern=[[-1, P]], channel_multiplier=1))
            link(pool.affine_select(out=before[:], in_=ones[:], compare_op=ALU.is_gt, fill=0.0, base=0,
                                    pattern=[[1, P]], channel_multiplier=-1))
            for b in (0, 2):
                link(pool.affine_select(out=mask_lt[:, b], in_=mask_lt[:, b], compare_op=ALU.is_gt, fill=0.0,
                                        base=0, pattern=[[1, P]], channel_multiplier=-1))
                link(pool.affine_select(out=mask_le[:, b], in_=mask_le[:, b], compare_op=ALU.is_ge, fill=0.0,
                                        base=0, pattern=[[1, P]], channel_multiplier=-1))
            link(pool.affine_select(out=head_sel[:], in_=head_sel[:], compare_op=ALU.is_equal, fill=0.0, base=0,
                                    pattern=[[-1, MH], [0, P]], channel_multiplier=1))
            link(pool.affine_select(out=half_ones[:, 0:1], in_=half_ones[:, 0:1], compare_op=ALU.is_gt, fill=0.0,
                                    base=64, pattern=[[0, 1]], channel_multiplier=-1))
            link(pool.affine_select(out=half_ones[:, 1:2], in_=half_ones[:, 1:2], compare_op=ALU.is_ge, fill=0.0,
                                    base=-64, pattern=[[0, 1]], channel_multiplier=1))
            link(pool.memset(cbd[:], 0.0))
            pool.iota(slots[:], pattern=[[1, CAP]], base=0, channel_multiplier=0,
                      allow_small_or_imprecise_dtypes=True).then_inc(consts, 1)

            def weights_low(first, end):
                for m in range(first, end):
                    n_ = UNIT_AT[SPLITS[m]]
                    pool.wait_ge(hi_ready, m + 1)
                    pool.tensor_tensor(wl[:, n_ % RING], ring[:, n_ % RING],
                                       wh[:, m % SPLIT_RING].bitcast(F32), ALU.subtract).then_inc(lo_ready, 1)

            weights_low(0, SPLIT_AT[("v2", 0)])
            pool.wait_ge(used, UNIT_AT["dn", FT - 1] + 1)
            pool.wait_ge(x_ready, 12)
            pool.dma_start(mixw, dram["mixw"]).then_inc(s_par2, 16)
            for g in range(2):
                pool.dma_start(bsp[64 * g:64 * g + 64], bass.AP(
                    tensor=dram["bsp"].tensor, offset=g * P, ap=[[0, 64], [2 * P, 4], [1, P]])).then_inc(s_par2, 16)
            pool.dma_start(w_if, dram["w_if"]).then_inc(s_par2, 16)
            pool.dma_start(b_if, dram["b_if"]).then_inc(s_par2, 16)
            pool.dma_start(w_r, dram["w_r"]).then_inc(s_par3, 16)
            pool.dma_start(b_r, bass.AP(tensor=dram["b_r"].tensor, offset=0, ap=[[0, P], [1, 36]])
                           ).then_inc(s_par3, 16)
            weights_low(SPLIT_AT[("v2", 0)], len(SPLITS))

        @block.scalar
        def _(act):
            n = [0]

            def link(ins):
                n[0] += 1
                ins.then_inc(act_chain, 1)
                act.wait_ge(act_chain, n[0])

            def square_input(norm, src, ready=None):
                if norm:
                    act.wait_ge(sums, norm)
                for i in range(4):
                    if ready is not None:
                        act.wait_ge(x_ready, ready + i + 1)
                    act.activation(sq[:, 2 * i:2 * i + 2], src[:, 2 * i:2 * i + 2], ACT.Square).then_inc(squares, 1)

            def square_banks(norm, key, unit):
                act.wait_ge(sums, norm)
                def squares_of(i):
                    unit_used(unit(i))
                    act.activation(two(sq, i), pb.bank((key, i))[:], ACT.Square).then_inc(squares, 1)

                def gained(i):
                    for c in range(2):
                        ins = act.mul(post[:, 2 * i + c], pb.bank((key, i))[:, c * T:c * T + T],
                                      col(NORMS[norm], 2 * i + c))
                    ins.then_inc(p_freed["act"], 1)

                together = unit(0) == unit(3)
                for i in range(4):
                    squares_of(i)
                    if not together:
                        gained(i)
                for i in range(4 if together else 0):
                    gained(i)
                weights_high(UNIT_AT[unit(3)] + 1 + SPLIT_RING)
                act.wait_ge(spread, norm + 1)
                act.copy(rb[:], STAT[:, T:2 * T]).then_inc(rb_ready, 1)

            def evict(key, unit, dst, scale=None):
                unit_used(unit)
                if scale is None:
                    act.copy(dst, pb.bank(key)[:]).then_inc(p_freed["act"], 1)
                else:
                    act.mul(dst, pb.bank(key)[:], scale).then_inc(p_freed["act"], 1)
                weights_high(UNIT_AT[unit] + 1 + SPLIT_RING)

            def two(v, i):
                return v[:, 2 * i:2 * i + 2].rearrange("p a t -> p (a t)")

            split = [0]

            def weights_high(end):
                while split[0] < len(SPLITS) and UNIT_AT[SPLITS[split[0]]] < end:
                    m, n_ = split[0], UNIT_AT[SPLITS[split[0]]]
                    act.wait_ge(landed[n_ % RING], 16 * (n_ // RING + 1))
                    if m >= SPLIT_RING:
                        act.wait_ge(used, UNIT_AT[SPLITS[m - SPLIT_RING]] + 1)
                    act.copy(wh[:, m % SPLIT_RING], ring[:, n_ % RING]).then_inc(hi_ready, 1)
                    split[0] += 1

            def unit_used(key):
                weights_high(UNIT_AT[key] + SPLIT_RING)
                act.wait_ge(used, UNIT_AT[key] + 1)

            highs = [0]

            def operand_high(dst, src, n_):
                for k in range(n_):
                    highs[0] += 1
                    act.wait_ge(op32, highs[0])
                    act.copy(dst[:, k], src[:, k]).then_inc(op_high, 1)

            act.dma_start(cols[:], dram["cols"]).then_inc(s_cols, 16)
            act.dma_start(ssm[:, 0:3], dram["ssm_a"]).then_inc(s_cols, 16)
            for i in range(4):
                act.wait_ge(s_x[i // 2], 16)
                act.activation(sq[:, 2 * i:2 * i + 2], x[:, 2 * i:2 * i + 2], ACT.Square).then_inc(squares, 1)
            act.wait_ge(s_cols, 32)
            act.activation(ssm[:, 3], ssm[:, 2], ACT.Exp).then_inc(ssm_trig, 1)
            weights_high(SPLIT_RING)
            operand_high(h0h, h, KT)
            act.wait_ge(s_mem, 16)
            square_input(1, mem)
            act.wait_ge(ssm_args, 1)
            act.activation(ssm[:, 6], ssm[:, 4], ACT.Exp).then_inc(ssm_trig, 1)
            act.wait_ge(ssm_args, 2)
            act.activation(ssm[:, 10], ssm[:, 8], ACT.Sin).then_inc(ssm_trig, 1)
            act.activation(ssm[:, 11], ssm[:, 9], ACT.Sin).then_inc(ssm_trig, 1)
            for i in range(2):
                evict(("u", i), ("u", 2 * i + 1), two(uT, i))
            for i in range(2):
                evict(("q", i), ("q", 2 * i + 1), two(qT, i), HD ** -0.5)
            for i in range(2):
                evict(("k", i), ("k", 2 * i + 1), two(kT, i))
            for i in range(2):
                evict(("v", i), ("v", 3), v1[:, i])

            def evict_xv(half):
                for tt in range(TT):
                    evict(("xv", 2 * half + tt), ("xv", 4 * half + 3), xv[:, tt, half * 512:half * 512 + 512])

            def filler(slot):
                for name, unit in FILLERS[slot]:
                    i = unit // 2
                    if name == "xk" and unit == 0:
                        act.wait_ge(ssm_ready, 2)
                    if name == "xk" and unit % 2:
                        evict(("xk", i), ("xk", unit), two(xkT, i))
                    if name == "xv" and unit == 3:
                        evict_xv(0)
                    if name == "gate" and unit == 0:
                        act.wait_ge(dve_halves, 1)
                    if name == "gate" and unit % 2:
                        unit_used(("gate", unit))
                        for c in range(2):
                            ins = act.activation(gates[:, 2 * i + c], pb.bank(("gate", i))[:, c * T:c * T + T],
                                                 ACT.Identity, bias=hb[:, 2 * i + c:2 * i + c + 1], scale=0.5)
                        ins.then_inc(p_freed["act"], 1)
                        weights_high(UNIT_AT[("gate", unit)] + 1 + SPLIT_RING)

            for r in range(HEADS + 1):
                if r < HEADS:
                    act.wait_ge(*xb.read(("z", r)))
                    if r:
                        act.wait_ge(sp_ready, r)
                    link(act.activation(az, zm[r % 2], ACT.Abs))
                    link(act.activation(az, az, ACT.Exp, scale=-1.0))
                    act.activation(az, az, ACT.Ln, bias=1.0).then_inc(sp_ln, 1)
                    filler(2 * r)
                if r:
                    act.wait_ge(*xb.read(("cum", r - 1)))
                    act.activation(w1, w1, ACT.Exp).then_inc(w_exp, 1)
                if r < HEADS:
                    filler(2 * r + 1)
                if r:
                    hd = r - 1
                    lo = HD * (hd % 2)
                    act.wait_ge(pv_done, r)
                    act.copy(oT[lo:lo + HD, hd // 2], xb.bank(("pv", hd))[lo:lo + HD, 0:T]).then_inc(x_freed["act"], 1)

            act.wait_ge(y_freed, 4)
            act.activation(gt, yT, ACT.Square).then_inc(gelu_sq, 1)
            act.wait_ge(gelu_in, 1)
            act.activation(gt, gt, ACT.Tanh, scale=GELU_K * GELU_C).then_inc(gelu_th, 1)
            filler(2 * HEADS)
            act.wait_ge(*pb.read(("gate", 7)))
            act.activation(gates, gates, ACT.Tanh).then_inc(gates_th, 1)
            for i in range(2):
                unit_used(("glu", i))
                if i == 0:
                    act.wait_ge(y_ready, 1)
                for c in range(2):
                    ins = act.activation(gt[:, 2 * i + c], pb.bank(("glu", i))[:, c * T:c * T + T], ACT.Tanh,
                                         bias=hb[:, 16 + 2 * i + c:17 + 2 * i + c], scale=0.5)
                ins.then_inc(p_freed["act"], 1)
            for i in range(4):
                act.wait_ge(merged_ready, i + 1)
                act.copy(two(hh, i), two(merged, i)).then_inc(merged_high, 1)
                weights_high(UNIT_AT[("out", i)])
            weights_high(UNIT_AT[("out", 0)] + SPLIT_RING)
            square_banks(2, "out", lambda i: ("out", 2 * i + 1))

            square_input(3, x, 0)
            weights_high(UNIT_AT[("xq", 0)] + SPLIT_RING)
            operand_high(hh, h, KT)
            evict_xv(1)
            def evict_queries(pair):
                evict(("xq", pair), ("xq", 2 * pair + 1), two(xqT, pair), (D // XH) ** -0.5)

            evict_queries(0)
            for i in range(8 + 1):
                if i < 8:
                    act.wait_ge(max_ready, i + 1)
                    if i >= 2:
                        act.wait_ge(pt_done, i - 1)
                    act.activation(prob[:, i % 2], xb.bank(("sc", i))[:, 0:T], ACT.Exp, bias=sm[:, 0, i:i + 1],
                                   accum_out=sm[:, 1, i:i + 1]).then_inc(x_freed["act"], 1)
                for unit in QUERIES_AT.get(i, ()):
                    if unit % 2:
                        evict_queries(unit // 2)
                if i:
                    head, tt = (i - 1) // 2, (i - 1) % 2
                    act.wait_ge(pt_done, i)
                    if head >= 2 and tt == 0:
                        act.wait_ge(xo_done, head - 1)
                    act.copy(probT[:, head % 2, :, tt * P:tt * P + P],
                             xb.bank(("pt", i - 1))[:, 0:T].rearrange("p (m t) -> p m t", m=TT)
                             ).then_inc(x_freed["act"], 1)
                    if tt:
                        act.wait_ge(xo_done, head + 1)
                        act.copy(two(yh, head), pb.bank(("xav", head))[:]).then_inc(xo_high, 1)
            square_banks(4, "xo", lambda i: ("xo", 2 * i + 1))

            square_input(5, x, 4)
            operand_high(hh, h, KT)
            for j in range(FT):
                b = j % 3
                unit_used(("fv", j))
                if j >= 3:
                    act.wait_ge(hid_ready, j - 2)
                bank = xb.bank(("up", j))
                act.copy(up[:, b, :, 4:4 + T], bank[:].rearrange("p (c t) -> p c t", c=2))
                for c in range(2):
                    ins = act.activation(acc[:, b, c], bank[:, c * T:c * T + T], ACT.Identity,
                                         bias=col("conv_b", FT * c + j), scale=col("conv2", FT * c + j))
                ins.then_inc(x_freed["act"], 1)
                weights_high(UNIT_AT[("fv", j)] + 1 + SPLIT_RING)
                act.wait_ge(conv_g, j + 1)
                act.activation(fs[:, b, 0], acc[:, b, 0], ACT.Square).then_inc(gelu_sq, 1)
                weights_high(UNIT_AT[("fv", j)] + 2 + SPLIT_RING)
                act.wait_ge(gelu_in, j + 2)
                act.activation(fs[:, b, 0], fs[:, b, 0], ACT.Tanh, scale=GELU_K * GELU_C).then_inc(gelu_th, 1)
            square_banks(6, "dn", lambda i: ("dn", FT - 1))
            square_input(7, x, 8)
            operand_high(hh, h, KT)

            act.wait_ge(if_ready, 1)
            link(act.activation(ifr[:, 2], ifr[:, 1], ACT.Abs))
            link(act.activation(ifr[:, 2], ifr[:, 2], ACT.Exp, scale=-1.0))
            act.activation(ifr[:, 2], ifr[:, 2], ACT.Ln, bias=1.0).then_inc(if_ln, 1)
            for i in range(2):
                evict(("v2", i), ("v2", 3), v2[:, i])
            act.wait_ge(if_rows, 1)
            act.activation(ifr[:, 7], ifr[:, 7], ACT.Exp).then_inc(em_ready, 1)
            act.wait_ge(gt_done, 1)
            act.copy(gT, xb.bank(("gT", 0))[:, 0:TT * MH].rearrange("p (a b) -> p a b", a=TT)
                     ).then_inc(x_freed["act"], 1)
            for i in range(4):
                unit_used(("qk2", 2 * i + 1))
                if i >= 2:
                    act.wait_ge(qk_ready, i - 1)
                bank = pb.bank(("qk2", i))
                act.copy(qraw[:, i % 2, :, 4:4 + T], bank[:].rearrange("p (c t) -> p c t", c=2))
                for c in range(2):
                    ins = act.mul(qs[:, i % 2, c], bank[:, c * T:c * T + T], col("qk3", 2 * i + c))
                ins.then_inc(p_freed["act"], 1)
                act.wait_ge(qk_conv, i + 1)
                act.activation(qt[:, i % 2], qs[:, i % 2], ACT.Tanh, scale=0.5).then_inc(qk_th, 1)

            def gelu2(g, key, unit, keep, scratch):
                unit_used(unit)
                act.copy(keep, pb.bank(key)[:])
                act.activation(scratch, pb.bank(key)[:], ACT.Square).then_inc(p_freed["act"], 1)
                act.wait_ge(gelu_in, g + 1)
                act.activation(scratch, scratch, ACT.Tanh, scale=GELU_K * GELU_C).then_inc(gelu_th, 1)

            for i in range(2):
                unit_used(("o2", 2 * i + 1))
                act.activation(two(so, i), pb.bank(("o2", i))[:], ACT.Tanh, scale=0.5).then_inc(p_freed["act"], 1)
                weights_high(UNIT_AT[("o2", 2 * i + 1)] + 1 + SPLIT_RING)
            for i in range(MH):
                act.wait_ge(dec_in, i + 1)
                act.activation(decay, decay, ACT.Exp, scale=-1.0).then_inc(dec_exp, 1)
                if i:
                    act.wait_ge(hm_ready, i)
                act.copy(emb, xb.bank(("rows", i))[:, T:2 * T]).then_inc(x_freed["act"], 1)
                weights_high(UNIT_AT[("vg", 0)] + 2 * i + 2 + SPLIT_RING)
                if i == 1:
                    for tt in range(TT):
                        gelu2(FT + 1 + tt, ("vg", tt), ("vg", 3), gv[:, tt], gvs[:, tt])
                if i == 2:
                    for tt in range(TT):
                        act.wait_ge(vb_ready, tt + 1)
                        act.activation(gvs[:, tt], gv[:, tt], ACT.Square, accum_out=vsum[:, tt:tt + 1]).then_inc(vsq, 1)
                    act.wait_ge(vsq, TT)
                if i >= 2:
                    gelu2(FT + 1 + i, ("ug", i - 2), ("ug", 2 * i - 3), two(ug, i - 2), two(ugs, i - 2))
            act.wait_ge(hm_ready, MH)
            act.activation(sq[:, 0:4], hm, ACT.Square).then_inc(hsq, 1)
            act.wait_ge(gm_ready, 1)
            act.activation(sq[:, 4:8], gm, ACT.Square).then_inc(hsq, 1)
            act.wait_ge(hsum, 1)
            operand_high(yh, h, KT)
            act.wait_ge(sums, 8)
            for i in range(4):
                weights_high(UNIT_AT[("out2", 2 * i + 1)] + 1 + SPLIT_RING)
                act.wait_ge(x_ready, 12 + i + 1)
                act.activation(two(sq, i), two(x, i), ACT.Square).then_inc(squares, 1)

            for i in range(4):
                act.wait_ge(tr_done, i + 1)
                act.copy(xtok[:, i // 2, (i % 2) * 512:(i % 2) * 512 + 512], xb.bank(("tr", i))[:]
                         ).then_inc(x_freed["act"], 1)
            act.wait_ge(rt_max, 1)
            for tt in range(TT):
                act.activation(rsm[:, tt, 8:12], lg[:, tt, 0:NG], ACT.Exp, bias=rsm[:, tt, 0:1],
                               accum_out=rsm[:, tt, 1:2]).then_inc(rt_exp, 1)
            act.wait_ge(rt_max, 2)
            act.activation(rsm[:, :, 4], rsm[:, :, 3], ACT.Exp).then_inc(rt_exp, 1)
            act.wait_ge(rounds_ready, 1)
            n_pairs = act.value_load(rounds[0:1, 0:1], min_val=1, max_val=MAXR) * PAIRS
            xg0 = xg[:, 0:4].rearrange("p k c -> p (k c)")
            act.wait_ge(gath_done, 1)
            act.copy(xg0, psum[6][:]).then_inc(xg_low, 1)
            with act.Fori(0, n_pairs) as it:
                act.wait_ge(used, it * PAIR + (DENSE + 2 * KT))
                act.wait_ge(hx_ready, it + 1)
                act.activation(gate_th, psum[4][:], ACT.Tanh, scale=0.5).then_inc(hid_th, 1)
                act.wait_ge(gath_done, 2 * it + 3)
                act.copy(xg0, psum[6][:]).then_inc(xg_low, 1)
                act.wait_ge(hT_done, it + 1)
                act.copy(hT.rearrange("p f c -> p (f c)"), psum[4][:]).then_inc(hT_ready, 1)
                act.wait_ge(used, it * PAIR + (DENSE + PAIR))
                act.copy(yg[:, 0:512], psum[6][:]).then_inc(yg_low, 1)
            square_input(9, x, 16)

        @block.vector
        def _(dve):
            n = [0]

            def link(ins):
                n[0] += 1
                ins.then_inc(dve_chain, 1)
                dve.wait_ge(dve_chain, n[0])

            def two(v, i):
                return v[:, 2 * i:2 * i + 2].rearrange("p a t -> p (a t)")

            def ts(o, a, s1, op0, s2=None, op1=None):
                if op1 is None:
                    return dve.tensor_scalar(o, a, s1, None, op0)
                return dve.tensor_scalar(o, a, s1, s2, op0, op1)

            def tt_(o, a, b, op):
                return dve.tensor_tensor(o, a, b, op)

            def stt(o, a, s1, b, op0, op1):
                return dve.scalar_tensor_tensor(out=o, in0=a, scalar=s1, in1=b, op0=op0, op1=op1)

            def rsqrt(w):
                a, y, t = ms[:, 0:w], rstd[:, 0:w], rt[:, 0:w]
                link(ts(ri[:, 0:w], a.bitcast(I32), 1, ALU.logical_shift_right))
                link(ts(y.bitcast(I32), ri[:, 0:w], -1, ALU.mult, RSQRT_SEED, ALU.add))
                for step in range(3):
                    if w == TT:
                        for c in range(w):
                            ins = stt(t[:, c:c + 1], y[:, c:c + 1], a[:, c:c + 1], y[:, c:c + 1], ALU.mult, ALU.mult)
                        link(ins)
                    else:
                        link(tt_(t, a, y, ALU.mult))
                        link(tt_(t, t, y, ALU.mult))
                    ins = stt(y, t, 1.5, y, ALU.add, ALU.mult)
                    if step < 2:
                        link(ins)
                return ins

            def norm_scale(norm):
                dve.wait_ge(sums, norm + 1)
                link(ts(ms[:, 0:TT], STAT[:, 0:TT], -0.5 / D, ALU.mult, -0.5 * EPS, ALU.add))
                rsqrt(TT).then_inc(scales, 1)

            def normed(norm, src, dst, done):
                dve.wait_ge(spread, norm + 1)
                for k in range(KT):
                    stt(dst[:, k], src[:, k], col(NORMS[norm], k), STAT[:, T:2 * T], ALU.mult, ALU.mult
                        ).then_inc(done, 1)

            def add_normed(norm, key):
                dve.wait_ge(rb_ready, norm // 2)
                rms = rb[:].unsqueeze(1).to_broadcast([P, 2, T])
                for i in range(5):
                    if i < 4:
                        dve.wait_ge(*pb.read((key, i)))
                        tt_(post[:, 2 * i:2 * i + 2], post[:, 2 * i:2 * i + 2], rms, ALU.mult).then_inc(scaled, 1)
                    if i:
                        done_x[0] += 1
                        dve.wait_ge(scaled, done_x[0])
                        tt_(x[:, 2 * i - 2:2 * i], x[:, 2 * i - 2:2 * i], post[:, 2 * i - 2:2 * i], ALU.add
                            ).then_inc(x_ready, 1)

            lows = [0]

            def operand_lows(dst_high, dst_low, src, made, n_, done):
                for k in range(n_ + 2):
                    if k < n_:
                        made(k).then_inc(op32, 1)
                    if k >= 2:
                        lows[0] += 1
                        dve.wait_ge(op_high, lows[0])
                        tt_(dst_low[:, k - 2], src[:, k - 2], dst_high[:, k - 2].bitcast(F32), ALU.subtract
                            ).then_inc(done, 1)

            def normed_split(norm, high=hh, low=hl):
                dve.wait_ge(spread, norm + 1)
                operand_lows(high, low, h, lambda k: stt(h[:, k], x[:, k], col(NORMS[norm], k), STAT[:, T:2 * T],
                                                      ALU.mult, ALU.mult), KT, h_ready)

            done_x = [0]

            norm_scale(0)
            dve.wait_ge(s_cols, 32)
            normed_split(0, h0h, h0l)
            ts(hb[:, 0:16], cols[:, COLS["b_gate"][0]:COLS["b_gate"][0] + 16], 0.5, ALU.mult)
            ts(hb[:, 16:20], cols[:, COLS["b_glu"][0]:COLS["b_glu"][0] + 4], 0.5, ALU.mult).then_inc(dve_halves, 1)
            are, aim, dt, adt, th = ssm[:, 0], ssm[:, 1], ssm[:, 3], ssm[:, 4], ssm[:, 5]
            rad, turns, ang, cang, sin, cos = ssm[:, 6], ssm[:, 7], ssm[:, 8], ssm[:, 9], ssm[:, 10], ssm[:, 11]
            lr, li, den, num = ssm[:, 12], ssm[:, 13], ssm[:, 15], ssm[:, 16]
            t1, t2, fre, fim = ssm[:, 17], ssm[:, 18], ssm[:, 19], ssm[:, 20]
            dve.wait_ge(ssm_trig, 1)
            tt_(adt, are, dt, ALU.mult).then_inc(ssm_args, 1)
            link(tt_(th, aim, dt, ALU.mult))
            link(ts(turns, th, 1.0 / (2 * np.pi), ALU.mult, ROUND, ALU.add))
            link(ts(turns, turns, -ROUND, ALU.add))
            link(stt(ang, turns, -TWO_PI_HI, th, ALU.mult, ALU.add))
            link(stt(ang, turns, -TWO_PI_LO, ang, ALU.mult, ALU.add))
            link(ts(ang, ang, 3.1415925, ALU.min, -3.1415925, ALU.max))
            link(ts(t1, ang, -1.0, ALU.mult))
            link(tt_(t1, t1, ang, ALU.max))
            ts(cang, t1, -1.0, ALU.mult, np.pi / 2, ALU.add).then_inc(ssm_args, 1)
            norm_scale(1)
            normed(1, mem, mem, h_ready)
            dve.wait_ge(ssm_trig, 4)
            link(tt_(lr, rad, cos, ALU.mult))
            link(tt_(li, rad, sin, ALU.mult))
            link(ts(num, lr, -1.0, ALU.add))
            link(tt_(t1, are, are, ALU.mult))
            link(tt_(t2, aim, aim, ALU.mult))
            link(tt_(den, t1, t2, ALU.add))
            link(dve.reciprocal(den, den))
            link(tt_(t1, num, are, ALU.mult))
            link(tt_(t2, li, aim, ALU.mult))
            link(tt_(t1, t1, t2, ALU.add))
            link(tt_(fre, t1, den, ALU.mult))
            link(tt_(t1, li, are, ALU.mult))
            link(tt_(t2, num, aim, ALU.mult))
            link(tt_(t1, t1, t2, ALU.subtract))
            link(tt_(fim, t1, den, ALU.mult))
            link(dve.tensor_copy(powers[:, 0, 0], cos))
            link(dve.tensor_copy(powers[:, 0, 1], sin))
            link(dve.memset(rot[:, 0, :, 0:1], 1.0))
            link(dve.memset(rot[:, 1, :, 0:1], 0.0))
            k, w = 0, 1
            while w < T:
                c_, s_ = powers[:, k % 2, 0], powers[:, k % 2, 1]
                cb, sbb = (v.unsqueeze(2).to_broadcast([P, STILES, w]) for v in (c_, s_))
                a3 = ta[:, 0:STILES * w].rearrange("p (j t) -> p j t", j=STILES)
                b3 = tb[:, 0:STILES * w].rearrange("p (j t) -> p j t", j=STILES)
                tt_(a3, rot[:, 0, :, 0:w], cb, ALU.mult)
                link(tt_(b3, rot[:, 1, :, 0:w], sbb, ALU.mult))
                link(tt_(rot[:, 0, :, w:2 * w], a3, b3, ALU.subtract))
                tt_(a3, rot[:, 0, :, 0:w], sbb, ALU.mult)
                link(tt_(b3, rot[:, 1, :, 0:w], cb, ALU.mult))
                link(tt_(rot[:, 1, :, w:2 * w], a3, b3, ALU.add))
                if 2 * w < T:
                    tt_(ptmp[:, 0], c_, c_, ALU.mult)
                    tt_(ptmp[:, 1], s_, s_, ALU.mult)
                    link(tt_(ptmp[:, 2], c_, s_, ALU.mult))
                    tt_(powers[:, (k + 1) % 2, 0], ptmp[:, 0], ptmp[:, 1], ALU.subtract)
                    link(ts(powers[:, (k + 1) % 2, 1], ptmp[:, 2], 2.0, ALU.mult))
                k, w = k + 1, 2 * w
            dve.wait_ge(s_par, 16 * 17)
            dve.wait_ge(consts, 2)
            fr, fi = (v.unsqueeze(2).to_broadcast([P, STILES, 16]) for v in (fre, fim))
            a3 = ta[:, 0:256].rearrange("p (j t) -> p j t", j=STILES)
            b3 = tb[:, 0:256].rearrange("p (j t) -> p j t", j=STILES)
            tt_(a3, craw[:, 0], fr, ALU.mult)
            link(tt_(b3, craw[:, 1], fi, ALU.mult))
            for g in range(2):
                link(tt_(cbd[64 * g:64 * g + 64, 0, :, 16 * g:16 * g + 16], a3[64 * g:64 * g + 64],
                         b3[64 * g:64 * g + 64], ALU.subtract))
            tt_(a3, craw[:, 0], fi, ALU.mult)
            link(tt_(b3, craw[:, 1], fr, ALU.mult))
            for g in range(2):
                stt(cbd[64 * g:64 * g + 64, 1, :, 16 * g:16 * g + 16], a3[64 * g:64 * g + 64], -1.0,
                    b3[64 * g:64 * g + 64], ALU.mult, ALU.subtract).then_inc(ssm_ready, 1)
            dve.wait_ge(ssm_ready, 2)

            def turned(j, which):
                return rot[:, which, j].unsqueeze(1).to_broadcast([P, 2, T])

            def recurrence(j):
                dve.wait_ge(bu_done, j + 1)
                bank = xb.bank(("bu", j))[:].rearrange("p (c t) -> p c t", c=2)
                tt_(m1, bank, turned(j, 0), ALU.mult)
                tt_(m2, bank, turned(j, 1), ALU.mult).then_inc(x_freed["dve"], 1)
                dve.wait_ge(*xb.read(("bu", j)))
                tt_(vr[:, 0], m1[:, 0], m2[:, 1], ALU.add)
                link(tt_(vr[:, 1], m1[:, 1], m2[:, 0], ALU.subtract))
                r_ = rad[:, j:j + 1].to_broadcast([P, T])
                for c in range(2):
                    ins = dve.tensor_tensor_scan(wr[:, c], r_, vr[:, c], 0.0, ALU.mult, ALU.add)
                link(ins)
                tt_(m1, wr, turned(j, 0), ALU.mult)
                link(tt_(m2, wr, turned(j, 1), ALU.mult))
                if j >= 2:
                    dve.wait_ge(y_done, j - 1)
                tt_(st[:, j % 2, 0], m1[:, 0], m2[:, 1], ALU.subtract)
                tt_(st[:, j % 2, 1], m1[:, 1], m2[:, 0], ALU.add).then_inc(st_ready, 1)
                dve.wait_ge(st_ready, j + 1)

            def y_out(i):
                dve.wait_ge(y_done, 4 * i + 4)
                stt(yT[:, i], uT[:, i], col("d", i), STAT[:, 0:T], ALU.mult, ALU.add).then_inc(y_freed, 1)

            for r in range(HEADS + 1):
                if r >= 3 and r % 2:
                    y_out((r - 3) // 2)
                if r < HEADS:
                    recurrence(2 * r)
                    dve.wait_ge(z_done, r + 1)
                    tt_(zm[r % 2], xb.bank(("z", r))[:, 0:384], mask_lt[:].rearrange("p a t -> p (a t)"), ALU.mult
                        ).then_inc(x_freed["dve"], 1)
                    dve.wait_ge(*xb.read(("z", r)))
                if r:
                    dve.wait_ge(cum_done, r)
                    if r >= 2:
                        dve.wait_ge(pv_done, r - 1)
                    tt_(w1, zm[(r - 1) % 2], xb.bank(("cum", r - 1))[:, 0:384], ALU.subtract
                        ).then_inc(x_freed["dve"], 1)
                if r < HEADS:
                    recurrence(2 * r + 1)
                    dve.wait_ge(sp_ln, r + 1)
                    link(stt(sp, zm[r % 2], 0.0, az, ALU.max, ALU.add))
                    tt_(sp, sp, mask_lt[:].rearrange("p a t -> p (a t)"), ALU.mult).then_inc(sp_ready, 1)
                if r:
                    dve.wait_ge(w_exp, r)
                    tt_(w1, w1, mask_lt[:].rearrange("p a t -> p (a t)"), ALU.mult).then_inc(w_ready, 1)
            y_out(3)
            dve.wait_ge(y_freed, 4)
            dve.wait_ge(gelu_sq, 1)
            stt(gt, gt, 1.0 / GELU_C, yT, ALU.add, ALU.mult).then_inc(gelu_in, 1)
            dve.wait_ge(gelu_th, 1)
            link(ts(gt, gt, 0.5, ALU.mult, 0.5, ALU.add))
            tt_(yT, gt, yT, ALU.mult).then_inc(y_ready, 1)
            dve.wait_ge(gates_th, 1)
            link(ts(gates, gates, 0.5, ALU.mult, 0.5, ALU.add))
            dve.wait_ge(*pb.read(("glu", 1)))
            link(ts(gt, gt, 0.5, ALU.mult, 0.5, ALU.add))
            tt_(gt, gt, yT, ALU.mult).then_inc(ossm_ready, 1)
            def merged_rest(i):
                dve.wait_ge(merged_high, i + 1)
                tt_(two(hl, i), two(merged, i), two(hh, i).bitcast(F32), ALU.subtract).then_inc(merged_low, 1)

            for i in range(4):
                for c, key in enumerate(("ba", "bs")):
                    dve.wait_ge(used, UNIT_AT[(key, i)] + 1)
                    if i and c == 0:
                        merged_rest(i - 1)
                    tt_(mg[:, c], two(gates, 4 * c + i), pb.bank((key, i))[:], ALU.mult).then_inc(p_freed["dve"], 1)
                    dve.wait_ge(*pb.read((key, i)))
                tt_(two(merged, i), mg[:, 0], mg[:, 1], ALU.add).then_inc(merged_ready, 1)
            merged_rest(3)
            norm_scale(2)
            add_normed(2, "out")

            norm_scale(3)
            normed_split(3)

            def attended(hh_):
                dve.wait_ge(xo_high, hh_ + 1)
                tt_(two(yl, hh_), pb.bank(("xav", hh_))[:], two(yh, hh_).bitcast(F32), ALU.subtract
                    ).then_inc(p_freed["dve"], 1)

            for i in range(8 + 1):
                if i < 8:
                    dve.wait_ge(sc_done, i + 1)
                    link(dve.tensor_reduce(sm[:, 2, i:i + 1], xb.bank(("sc", i))[:, 0:T], AX.X, ALU.max))
                    ts(sm[:, 0, i:i + 1], sm[:, 2, i:i + 1], -1.0, ALU.mult).then_inc(max_ready, 1)
                if i:
                    dve.wait_ge(*xb.read(("sc", i - 1)))
                    link(dve.reciprocal(sm[:, 3, i - 1:i], sm[:, 1, i - 1:i]))
                    ts(prob[:, (i - 1) % 2], prob[:, (i - 1) % 2], sm[:, 3, i - 1:i], ALU.mult
                       ).then_inc(prob_ready, 1)
                if i >= 3 and i % 2:
                    attended(i // 2 - 1)
            attended(XH - 1)
            norm_scale(4)
            add_normed(4, "xo")

            norm_scale(5)
            normed_split(5)
            link(dve.memset(up[:, :, :, 0:4], 0.0))
            for j in range(FT):
                b = j % 3
                dve.wait_ge(*xb.read(("up", j)))
                for tap, lag in ((1, 1), (0, 2)):
                    for c in range(2):
                        ins = stt(acc[:, b, c], up[:, b, c, 4 - lag:4 - lag + T], col(f"conv{tap}", FT * c + j),
                                  acc[:, b, c], ALU.mult, ALU.add)
                    if tap:
                        link(ins)
                ins.then_inc(conv_g, 1)
                dve.wait_ge(conv_g, j + 1)
                dve.wait_ge(gelu_sq, j + 2)
                stt(fs[:, b, 0], fs[:, b, 0], 1.0 / GELU_C, acc[:, b, 0], ALU.add, ALU.mult).then_inc(gelu_in, 1)
                dve.wait_ge(gelu_th, j + 2)
                link(stt(fs[:, b, 1], fs[:, b, 0], 1.0, acc[:, b, 0], ALU.add, ALU.mult))
                if j >= 3:
                    dve.wait_ge(used, UNIT_AT[("dn", j - 3)] + 1)
                link(stt(hid32[:, b], fs[:, b, 1], 0.5, acc[:, b, 1], ALU.mult, ALU.mult))
                link(dve.tensor_copy(yh[:, b], hid32[:, b]))
                tt_(yl[:, b], hid32[:, b], yh[:, b].bitcast(F32), ALU.subtract).then_inc(hid_ready, 1)
            norm_scale(6)
            add_normed(6, "dn")

            norm_scale(7)
            normed_split(7)
            dve.wait_ge(s_par2, 16 * 5)
            dve.wait_ge(if_done, 1)
            bank = xb.bank(("if", 0))
            ts(ifr[:, 1], bank[0:MH, T:2 * T], b_if[:, 1:2], ALU.add).then_inc(if_ready, 1)
            link(ts(ifr[:, 0], bank[0:MH, 0:T], b_if[:, 0:1], ALU.add))
            link(dve.memset(ifr[:, 9], 1.0))
            tt_(mixw, mixw, mask_le[:, 0].unsqueeze(1).to_broadcast([P, GG, P]), ALU.mult).then_inc(x_freed["dve"], 1)
            dve.wait_ge(*xb.read(("if", 0)))
            dve.wait_ge(if_ln, 1)
            link(stt(ifr[:, 3], ifr[:, 1], 0.0, ifr[:, 2], ALU.min, ALU.subtract))
            link(dve.tensor_tensor_scan(ifr[:, 4], ifr[:, 9], ifr[:, 3], 0.0, ALU.mult, ALU.add))
            link(tt_(ifr[:, 5], ifr[:, 0], ifr[:, 4], ALU.subtract))
            link(dve.tensor_tensor_scan(ifr[:, 6], ifr[:, 5], ifr[:, 5], 0.0, ALU.max, ALU.max))
            link(tt_(ifr[:, 7], ifr[:, 4], ifr[:, 6], ALU.add))
            ts(ifr[:, 7], ifr[:, 7], -1.0, ALU.mult, 87.0, ALU.min).then_inc(if_rows, 1)
            link(dve.memset(qraw[:, :, :, 0:4], 0.0))
            dve.wait_ge(if_rows, 1)
            dve.nop().then_inc(qpad, 1)
            for i in range(4):
                b = i % 2
                dve.wait_ge(*pb.read(("qk2", i)))
                for tap in (2, 1, 0):
                    for c in range(2):
                        ins = stt(qs[:, b, c], qraw[:, b, c, 1 + tap:1 + tap + T], col(f"qk{tap}", 2 * i + c),
                                  qs[:, b, c], ALU.mult, ALU.add)
                    if tap:
                        link(ins)
                ins.then_inc(qk_conv, 1)
                dve.wait_ge(qk_th, i + 1)
                stt(qk2[:, 2 * i:2 * i + 2], qt[:, b], 1.0, qs[:, b], ALU.add, ALU.mult).then_inc(qk_ready, 1)

            def gelu2(g, keep, scratch):
                stt(scratch, scratch, 1.0 / GELU_C, keep, ALU.add, ALU.mult).then_inc(gelu_in, 1)
                dve.wait_ge(gelu_th, g + 1)
                link(ts(scratch, scratch, 0.5, ALU.mult, 0.5, ALU.add))
                return tt_(keep, keep, scratch, ALU.mult)

            def branch_gelu(i):
                if i == 1:
                    for tt in range(TT):
                        dve.wait_ge(*pb.read(("vg", tt)))
                        gelu2(FT + 1 + tt, gv[:, tt], gvs[:, tt]).then_inc(vb_ready, 1)
                if i == 2:
                    for tt in range(TT):
                        dve.wait_ge(vsq, tt + 1)
                    link(ts(ms[:, 0:TT], vsum, -0.5 / 512, ALU.mult, -0.5 * EPS, ALU.add))
                    link(rsqrt(TT))
                    for tt in range(TT):
                        ts(gv[:, tt], gv[:, tt], rstd[:, tt:tt + 1], ALU.mult).then_inc(vb_ready, 1)
                if i >= 2:
                    dve.wait_ge(*pb.read(("ug", i - 2)))
                    link(gelu2(FT + 1 + i, two(ug, i - 2), two(ugs, i - 2)))

            dve.wait_ge(*pb.read(("o2", 1)))
            link(ts(so, so, 0.5, ALU.mult, 0.5, ALU.add))
            c2 = 0.25 * P ** -0.5
            def decay_in(i):
                dve.wait_ge(rows_done, i + 1)
                bank = xb.bank(("rows", i))
                ts(decay[:, 0:T], bank[:, 0:T], gT[:, 0, i:i + 1], ALU.subtract, 0.0, ALU.max)
                ts(decay[:, T:384], bank[:, P:T], gT[:, 1, i:i + 1], ALU.subtract, 0.0, ALU.max).then_inc(dec_in, 1)

            decay_in(0)
            for i in range(MH):
                dve.wait_ge(dec_exp, i + 1)
                link(tt_(decay, decay, mask_le[:].rearrange("p a t -> p (a t)"), ALU.mult))
                dve.wait_ge(s2_done, i + 1)
                stt(st2, xb.bank(("s2", i))[:, 0:384], c2, decay, ALU.mult, ALU.mult).then_inc(x_freed["dve"], 1)
                if i + 1 < MH:
                    dve.wait_ge(*xb.read(("s2", i)))
                    decay_in(i + 1)
                dve.wait_ge(*xb.read(("rows", i)))
                dve.wait_ge(num_done, i + 1)
                bank = xb.bank(("num", i))
                link(stt(hden, bank[:, T:2 * T], -1.0, emb, ALU.mult, ALU.max))
                link(tt_(hden, bank[:, T:2 * T], hden, ALU.max))
                link(dve.reciprocal(hden, hden))
                tt_(hden, bank[:, 0:T], hden, ALU.mult).then_inc(x_freed["dve"], 1)
                dve.wait_ge(*xb.read(("num", i)))
                tt_(hm[:, i], hden, so[:, i], ALU.mult).then_inc(hm_ready, 1)
                dve.wait_ge(hm_ready, i + 1)
                branch_gelu(i)
            for i in range(2):
                dve.wait_ge(mix_done, i + 1)
                bank = xb.bank(("mix", i))
                for c in range(2):
                    t_ = 2 * i + c
                    ins = stt(gm[:, t_].rearrange("p (n t) -> p n t", n=TT),
                              bank[:, c * T:c * T + T].rearrange("p (n t) -> p n t", n=TT), col("g_v", t_),
                              bsp[:, t_].unsqueeze(1).to_broadcast([P, TT, P]), ALU.mult, ALU.add)
                ins.then_inc(x_freed["dve"], 1)
            dve.wait_ge(*xb.read(("mix", 1)))
            tt_(gm, gm, ug, ALU.mult).then_inc(gm_ready, 1)
            dve.wait_ge(hsum, 1)
            bank = xb.bank(("hsum", 0))
            ts(ms[:, 0:8], bank[:, 0:8], -0.5 / P, ALU.mult, -0.5 * EPS, ALU.add)
            ts(ms[:, 8:24], bank[:, 8:24], -0.5 / 64, ALU.mult, -0.5 * EPS, ALU.add).then_inc(x_freed["dve"], 1)
            dve.wait_ge(*xb.read(("hsum", 0)))
            rsqrt(24).then_inc(hscale, 1)

            def headed(t_):
                i, c = t_ // 2, t_ % 2
                if c == 0:
                    dve.wait_ge(hspread, i + 1)
                src, g_ = (hm[:, t_], col("g_mlstm", t_)) if t_ < 4 else (gm[:, t_ - 4], col("g_gmlp", t_ - 4))
                return stt(h[:, t_], src, g_, xb.bank(("hspread", i))[:, c * T:c * T + T], ALU.mult, ALU.mult)

            operand_lows(yh, yl, h, headed, KT, op_low)
            link(ts(first, slots[:, 0:EG], -1.0, ALU.mult, float(EG), ALU.add))
            link(dve.memset(rank, -1.0))
            link(dve.memset(wall, 0.0))
            dve.memset(zero, 0.0).then_inc(y_zeroed, 1)
            dve.memset(scwT, 0.0).then_inc(scwT_ready, 1)
            dve.memset(hT, 0.0).then_inc(hT_ready, 1)
            dve.memset(hx, 0.0).then_inc(hx_ready, 1)
            for i in range(4):
                dve.wait_ge(used, UNIT_AT[("out2", 2 * i + 1)] + 1)
                if i == 0:
                    dve.wait_ge(x_ready, done_x[0])
                tt_(two(x, i), two(x, i), pb.bank(("out2", i))[:], ALU.add).then_inc(x_ready, 1)
            norm_scale(8)
            normed(8, x, h, h_ready)

            dve.memset(yg[:, 0:512], 0.0).then_inc(yg_low, 1)
            dve.memset(yg[:, 512:D], 0.0).then_inc(yg_high, 1)
            dve.wait_ge(s_par3, 32)
            dve.wait_ge(lg_done, 1)
            logits = xb.bank(("lg", 0))[:, 0:64 * TT].rearrange("p (a c) -> p a c", a=TT)[:, :, 0:36]
            tt_(lg, logits, b_r.unsqueeze(1).to_broadcast([P, TT, 36]), ALU.add).then_inc(x_freed["dve"], 1)
            dve.wait_ge(*xb.read(("lg", 0)))

            def over(values, w):
                return values.unsqueeze(2).to_broadcast([P, TT, w])

            def pick(values, w, where, best, tmp):
                link(dve.tensor_reduce(best, values, AX.X, ALU.max))
                link(tt_(where, values, over(best, w), ALU.is_equal))
                link(tt_(where, where, first[:, 0:w].unsqueeze(1).to_broadcast([P, TT, w]), ALU.mult))
                link(dve.tensor_reduce(tmp, where, AX.X, ALU.max))
                link(tt_(where, where, over(tmp, w), ALU.is_equal))

            r_ = [rsm[:, :, q] for q in range(16)]
            le, rest, both, wts = (lsel[:, q] for q in range(4))
            spread_groups = [P, TT, NG, EG]
            in_group = gsel.unsqueeze(3).to_broadcast(spread_groups)
            pick(lg[:, :, 0:NG], NG, gsel, r_[5], r_[6])
            ts(r_[0], r_[5], -1.0, ALU.mult).then_inc(rt_max, 1)
            link(tt_(lgrp, lg[:, :, NG:NG + NE].rearrange("p a (g e) -> p a g e", g=NG), in_group, ALU.mult))
            link(dve.tensor_reduce(le, lgrp.rearrange("p a g e -> p a e g"), AX.X, ALU.add))
            pick(le, EG, sel1, r_[7], r_[6])
            link(stt(rest, sel1, -3.0e38, le, ALU.mult, ALU.add))
            pick(rest, EG, sel2, r_[12], r_[6])
            tt_(r_[3], r_[12], r_[7], ALU.subtract).then_inc(rt_max, 1)
            link(tt_(both, sel1, sel2, ALU.add))
            tt_(selm.rearrange("p a (g e) -> p a g e", g=NG), both.unsqueeze(2).to_broadcast(spread_groups), in_group,
                ALU.mult).then_inc(sel_ready, 1)
            dve.wait_ge(rt_exp, TT + 1)
            link(ts(r_[13], r_[4], 1.0, ALU.add))
            link(tt_(r_[13], r_[13], r_[1], ALU.mult))
            link(dve.reciprocal(r_[14], r_[13]))
            link(tt_(r_[15], r_[14], r_[4], ALU.mult))
            tt_(wts, sel1, over(r_[14], EG), ALU.mult)
            link(tt_(rest, sel2, over(r_[15], EG), ALU.mult))
            link(tt_(wts, wts, rest, ALU.add))
            link(tt_(selw.rearrange("p a (g e) -> p a g e", g=NG), wts.unsqueeze(2).to_broadcast(spread_groups),
                     in_group, ALU.mult))
            dve.wait_ge(rank_done, 1)
            bank = xb.bank(("rank", 0))
            tt_(lmask, bank[:, 0:TT * NE].rearrange("p (a e) -> p a e", a=TT), selm, ALU.mult)
            dve.tensor_reduce(cnt[:, 0:1], bank[:, 2 * NE:3 * NE], AX.X, ALU.max).then_inc(x_freed["dve"], 1)
            dve.wait_ge(*xb.read(("rank", 0)))
            link(stt(lmask, selm, -1.0, lmask, ALU.add, ALU.add))

            def places(r):
                dve.tensor_copy(wall[:, :, NE * r:NE * r + NE], selw)
                link(ts(rank[:, :, NE * r:NE * r + NE], lmask, float(-CAP * r), ALU.add))

            def gather_matrix(first_column):
                for e in range(2):
                    for tt in range(TT):
                        ins = ts(gat[:, tt, CAP * e:CAP * e + CAP], slots[:],
                                 rank[:, tt, bass.ds(first_column + e, 1)], ALU.is_equal)
                ins.then_inc(g_ready, 1)

            places(0)
            gather_matrix(0)
            link(ts(cnt[:, 1:2], cnt[:, 0:1], CAP + 0.5, ALU.is_gt, 1.0, ALU.add))
            for r in range(2, MAXR):
                link(ts(cnt[:, 2:3], cnt[:, 0:1], CAP * r + 0.5, ALU.is_gt))
                link(tt_(cnt[:, 1:2], cnt[:, 1:2], cnt[:, 2:3], ALU.add))
            dve.tensor_copy(rounds[0:1, 0:1], cnt[0:1, 1:2]).then_inc(rounds_ready, 1)
            for r in range(1, MAXR):
                places(r)

            dve.wait_ge(rounds_ready, 1)
            n_pairs = dve.value_load(rounds[0:1, 0:1], min_val=1, max_val=MAXR) * PAIRS
            xg1 = xg[:, 4:8].rearrange("p k c -> p (k c)")
            dve.wait_ge(gath_done, 2)
            dve.tensor_copy(xg1, psum[7][:]).then_inc(xg_high, 1)
            with dve.Fori(0, n_pairs) as it:
                dve.wait_ge(gath_done, 2 * it + 2)
                gather_matrix(2 * it + 2)
                dve.wait_ge(scwT_ready, it + 1)
                for e in range(2):
                    for tt in range(TT):
                        ins = ts(scw[:, tt, CAP * e:CAP * e + CAP], slots[:], rank[:, tt, bass.ds(2 * it + e, 1)],
                                 ALU.is_equal, wall[:, tt, bass.ds(2 * it + e, 1)], ALU.mult)
                ins.then_inc(scw_ready, 1)
                dve.wait_ge(hid_th, it + 1)
                stt(act_, gate_th, 1.0, psum[4][:], ALU.add, ALU.mult).then_inc(silu_done, 1)
                dve.wait_ge(silu_done, it + 1)
                stt(hx, act_, 0.5, psum[5][:], ALU.mult, ALU.mult).then_inc(hx_ready, 1)
                dve.wait_ge(gath_done, 2 * it + 4)
                dve.tensor_copy(xg1, psum[7][:]).then_inc(xg_high, 1)
                dve.wait_ge(scwT_done, it + 1)
                dve.tensor_copy(scwT, psum[5][:, 0:T]).then_inc(scwT_ready, 1)
                dve.wait_ge(used, it * PAIR + (DENSE + PAIR))
                dve.tensor_copy(yg[:, 512:D], psum[7][:]).then_inc(yg_high, 1)
            dve.wait_ge(moe_done, 1)
            for i in range(4):
                tt_(two(x, i), two(x, i), psum[i][:], ALU.add).then_inc(x_ready, 1)
            norm_scale(9)
            dve.wait_ge(x_ready, 20)
            normed(9, x, res, res_ready)

        @block.tensor
        def _(pe):
            def unit(key):
                k = UNIT_AT[key]
                pe.wait_ge(landed[k % RING], 16 * (k // RING + 1))
                return ring[:, k % RING]

            def mm(o, a, b, start, stop):
                return pe.matmul(o, a, b, start=start, stop=stop, skip_group_check=True)

            def split_unit(key):
                m = SPLIT_AT[key]
                pe.wait_ge(lo_ready, m + 1)
                return wh[:, m % SPLIT_RING], wl[:, UNIT_AT[key] % RING]

            def mm_split(o, a_parts, b_parts, start, stop):
                (ah, al), (bh, bl) = a_parts, b_parts
                mm(o, ah, bh, start, False)
                mm(o, ah, bl, False, False)
                return mm(o, al, bh, False, stop)

            def norm_sum(norm, i):
                pe.wait_ge(squares, 4 * norm + i + 1)
                for k in range(2 * i, 2 * i + 2):
                    for tt in range(TT):
                        ins = mm(STAT[:, tt:tt + 1], sq[:, k, tt * P:tt * P + P], ones[:, 0:1],
                                 k == 0 and tt == 0, k == KT - 1)
                if i == 3:
                    ins.then_inc(sums, 1)

            def norm_sums(norm, first=0, beside=None):
                for i in range(first, 4):
                    norm_sum(norm, i)
                if beside is not None:
                    beside()
                pe.wait_ge(scales, norm + 1)
                for tt in range(TT):
                    ins = mm(STAT[:, T + tt * P:T + tt * P + P], rstd[:, tt:tt + 1].to_broadcast([P, P]), ident[:],
                             True, True)
                ins.then_inc(spread, 1)

            def tile_column(bank, key, i, c, src, ready, base):
                w = unit((key, 2 * i + c))
                for k in range(KT):
                    if ready is not None and i == 0 and c == 0:
                        pe.wait_ge(ready, base + k + 1)
                    ins = mm(bank[:, c * T:c * T + T], w[:, k * P:k * P + P], src[:, k], k == 0, k == KT - 1)
                ins.then_inc(used, 1)

            def rows_part(banks, key, first_unit, n_units, src, total, k0):
                for u in range(n_units):
                    w = unit((key, first_unit + u))
                    for kk in range(2):
                        k = k0 + 2 * u + kk
                        for tt in range(TT):
                            ins = mm(banks[tt][:], src[:, k, tt * P:tt * P + P], w[:, kk * 512:kk * 512 + 512],
                                     k == 0, k == total - 1)
                    ins.then_inc(used, 1)

            def split_tile_column(bank, key, i, c, src, ready, base):
                w_high, w_low = split_unit((key, 2 * i + c))
                for k in range(KT):
                    if ready is not None and i == 0 and c == 0:
                        pe.wait_ge(ready, base + k + 1)
                    tile = slice(k * P, k * P + P)
                    ins = mm_split(bank[:, c * T:c * T + T], (w_high[:, tile], w_low[:, tile]),
                                   (src[0][:, k], src[1][:, k]), k == 0, k == KT - 1)
                ins.then_inc(used, 1)

            def split_cols_pair(bank, key, i, src, ready, base):
                for c in range(2):
                    split_tile_column(bank, key, i, c, src, ready, base)

            def split_rows(key, src, first, end):
                if first == 0:
                    for i in range(TT):
                        pb.claim(pe, (key, i))
                for u in range(first, end):
                    w_high, w_low = split_unit((key, u))
                    for kk in range(2):
                        k = 2 * u + kk
                        for tt in range(TT):
                            tile, columns = slice(tt * P, tt * P + P), slice(kk * 512, kk * 512 + 512)
                            ins = mm_split(pb.bank((key, tt))[:], (src[0][:, k, tile], src[1][:, k, tile]),
                                           (w_high[:, columns], w_low[:, columns]), k == 0, k == KT - 1)
                    ins.then_inc(used, 1)

            def pairs(key, n, src, ready=None, base=0, norm=None):
                for i in range(n):
                    pb.claim(pe, (key, i))
                    split_cols_pair(pb.bank((key, i)), key, i, src, ready, base)
                    if norm is not None and i:
                        norm_sum(norm, i - 1)

            pe.wait_ge(consts, 1)
            norm_sums(0)
            pairs("u", 2, (h0h, h0l), h_ready, 0)
            norm_sums(1)
            pairs("q", 2, (h0h, h0l))
            pairs("k", 2, (h0h, h0l))
            split_rows("v", (h0h, h0l), 0, 4)

            def xv_units(half, first, end):
                if first == 0:
                    for tt in range(TT):
                        pb.claim(pe, ("xv", 2 * half + tt))
                rows_part([pb.bank(("xv", 2 * half + tt)) for tt in range(TT)], "xv", 4 * half + first, end - first,
                          mem, KT, 2 * first)

            def filler(slot):
                for name, unit in FILLERS[slot]:
                    i, c = unit // 2, unit % 2
                    if name == "xv":
                        xv_units(0, unit, unit + 1)
                        continue
                    if c == 0:
                        pb.claim(pe, (name, i))
                    if name == "xk":
                        tile_column(pb.bank(("xk", i)), "xk", i, c, mem, h_ready, 8)
                    else:
                        split_tile_column(pb.bank(("gate", i)), "gate", i, c, (h0h, h0l), None, 0)

            def inputs_of(j):
                i, q = j // 4, j % 4
                if j == 0:
                    pe.wait_ge(s_par, 16 * 17)
                    pe.wait_ge(*pb.read(("u", 1)))
                xb.claim(pe, ("bu", j))
                for c in range(2):
                    ins = mm(xb.bank(("bu", j))[:, c * T:c * T + T], bbd[32 * q:32 * q + 32, c, i],
                             uT[32 * q:32 * q + 32, i], True, True)
                ins.then_inc(bu_done, 1)

            def outputs_of(j):
                i, q = j // 4, j % 4
                pe.wait_ge(st_ready, j + 1)
                if q == 0 and i:
                    pe.wait_ge(y_freed, i)
                for c in range(2):
                    ins = mm(STAT[32 * q:32 * q + 32, 0:T], cbd[:, c, j], st[:, j % 2, c], c == 0, c == 1)
                ins.then_inc(y_done, 1)

            for r in range(HEADS + 1):
                lo = HD * (r % 2)
                if r < HEADS:
                    inputs_of(2 * r)
                    if r == 0:
                        pe.wait_ge(*pb.read(("v", 1)))
                    xb.claim(pe, ("z", r))
                    z = xb.bank(("z", r))
                    qh, kh = qT[lo:lo + HD, r // 2], kT[lo:lo + HD, r // 2]
                    mm(z[:, 0:T], kh[:, 0:P], qh, True, True)
                    mm(z[:, T:384], kh[:, P:T], qh[:, P:T], True, True).then_inc(z_done, 1)
                if r:
                    outputs_of(2 * r - 2)
                    outputs_of(2 * r - 1)
                if r < HEADS:
                    filler(2 * r)
                if r:
                    xb.claim(pe, ("cum", r - 1))
                    pe.wait_ge(sp_ready, r)
                    z = xb.bank(("cum", r - 1))
                    mm(z[:, 0:T], tri[:], sp[:, 0:T], True, False)
                    mm(z[:, P:T], ones[:], sp[:, T:384], False, True)
                    mm(z[:, T:384], tri[:], sp[:, T:384], True, True).then_inc(cum_done, 1)
                if r < HEADS:
                    inputs_of(2 * r + 1)
                    filler(2 * r + 1)
                if r:
                    hd = r - 1
                    lo = HD * (hd % 2)
                    xb.claim(pe, ("pv", hd))
                    pe.wait_ge(w_ready, r)
                    o = xb.bank(("pv", hd))[lo:lo + HD]
                    mm(o[:, 0:T], v1[:, 0, HD * hd:HD * hd + HD], w1[:, 0:T], True, False)
                    mm(o[:, P:T], v1[:, 1, HD * hd:HD * hd + HD], w1[:, T:384], False, True).then_inc(pv_done, 1)

            def half_depth(bank, key, i, src):
                w = unit((key, i))
                for c in range(2):
                    for k in range(4):
                        ins = mm(bank[:, c * T:c * T + T], w[:, (4 * c + k) * P:(4 * c + k + 1) * P], src[:, k],
                                 k == 0, k == 3)
                ins.then_inc(used, 1)

            filler(2 * HEADS)
            pe.wait_ge(y_ready, 1)
            for i in range(2):
                pb.claim(pe, ("glu", i))
                half_depth(pb.bank(("glu", i)), "glu", i, yT)
            pe.wait_ge(*xb.read(("pv", HEADS - 1)))
            for i in range(4):
                pb.claim(pe, ("ba", i))
                half_depth(pb.bank(("ba", i)), "ba", i, oT)
                if i == 0:
                    pe.wait_ge(ossm_ready, 1)
                pb.claim(pe, ("bs", i))
                half_depth(pb.bank(("bs", i)), "bs", i, gt)
            pe.wait_ge(merged_low, 4)
            pairs("out", 4, (hh, hl), norm=2)
            norm_sums(2, 3, lambda: xv_units(1, 0, 1))
            xv_units(1, 1, 3)

            norm_sums(3, 0, lambda: xv_units(1, 3, 4))
            def query_unit(n):
                pair, c = n // 2, n % 2
                if c == 0:
                    pb.claim(pe, ("xq", pair))
                split_tile_column(pb.bank(("xq", pair)), "xq", pair, c, (hh, hl), h_ready, 16)

            query_unit(0)
            query_unit(1)
            for i in range(8 + 1):
                if i < 8:
                    pe.wait_ge(*pb.read(("xq", i // 2)))
                    head, tt = i // 2, i % 2
                    xb.claim(pe, ("sc", i))
                    for k in range(2):
                        ins = mm(xb.bank(("sc", i))[:, 0:T], xqT[:, 2 * head + k, tt * P:tt * P + P],
                                 xkT[:, 2 * head + k], k == 0, k == 1)
                    ins.then_inc(sc_done, 1)
                for unit_ in QUERIES_AT.get(i, ()):
                    query_unit(unit_)
                if i:
                    head, tt = (i - 1) // 2, (i - 1) % 2
                    xb.claim(pe, ("pt", i - 1))
                    pe.wait_ge(prob_ready, i)
                    for m in range(2):
                        ins = pe.transpose(xb.bank(("pt", i - 1))[:, m * P:m * P + P],
                                           prob[:, (i - 1) % 2, m * P:m * P + P], ident[:])
                    ins.then_inc(pt_done, 1)
                    if tt:
                        pb.claim(pe, ("xav", head))
                        pe.wait_ge(*xb.read(("pt", i - 1)))
                        for c in range(2):
                            for m in range(2):
                                ins = mm(pb.bank(("xav", head))[:, c * T:c * T + T],
                                         xv[:, m, (2 * head + c) * P:(2 * head + c + 1) * P], probT[:, head % 2, m],
                                         m == 0, m == 1)
                        ins.then_inc(xo_done, 1)
            pe.wait_ge(*pb.read(("xav", XH - 1)))
            pairs("xo", 4, (yh, yl), norm=4)
            norm_sums(4, 3)

            norm_sums(5)
            for i in range(4):
                pb.claim(pe, ("dn", i))
            for j in range(FT + 2):
                if j < FT:
                    xb.claim(pe, ("up", j))
                    for c, key in enumerate(("fg", "fv")):
                        w_high, w_low = split_unit((key, j))
                        for k in range(KT):
                            if j == 0 and c == 0:
                                pe.wait_ge(h_ready, 24 + k + 1)
                            tile = slice(k * P, k * P + P)
                            ins = mm_split(xb.bank(("up", j))[:, c * T:c * T + T], (w_high[:, tile], w_low[:, tile]),
                                           (hh[:, k], hl[:, k]), k == 0, k == KT - 1)
                        ins.then_inc(used, 1)
                if j >= 2:
                    w_high, w_low = split_unit(("dn", j - 2))
                    pe.wait_ge(hid_ready, j - 1)
                    b = (j - 2) % 3
                    for c in range(KT):
                        tile = slice(c * P, c * P + P)
                        ins = mm_split(pb.bank(("dn", c // 2))[:, (c % 2) * T:(c % 2) * T + T],
                                       (w_high[:, tile], w_low[:, tile]), (yh[:, b], yl[:, b]),
                                       j == 2 and c % 2 == 0, j == FT + 1)
                    ins.then_inc(used, 1)
            norm_sums(6)

            norm_sums(7)
            pe.wait_ge(s_par2, 16 * 5)
            xb.claim(pe, ("if", 0))
            for c in range(2):
                for k in range(KT):
                    if c == 0:
                        pe.wait_ge(h_ready, 32 + k + 1)
                    ins = mm(xb.bank(("if", 0))[0:MH, c * T:c * T + T], w_if[:, k, MH * c:MH * c + MH], h[:, k],
                             k == 0, k == KT - 1)
            ins.then_inc(if_done, 1)
            split_rows("v2", (hh, hl), 0, 4)
            xb.claim(pe, ("gT", 0))
            pe.wait_ge(if_rows, 1)
            for tt in range(TT):
                ins = pe.transpose(xb.bank(("gT", 0))[:, MH * tt:MH * tt + MH], ifr[:, 5, tt * P:tt * P + P],
                                   ident[0:MH, 0:MH])
            ins.then_inc(gt_done, 1)
            pe.wait_ge(qpad, 1)
            pairs("qk2", 4, (hh, hl))
            pairs("o2", 2, (hh, hl))
            pe.wait_ge(em_ready, 1)
            pe.wait_ge(qk_ready, 4)
            for i in range(MH + 1):
                if i < MH:
                    xb.claim(pe, ("rows", i))
                    for c, row in enumerate((6, 7)):
                        ins = mm(xb.bank(("rows", i))[:, c * T:c * T + T], head_sel[:, i], ifr[:, row], True, True)
                    ins.then_inc(rows_done, 1)
                if i:
                    xb.claim(pe, ("num", i - 1))
                    pe.wait_ge(*xb.read(("s2", i - 1)))
                    o = xb.bank(("num", i - 1))
                    for c in range(2):
                        w0 = v2[:, 0, (i - 1) * P:i * P] if c == 0 else ones[:]
                        w1_ = v2[:, 1, (i - 1) * P:i * P] if c == 0 else ones[:]
                        mm(o[:, c * T:c * T + T], w0, st2[:, 0:T], True, False)
                        ins = mm(o[:, c * T + P:c * T + T], w1_, st2[:, T:384], False, True)
                    ins.then_inc(num_done, 1)
                if i < MH:
                    xb.claim(pe, ("s2", i))
                    z = xb.bank(("s2", i))
                    qh, kh = qk2[:, i], qk2[:, MH + i]
                    mm(z[:, 0:T], kh[:, 0:P], qh, True, True)
                    mm(z[:, T:384], kh[:, P:T], qh[:, P:T], True, True).then_inc(s2_done, 1)
                    if i < 2:
                        split_rows("vg", (hh, hl), 2 * i, 2 * i + 2)
                    else:
                        pb.claim(pe, ("ug", i - 2))
                        split_cols_pair(pb.bank(("ug", i - 2)), "ug", i - 2, (hh, hl), None, 0)
            pe.wait_ge(vb_ready, 4)
            for i in range(2):
                xb.claim(pe, ("mix", i))
                for c in range(2):
                    for half in range(2):
                        g = 4 * i + 2 * c + half
                        for nb in range(TT):
                            ins = mm(xb.bank(("mix", i))[64 * half:64 * half + 64, c * T + nb * P:c * T + nb * P + P],
                                     gv[:, nb, 64 * g:64 * g + 64], mixw[:, g], True, True)
                ins.then_inc(mix_done, 1)
            xb.claim(pe, ("hsum", 0))
            pe.wait_ge(hsq, 1)
            o = xb.bank(("hsum", 0))
            for i in range(4):
                for tt in range(TT):
                    mm(o[:, 2 * i + tt:2 * i + tt + 1], sq[:, i, tt * P:tt * P + P], ones[:, 0:1], True, True)
            pe.wait_ge(hsq, 2)
            for i in range(4):
                for tt in range(TT):
                    a = 8 + 4 * i + 2 * tt
                    ins = mm(o[:, a:a + 2], sq[:, 4 + i, tt * P:tt * P + P], half_ones[:], True, True)
            ins.then_inc(hsum, 1)
            pe.wait_ge(hscale, 1)
            for i in range(4):
                xb.claim(pe, ("hspread", i))
                for c in range(2):
                    t_ = 2 * i + c
                    for tt in range(TT):
                        o = xb.bank(("hspread", i))[:, c * T + tt * P:c * T + tt * P + P]
                        if t_ < 4:
                            w = rstd[:, 2 * t_ + tt:2 * t_ + tt + 1].to_broadcast([P, P])
                            ins = mm(o, w, ident[:], True, True)
                        for half in range(2 if t_ >= 4 else 0):
                            a = 8 + 4 * (t_ - 4) + 2 * tt + half
                            ins = mm(o[64 * half:64 * half + 64], rstd[:, a:a + 1].to_broadcast([P, 64]), ident[:],
                                     True, True)
                ins.then_inc(hspread, 1)
            pairs("out2", 4, (yh, yl), op_low, 0, norm=8)

            norm_sums(8, 3)
            pe.wait_ge(h_ready, 48)
            xb.claim(pe, ("lg", 0))
            pe.wait_ge(s_par3, 32)
            for tt in range(TT):
                for k in range(KT):
                    ins = mm(xb.bank(("lg", 0))[:, 64 * tt:64 * tt + 36], h[:, k, tt * P:tt * P + P], w_r[:, k],
                             k == 0, k == KT - 1)
            ins.then_inc(lg_done, 1)
            for i in range(4):
                xb.claim(pe, ("tr", i))
                for k in range(4):
                    ins = pe.transpose(xb.bank(("tr", i))[:, k * P:k * P + P],
                                       h[:, 4 * (i % 2) + k, (i // 2) * P:(i // 2) * P + P], ident[:])
                ins.then_inc(tr_done, 1)
            pe.wait_ge(y_zeroed, 1)
            pe.wait_ge(x_ready, 16)
            for i in range(4):
                mm(psum[i][:], ident[:], zero, True, True)
            xb.claim(pe, ("rank", 0))
            pe.wait_ge(sel_ready, 1)
            o = xb.bank(("rank", 0))
            mm(o[:, 0:NE], before[:], selm[:, 0], True, True)
            mm(o[:, NE:2 * NE], before[:], selm[:, 1], True, False)
            mm(o[:, NE:2 * NE], ones[:], selm[:, 0], False, True)
            mm(o[:, 2 * NE:3 * NE], ones[:], selm[:, 0], True, False)
            mm(o[:, 2 * NE:3 * NE], ones[:], selm[:, 1], False, True).then_inc(rank_done, 1)
            pe.wait_ge(*xb.read(("tr", 3)))
            pe.wait_ge(*xb.read(("rank", 0)))
            def gather():
                for k in range(KT):
                    c = (k % 4) * 2 * CAP
                    for tt in range(TT):
                        ins = mm(psum[6 + k // 4][:, c:c + 2 * CAP], xtok[:, tt, k * P:k * P + P], gat[:, tt],
                                 tt == 0, tt == 1)
                    if k % 4 == 3:
                        ins.then_inc(gath_done, 1)

            def scatter():
                for k in range(KT):
                    ins = mm(psum[k // 2][:, (k % 2) * T:(k % 2) * T + T], yg[:, k * P:k * P + P], scwT, False, True)
                return ins

            def pair_unit(it, n):
                pe.wait_ge(landed[n], it * 16 + 16 * (DENSE // RING + 1 if n < RING else 1))
                return pair_slot[n]

            half = (slice(0, CAP), slice(CAP, 2 * CAP))
            pe.wait_ge(g_ready, 1)
            gather()
            pe.wait_ge(rounds_ready, 1)
            n_pairs = pe.value_load(rounds[0:1, 0:1], min_val=1, max_val=MAXR) * PAIRS
            with pe.Fori(0, n_pairs) as it:
                pe.wait_ge(xg_low, it + 1)
                pe.wait_ge(xg_high, it + 1)
                pe.wait_ge(hT_ready, it + 1)
                pe.wait_ge(scwT_ready, it + 1)
                for k in range(KT):
                    w = [pair_unit(it, 2 * k + e) for e in range(2)]
                    for c in range(2):
                        for e in range(2):
                            ins = mm(psum[4 + c][half[e]], xg[:, k, half[e]], w[e][:, c * FE:c * FE + FE],
                                     k == 0, k == KT - 1)
                            if c:
                                ins.then_inc(used, 1)
                pe.wait_ge(g_ready, it + 2)
                pe.wait_ge(yg_low, it + 1)
                pe.wait_ge(yg_high, it + 1)
                gather()
                scatter()
                pe.wait_ge(hx_ready, it + 2)
                for f in range(FE // P):
                    ins = pe.transpose(psum[4][:, f * P:f * P + P], hx[:, f * P:f * P + P], ident[:])
                ins.then_inc(hT_done, 1)
                pe.wait_ge(scw_ready, it + 1)
                for tt in range(TT):
                    ins = pe.transpose(psum[5][:, tt * P:tt * P + P], scw[:, tt], ident[:])
                ins.then_inc(scwT_done, 1)
                pe.wait_ge(xg_low, it + 2)
                pe.wait_ge(xg_high, it + 2)
                pe.wait_ge(hT_ready, it + 2)
                for f in range(FE // P):
                    w = [pair_unit(it, 2 * KT + 2 * f + e) for e in range(2)]
                    for c in range(2):
                        for e in range(2):
                            ins = mm(psum[6 + c][half[e]], hT[:, f, half[e]], w[e][:, c * 512:c * 512 + 512],
                                     f == 0, f == FE // P - 1)
                            if c:
                                ins.then_inc(used, 1)
            pe.wait_ge(yg_low, n_pairs + 1)
            pe.wait_ge(yg_high, n_pairs + 1)
            pe.wait_ge(scwT_ready, n_pairs + 1)
            scatter().then_inc(moe_done, 1)
            norm_sums(9)


def tiles_of(w):
    k, n = w.shape
    return w.reshape(k // P, P, n // P, P).transpose(2, 1, 0, 3).reshape(n // P, P, k)


def half_tiles_of(w):
    t = tiles_of(w)
    return t.reshape(-1, 2, P, 512).transpose(0, 2, 1, 3).reshape(-1, P, UNIT)


def row_tiles_of(w):
    k, n = w.shape
    return w.reshape(k // 256, 2, P, n // 512, 512).transpose(3, 0, 2, 1, 4).reshape(-1, P, UNIT)


def lay_out(a):
    win, win2 = a["w_in"][0], a["w_in_2"][0]
    parts = {
        "q": tiles_of(win[:, 0:512]), "k": tiles_of(win[:, 512:1024]), "v": row_tiles_of(win[:, 1024:1536]),
        "u": tiles_of(win[:, 1536:2048]), "gate": tiles_of(win[:, 2048:4096]),
        "xk": tiles_of(a["xa_wk"][0]), "xv": row_tiles_of(a["xa_wv"][0]), "xq": tiles_of(a["xa_wq"][0]),
        "xo": tiles_of(a["xa_wo"][0]), "glu": half_tiles_of(a["ssm_w_glu"][0]),
        "ba": half_tiles_of(a["w_branch_attn"][0]), "bs": half_tiles_of(a["w_branch_ssm"][0]),
        "out": tiles_of(a["w_out"][0]), "fg": tiles_of(a["ffn_w_up"][0][:, :FT * P]),
        "fv": tiles_of(a["ffn_w_up"][0][:, FT * P:]), "dn": a["ffn_w_down"][0].reshape(FT, P, D),
        "qk2": tiles_of(win2[:, 0:1024]), "v2": row_tiles_of(win2[:, 1024:1536]), "o2": tiles_of(win2[:, 1536:2048]),
        "ug": tiles_of(win2[:, 2056:2568]), "vg": row_tiles_of(win2[:, 2568:3080]), "out2": tiles_of(a["w_out_2"][0]),
    }
    stream = np.empty((DENSE + NE * PER_EXPERT, P, UNIT), np.float32)
    for n, (key, i) in enumerate(UNITS):
        stream[n] = parts[key][i]
    for e in range(NE):
        n = DENSE + (e // 2) * PAIR + e % 2
        stream[n:n + 2 * KT:2, :, :FE] = a["w_gate_2"][0, e].reshape(KT, P, FE)
        stream[n:n + 2 * KT:2, :, FE:] = a["w_up_2"][0, e].reshape(KT, P, FE)
        stream[n + 2 * KT:n + PAIR:2] = a["w_down_2"][0, e].reshape(FE // P, P, D)

    def column(v):
        return v.reshape(-1, P).T

    vectors = {
        "mix_pre": a["norm_mix_pre"], "mix_post": a["norm_mix_post"], "xa_pre": a["norm_xa_pre"],
        "xa_post": a["norm_xa_post"], "mem": a["norm_mem"], "ffn_pre": a["norm_ffn_pre"],
        "ffn_post": a["norm_ffn_post"], "norm1": a["norm1_g_2"], "norm2": a["norm2_g_2"], "final": a["final_g_2"],
        "b_gate": a["b_gate"], "d": a["ssm_d"], "b_glu": a["ssm_b_glu"], "conv0": a["ffn_conv_w"][0, 0],
        "conv1": a["ffn_conv_w"][0, 1], "conv2": a["ffn_conv_w"][0, 2], "conv_b": a["ffn_conv_b"],
        "qk0": a["conv_qk_2"][0, 0], "qk1": a["conv_qk_2"][0, 1], "qk2": a["conv_qk_2"][0, 2],
        "qk3": a["conv_qk_2"][0, 3], "g_mlstm": a["g_mlstm_out_2"], "g_v": a["g_gmlp_v_2"],
        "g_gmlp": a["g_gmlp_out_2"],
    }

    def states(v):
        return v.reshape(STILES, P).T

    log_dt = np.broadcast_to(a["ssm_log_dt"][0][:, None], (2 * STILES, 64))
    b = np.stack([a["ssm_b_re"][0], a["ssm_b_im"][0]])
    c = np.stack([a["ssm_c_re"][0], a["ssm_c_im"][0]])
    return {
        "stream": stream,
        "xT": a["x"][0].T.reshape(KT, P, T).transpose(1, 0, 2),
        "memT": a["mem"][0].T.reshape(KT, P, T).transpose(1, 0, 2),
        "cols": np.concatenate([column(vectors[name]) for name in COLS], axis=1),
        "ssm_a": np.stack([states(a["ssm_a_re"][0]), states(a["ssm_a_im"][0]), states(log_dt)], axis=1),
        "ssm_b": b.reshape(2, 4, 8, 64, 16).transpose(2, 4, 0, 1, 3).reshape(P, 2, 4, 64),
        "ssm_c": c.reshape(2, STILES, 2, 16, 64).transpose(2, 4, 0, 1, 3).reshape(P, 2, STILES, 16),
        "mixw": a["w_spatial_2"][0].transpose(2, 0, 1),
        "bsp": a["b_spatial_2"][0],
        "w_if": win2[:, 2048:2056].reshape(KT, P, 8).transpose(1, 0, 2),
        "b_if": np.stack([a["b_igate_2"][0], a["b_fgate_2"][0]], axis=1),
        "w_r": np.concatenate([a["w_router_group_2"][0], a["w_router_expert_2"][0]], axis=1
                              ).reshape(KT, P, 36).transpose(1, 0, 2),
        "b_r": np.concatenate([a["b_router_group_2"][0], a["b_router_expert_2"][0]]),
    }


def kernel(**inputs):
    import concourse.bacc as bacc
    from concourse.bass_utils import run_bass_kernel_spmd

    laid = {k: np.ascontiguousarray(v) for k, v in lay_out({k: np.asarray(v) for k, v in inputs.items()}).items()}
    nc = bacc.Bacc("TRN2", target_bir_lowering=False, num_devices=1)
    dram = {k: nc.dram_tensor(f"in_{k}", v.shape, mybir.dt.from_np(v.dtype), kind="ExternalInput").ap()
            for k, v in laid.items()}
    out = nc.dram_tensor("out_y", (P, KT, T), F32, kind="ExternalOutput").ap()
    program(nc, dram, out)
    got = run_bass_kernel_spmd(nc, [{f"in_{k}": v for k, v in laid.items()}], core_ids=[0]).results[0]["out_y"]
    return got.reshape(P, KT, T).transpose(2, 1, 0).reshape(1, T, D)
```
